# Optimizing a Trainium2 kernel written in Bass

```python
import math
import jax, jax.numpy as jnp
from jax import lax
import numpy as np

D_MODEL = 1024
BATCH = 1
SEQ = 256
DEPTH = 2

PLE_DIM = 256
EPS = 1e-6
NEG_INF = -1e30
MAX_POS_OFFSET = 1024

DIL_GROUPS = ((128, 1), (512, 4), (2048, 16))
N_GROUPS = len(DIL_GROUPS)
A_HEADS = 4
A_HEAD_DIM = 128
A_WIDTH = A_HEADS * A_HEAD_DIM
BLK = 64
ROT_DIM = A_HEAD_DIM // 4
ROPE_THETA = 500000.0

B_HEADS = 4
B_KEY = 128
B_VAL = 128
B_WIDTH = B_HEADS * B_KEY
CHUNK = 64

C_WIDTH = 512
CONV_W = 3

N_BRANCH = 3
BRANCH_WIDTH = 512

D_FF = 2816
N_EXPERTS = 8
TOP_K = 2
D_FF_EXPERT = 3584
N_DENSE = (DEPTH + 1) // 2
N_MOE = DEPTH // 2

A_COLS = N_GROUPS * 3 * A_WIDTH
B_COLS = 5 * B_WIDTH
C_COLS = 3 * C_WIDTH
G_COLS = N_BRANCH * D_MODEL
IN_COLS = A_COLS + B_COLS + C_COLS + G_COLS

kernel_name = "hybrid_dilated_hgrn2_shortconv_moe_encoder"

def rms_norm(x, g):
    xf = x.astype(jnp.float32)
    y = xf * lax.rsqrt(jnp.mean(xf * xf, axis=-1, keepdims=True) + EPS) * g.astype(jnp.float32)
    return y.astype(x.dtype)

def rope_tables(positions, dtype):
    inv_freq = ROPE_THETA ** (-jnp.arange(0, ROT_DIM, 2, dtype=jnp.float32) / ROT_DIM)
    ang = positions.astype(jnp.float32)[..., None] * inv_freq
    return jnp.cos(ang)[:, :, None, :].astype(dtype), jnp.sin(ang)[:, :, None, :].astype(dtype)

def apply_partial_rope(t, cos, sin):
    half = ROT_DIM // 2
    t1 = t[..., :half]
    t2 = t[..., half:ROT_DIM]
    return jnp.concatenate([t1 * cos - t2 * sin, t2 * cos + t1 * sin, t[..., ROT_DIM:]], axis=-1)

def dilated_window_attention(q, k, v, dil, half_span):
    b, s, h, dh = q.shape
    L = s // dil
    nb = -(-L // BLK)
    Lp = nb * BLK

    def to_sub(t):
        t = t.reshape(b, L, dil, h, dh).transpose(0, 2, 3, 1, 4)
        return jnp.pad(t, ((0, 0), (0, 0), (0, 0), (0, Lp - L), (0, 0)))

    def band(t):
        tp = jnp.pad(t, ((0, 0), (0, 0), (0, 0), (BLK, BLK), (0, 0))).reshape(b, dil, h, nb + 2, BLK, dh)
        return jnp.concatenate([tp[:, :, :, :-2], tp[:, :, :, 1:-1], tp[:, :, :, 2:]], axis=4)

    qb = to_sub(q).reshape(b, dil, h, nb, BLK, dh)
    kb = band(to_sub(k))
    vb = band(to_sub(v))
    qi = jnp.arange(nb)[:, None, None] * BLK + jnp.arange(BLK)[None, :, None]
    ki = (jnp.arange(nb)[:, None, None] - 1) * BLK + jnp.arange(3 * BLK)[None, None, :]
    valid = (jnp.abs(ki - qi) <= half_span) & (ki >= 0) & (ki < L)
    scores = jnp.einsum('brhnqd,brhnkd->brhnqk', qb, kb,
                        preferred_element_type=jnp.float32) * (1.0 / math.sqrt(dh))
    scores = jnp.where(valid, scores, NEG_INF)
    lse = jax.nn.logsumexp(scores, axis=-1)
    probs = jnp.exp(scores - lse[..., None]).astype(v.dtype)
    out = jnp.einsum('brhnqk,brhnkd->brhnqd', probs, vb)
    out = out.reshape(b, dil, h, Lp, dh)[:, :, :, :L].transpose(0, 3, 1, 2, 4).reshape(b, s, h, dh)
    lse = lse.reshape(b, dil, h, Lp)[..., :L].transpose(0, 3, 1, 2).reshape(b, s, h)
    return out, lse

def mixer_a(cols, cos, sin):
    b, s, _ = cols.shape
    outs, lses = [], []
    for g, (win, dil) in enumerate(DIL_GROUPS):
        blk = cols[..., g * 3 * A_WIDTH:(g + 1) * 3 * A_WIDTH].reshape(b, s, 3, A_HEADS, A_HEAD_DIM)
        q = apply_partial_rope(blk[:, :, 0], cos, sin)
        k = apply_partial_rope(blk[:, :, 1], cos, sin)
        o, l = dilated_window_attention(q, k, blk[:, :, 2], dil, win // (2 * dil))
        outs.append(o)
        lses.append(l)
    wts = jax.nn.softmax(jnp.stack(lses, axis=0), axis=0).astype(cols.dtype)
    out = jnp.einsum('gbsh,gbshd->bshd', wts, jnp.stack(outs, axis=0))
    return out.reshape(b, s, A_WIDTH)

def hgrn_lower_bounds(logits):
    sm = jax.nn.softmax(logits.astype(jnp.float32), axis=1)
    return jnp.cumsum(sm, axis=1) - sm[:, :1]

def hgrn2_scan(q, z, v, lb):
    b, s, h, dk = q.shape
    dv = v.shape[-1]
    nc = s // CHUNK
    f = lb + (1.0 - lb) * jax.nn.sigmoid(z)
    logf = jnp.log(f)
    k = (1.0 - lb) * jax.nn.sigmoid(-z)

    def chunks(t):
        return t.reshape(b, nc, CHUNK, h, t.shape[-1]).transpose(1, 0, 3, 2, 4)

    q, k, v, logf = chunks(q), chunks(k), chunks(v), chunks(logf)
    cum = jnp.cumsum(logf, axis=3)
    total = cum[:, :, :, -1:, :]
    mid = cum[:, :, :, CHUNK // 2 - 1:CHUNK // 2, :]
    att = jnp.einsum('nbhtc,nbhsc->nbhts', q * jnp.exp(cum - mid), k * jnp.exp(mid - cum))
    tril = jnp.tril(jnp.ones((CHUNK, CHUNK), dtype=bool))
    att = jnp.where(tril, att, 0.0)
    o_intra = jnp.einsum('nbhts,nbhsv->nbhtv', att, v)
    q_dec = q * jnp.exp(cum)
    k_dec = k * jnp.exp(total - cum)
    chunk_decay = jnp.exp(total[:, :, :, 0, :])

    def step(state, inp):
        q_c, k_c, v_c, d_c = inp
        o_c = jnp.einsum('bhtc,bhcv->bhtv', q_c, state)
        state = d_c[..., None] * state + jnp.einsum('bhsc,bhsv->bhcv', k_c, v_c)
        return state, o_c

    s0 = jnp.zeros((b, h, dk, dv), jnp.float32)
    _, o_inter = lax.scan(step, s0, (q_dec, k_dec, v, chunk_decay))
    o = o_intra + o_inter
    return o.transpose(1, 0, 3, 2, 4).reshape(b, s, h, dv)

def mixer_b(cols, lb_fwd, lb_bwd, norm_g):
    b, s, _ = cols.shape
    parts = [cols[..., n * B_WIDTH:(n + 1) * B_WIDTH] for n in range(5)]
    q, z_f, z_b, inp = [t.astype(jnp.float32).reshape(b, s, B_HEADS, B_KEY) for t in parts[:4]]
    gate = parts[4]
    lf = lb_fwd.reshape(B_HEADS, B_KEY)
    lbk = lb_bwd.reshape(B_HEADS, B_KEY)
    o_f = hgrn2_scan(q, z_f, inp, lf)
    o_b = jnp.flip(hgrn2_scan(jnp.flip(q, 1), jnp.flip(z_b, 1), jnp.flip(inp, 1), lbk), 1)
    o = o_f + o_b
    o = o * lax.rsqrt(jnp.mean(o * o, axis=-1, keepdims=True) + EPS) * norm_g.astype(jnp.float32).reshape(B_HEADS, B_VAL)
    return o.reshape(b, s, B_WIDTH).astype(cols.dtype) * jax.nn.silu(gate)

def mixer_c(cols, conv_w):
    u = cols[..., :C_WIDTH]
    b_gate = cols[..., C_WIDTH:2 * C_WIDTH]
    c_gate = cols[..., 2 * C_WIDTH:]
    y = lax.conv_general_dilated(c_gate * u, conv_w[:, None, :].astype(cols.dtype), window_strides=(1,),
                                 padding=((CONV_W // 2, CONV_W // 2),),
                                 dimension_numbers=('NWC', 'WIO', 'NWC'), feature_group_count=C_WIDTH)
    return b_gate * y

def swiglu(h, wg, wu, wd):
    return (jax.nn.silu(h @ wg) * (h @ wu)) @ wd

def moe_swiglu(h, router, wg, wu, wd):
    logits = jnp.einsum('bsd,de->bse', h, router).astype(jnp.float32)
    top_val, top_idx = lax.top_k(logits, TOP_K)
    top_w = jax.nn.softmax(top_val, axis=-1)
    combine = jnp.einsum('bsk,bske->bse', top_w,
                         jax.nn.one_hot(top_idx, N_EXPERTS, dtype=jnp.float32)).astype(h.dtype)
    out = jnp.zeros_like(h)
    for e in range(N_EXPERTS):
        out = out + combine[..., e:e + 1] * swiglu(h, wg[e], wu[e], wd[e])
    return out

def setup_inputs(seed: int = 0) -> dict:
    key = jax.random.key(seed)
    ks = jax.random.split(key, 26)
    f32 = jnp.float32

    def nrm(k, shape, fan_in):
        return jax.random.normal(k, shape, f32) * (fan_in ** -0.5)

    def gain(k, shape):
        return 1.0 + 0.05 * jax.random.normal(k, shape, f32)

    positions = (jnp.arange(SEQ, dtype=jnp.int32)[None, :]
                 + jax.random.randint(ks[2], (BATCH, 1), 0, MAX_POS_OFFSET, dtype=jnp.int32))
    return {
        "x": jax.random.normal(ks[0], (BATCH, SEQ, D_MODEL), f32),
        "p": jax.random.normal(ks[1], (DEPTH, BATCH, SEQ, PLE_DIM), f32),
        "positions": positions,
        "w_in": nrm(ks[3], (DEPTH, D_MODEL, IN_COLS), D_MODEL),
        "conv_w": nrm(ks[4], (DEPTH, CONV_W, C_WIDTH), CONV_W),
        "hgrn_lb_logits": jax.random.normal(ks[5], (2, DEPTH, B_WIDTH), f32),
        "hgrn_norm_g": gain(ks[6], (DEPTH, B_WIDTH)),
        "w_branch": nrm(ks[7], (DEPTH, N_BRANCH, BRANCH_WIDTH, D_MODEL), BRANCH_WIDTH),
        "w_out": nrm(ks[8], (DEPTH, D_MODEL, D_MODEL), D_MODEL),
        "g_mix_pre": gain(ks[9], (DEPTH, D_MODEL)),
        "g_mix_post": gain(ks[10], (DEPTH, D_MODEL)),
        "g_ffn_pre": gain(ks[11], (DEPTH, D_MODEL)),
        "g_ffn_post": gain(ks[12], (DEPTH, D_MODEL)),
        "dense_w_gate": nrm(ks[13], (N_DENSE, D_MODEL, D_FF), D_MODEL),
        "dense_w_up": nrm(ks[14], (N_DENSE, D_MODEL, D_FF), D_MODEL),
        "dense_w_down": nrm(ks[15], (N_DENSE, D_FF, D_MODEL), D_FF),
        "moe_router": nrm(ks[16], (N_MOE, D_MODEL, N_EXPERTS), D_MODEL),
        "moe_w_gate": nrm(ks[17], (N_MOE, N_EXPERTS, D_MODEL, D_FF_EXPERT), D_MODEL),
        "moe_w_up": nrm(ks[18], (N_MOE, N_EXPERTS, D_MODEL, D_FF_EXPERT), D_MODEL),
        "moe_w_down": nrm(ks[19], (N_MOE, N_EXPERTS, D_FF_EXPERT, D_MODEL), D_FF_EXPERT),
        "ple_w_proj": nrm(ks[20], (DEPTH, PLE_DIM, D_MODEL), PLE_DIM),
        "ple_w_gate": nrm(ks[21], (DEPTH, D_MODEL, D_MODEL), D_MODEL),
        "ple_g_in": gain(ks[22], (DEPTH, D_MODEL)),
        "ple_g_post": gain(ks[23], (DEPTH, D_MODEL)),
    }

def reference(x, p, positions, w_in, conv_w, hgrn_lb_logits, hgrn_norm_g, w_branch, w_out,
              g_mix_pre, g_mix_post, g_ffn_pre, g_ffn_post,
              dense_w_gate, dense_w_up, dense_w_down,
              moe_router, moe_w_gate, moe_w_up, moe_w_down,
              ple_w_proj, ple_w_gate, ple_g_in, ple_g_post):
    b, s, _ = x.shape
    cos, sin = rope_tables(positions, x.dtype)
    lower_bounds = hgrn_lower_bounds(hgrn_lb_logits)
    for i in range(DEPTH):
        h = rms_norm(x, g_mix_pre[i])
        proj = jnp.einsum('bsd,dc->bsc', h, w_in[i])
        o_a = mixer_a(proj[..., :A_COLS], cos, sin)
        o_b = mixer_b(proj[..., A_COLS:A_COLS + B_COLS], lower_bounds[0, i], lower_bounds[1, i], hgrn_norm_g[i])
        o_c = mixer_c(proj[..., A_COLS + B_COLS:A_COLS + B_COLS + C_COLS], conv_w[i])
        gates = jax.nn.sigmoid(proj[..., A_COLS + B_COLS + C_COLS:].reshape(b, s, N_BRANCH, D_MODEL))
        branches = jnp.stack([o_a, o_b, o_c], axis=2)
        up = jnp.einsum('bsnw,nwd->bsnd', branches, w_branch[i])
        merged = jnp.sum(gates * up, axis=2)
        y = merged @ w_out[i]
        x = x + rms_norm(y, g_mix_post[i])
        h = rms_norm(x, g_ffn_pre[i])
        j = i // 2
        if i % 2 == 0:
            y = swiglu(h, dense_w_gate[j], dense_w_up[j], dense_w_down[j])
        else:
            y = moe_swiglu(h, moe_router[j], moe_w_gate[j], moe_w_up[j], moe_w_down[j])
        x = x + rms_norm(y, g_ffn_post[i])
        gate = jax.nn.sigmoid(rms_norm(x, ple_g_in[i]) @ ple_w_gate[i])
        e = (p[i] @ ple_w_proj[i]) * gate
        x = x + rms_norm(e, ple_g_post[i])
    return x


_drawn_inputs = setup_inputs


def setup_inputs(seed=0):
    import zlib

    import numpy as np

    out = dict(_drawn_inputs(seed))
    spreads = {}
    factors = {}
    for name, (base, spread) in spreads.items():
        noise = np.random.default_rng([zlib.crc32(name.encode()), seed]).standard_normal(out[name].shape)
        drawn = base * np.exp(spread * noise) if base else spread * noise
        out[name] = __import__('jax').numpy.asarray(drawn.astype(out[name].dtype))
    for name, factor in factors.items():
        out[name] = (out[name] * factor).astype(out[name].dtype)
    return out
```

```python
from contextlib import ExitStack

import concourse.bass as bass
from concourse import mybir

F32 = mybir.dt.float32
F32R = mybir.dt.float32r
BF16 = mybir.dt.bfloat16
I32 = mybir.dt.int32
U32 = mybir.dt.uint32
ALU = mybir.AluOpType
ACT = mybir.ActivationFunctionType
AX = mybir.AxisListType

P = 128
DM = 1024
S = 256
NT = S // P
KT = DM // P
DEPTH = 2
EPS = 1e-6
NH = 4
HD = 128
ROT = HD // 4
NG = 3
CH = 64
NCH = S // CH
BW = 512
FD = 2816
NE = 8
FE = 3584
PLE = 256
SCALE = float(HD) ** -0.5
UC = 512
UN = 2048
RING = 6
NSPL = 2
LEAD = NSPL - 1
PARTS = 2
PC = UN // PARTS

CHUNKS = [("zf", 10, "feat"), ("zb", 11, "feat"), ("q", 9, "feat"), ("inp", 12, "feat"), ("gate", 13, "feat"),
          ("cu", 14, "feat"), ("cb", 15, "feat"), ("cc", 16, "feat")]
for _g in range(NG):
    CHUNKS += [(f"aq{_g}", 3 * _g, "feat"), (f"ak{_g}", 3 * _g + 1, "feat"), (f"av{_g}", 3 * _g + 2, "tok")]
NCHK = len(CHUNKS)
BRANCH_ORDER = [2, 1, 0]
U_GATE = 2 * NCHK
U_OUT = U_GATE + 3 * 6
U_MIX = U_OUT + 4
NFC = FD // UC
U_DENSE = 6 * NFC + 3
U_PLE = 5
NEC = FE // UC
U_EXP = 6 * NEC
TURNS_EXP = U_EXP // RING
U_L0 = U_MIX + U_DENSE + U_PLE
N_FILL = NCHK + 12
CIDX = {name: n for n, (name, _, _) in enumerate(CHUNKS)}
ROPED = [f"a{x}{g}" for g in range(NG) for x in "qk"]

C_ID, C_ONE, C_LT, C_IOTA, C_SCAN = 0, 128, 256, 384, 512
C_MASK, C_ROT, C_INV, C_I8, C_END = 1024, 1280, 1312, 1313, 1321
R_MIX, R_FFN, R_PLE, R_CONV, R_LB, R_NG, R_END = 0, 16, 32, 48, 72, 88, 96


def build(nc, io, out):
    ctx = ExitStack()
    with ctx:
        def sb(name, shape, dt=F32):
            return ctx.enter_context(nc.sbuf_tensor(name, shape, dt))

        def sem(name):
            return ctx.enter_context(nc.semaphore(name))

        x = sb("x", [P, NT, DM])
        raw = sb("raw", [P, RING, UN])
        w_hi = sb("w_hi", [P, NSPL, UN], F32R)
        w_lo = sb("w_lo", [P, NSPL, UN], F32R)
        hT_hi = sb("hT_hi", [P, KT, S], F32R)
        hT_lo = sb("hT_lo", [P, KT, S], F32R)
        br_hi = sb("br_hi", [P, 3, 1024], F32R)
        br_lo = sb("br_lo", [P, 3, 1024], F32R)
        cst = sb("cst", [P, C_END])
        prm = sb("prm", [P, R_END])
        maskb = sb("maskb", [P, 2, 512], BF16)
        identb = sb("identb", [P, P], BF16)
        rc = sb("rc", [ROT, 2, S])
        lb = sb("lb", [P, 2, DEPTH, NH])
        omlb = sb("omlb", [P, 2, DEPTH, NH])
        small = sb("small", [P, 96])
        arena = sb("arena", [P, 20 * 1024])

        ident = cst[:, C_ID:C_ID + P]
        ones = cst[:, C_ONE:C_ONE + P]
        lower = cst[:, C_LT:C_LT + P]
        iota = cst[:, C_IOTA:C_IOTA + P]
        scan_keep = cst[:, C_SCAN:C_SCAN + 512]
        causal = [cst[:, C_MASK + P * d:C_MASK + P * d + P].bitcast(U32) for d in range(2)]
        rotm = cst[0:ROT, C_ROT:C_ROT + ROT]
        inv_freq = cst[0:ROT, C_INV:C_INV + 1]
        iota8 = cst[:, C_I8:C_I8 + NE]

        def area(k, n=1024):
            return arena[:, 1024 * k:1024 * k + n]

        A = {f"a{x}{g}": area(3 * g + j) for g in range(NG) for j, x in enumerate("qkv")}
        B = {"zf": area(9), "zb": area(10), "q": area(11), "inp": area(12), "gate": area(13)}
        hL, hC, h1, h2 = area(14), area(15), area(16), area(17)
        kdT = area(18)
        attT = area(19)
        hS = sb("hS", [P, NH * HD])[:, :]
        conv = {"cu": A["aq2"], "cb": A["ak2"], "cc": A["av2"]}
        DEST = {**A, **B, **conv, "inp": h1}
        IN_TIME = (*B, *conv)
        merged = arena[:, 1024 * 9:1024 * 11]
        gtile = area(11)
        aP, aPT = area(12), area(13)
        adiag = area(14, 256)
        utmp = area(15)
        xn = arena[:, 0:2048]
        ptmp = area(16)
        junk = area(17)
        gb = area(18)
        dsg = area(4)
        yacc = arena[:, 1024 * 2:1024 * 4]
        ye = area(4)
        xg = area(5)
        hid = area(6, 512)
        msg = arena[:, 1024 * 6 + 512:1024 * 7]
        sel = area(7, 256)
        selc = arena[:, 1024 * 7 + 256:1024 * 7 + 512]
        selct = arena[:, 1024 * 7 + 512:1024 * 7 + 768]
        rout = arena[:, 1024 * 7 + 768:1024 * 7 + 832]
        rt = arena[:, 1024 * 7 + 832:1024 * 8]
        rk = sb("rk", [P, 4])
        minus_half = sb("minus_half", [P, 8])
        nsw_i = sb("nsw_i", [P, 1], I32)
        r_hi = sb("r_hi", [P, KT * NE], F32R)
        r_lo = sb("r_lo", [P, KT * NE], F32R)
        ptok = area(8, 512)
        sig = arena[:, 1024 * 10:1024 * 12]
        eprod = arena[:, 1024 * 12:1024 * 14]

        ps = ctx.enter_context(nc.psum_tensor("ps", [P, 8 * 512], F32))

        def bank(b, n=512):
            return ps[:, 512 * b:512 * b + n]

        raw_loaded = [sem(f"raw_loaded{n}") for n in range(RING)]
        hi_ready, lo_ready, part_used = sem("hi_ready"), sem("lo_ready"), sem("part_used")
        x_loaded, const_loaded, pos_loaded = sem("x_loaded"), sem("const_loaded"), sem("pos_loaded")
        gb_loaded, p_loaded, rout_loaded = sem("gb_loaded"), sem("p_loaded"), sem("rout_loaded")
        prm_turned, prm_ready, pre = sem("prm_turned"), sem("prm_ready"), sem("pre")
        pre_act = sem("pre_act")
        ssq, var_ready, rstd_ready, xn_ready = sem("ssq"), sem("var_ready"), sem("rstd_ready"), sem("xn_ready")
        turned, hT_hi_ready, hT_lo_ready = sem("turned"), sem("hT_hi_ready"), sem("hT_lo_ready")
        post_ssq, post_var, post_rstd, post_tmp, x_ready = (
            sem("post_ssq"), sem("post_var"), sem("post_rstd"), sem("post_tmp"), sem("x_ready"))
        evac_act, evac_dve = sem("evac_act"), sem("evac_dve")
        half_ready, z_att = sem("half_ready"), sem("z_att")
        inp_turned, inp_ready = sem("inp_turned"), sem("inp_ready")
        rot_done, rope_t1, rope_step = sem("rot_done"), sem("rope_t1"), sem("rope_step")
        h_pe, h_act, h_dve, h_pow = sem("h_pe"), sem("h_act"), sem("h_dve"), sem("h_pow")
        conv_step, conv_hi = sem("conv_step"), sem("conv_hi")
        at_s, at_t, at_v = sem("at_s"), sem("at_t"), sem("at_v")
        at_max, at_nm, at_exp, at_dve, at_pt_act, at_pt_dve = (
            sem("at_max"), sem("at_nm"), sem("at_exp"), sem("at_dve"), sem("at_pt_act"), sem("at_pt_dve"))
        at_hi, at_lo = sem("at_hi"), sem("at_lo")
        mg, m_hi, m_lo = sem("mg"), sem("m_hi"), sem("m_lo")
        d_sg, d_hid, d_hi, d_lo = sem("d_sg"), sem("d_hid"), sem("d_hi"), sem("d_lo")
        p_turned, p_hi, p_lo = sem("p_turned"), sem("p_hi"), sem("p_lo")
        pl_sig, pl_prod = sem("pl_sig"), sem("pl_prod")
        r_split, r_log, r_step, r_exp, r_rank = (
            sem("r_split"), sem("r_log"), sem("r_step"), sem("r_exp"), sem("r_rank"))
        sweeps_ready = sem("sweeps_ready")
        e_step, e_sel, e_gath, e_selc, e_xhi, e_xlo = (
            sem("e_step"), sem("e_sel"), sem("e_gath"), sem("e_selc"), sem("e_xhi"), sem("e_xlo"))
        e_sg, e_hid, e_turn, e_thi, e_tlo = sem("e_sg"), sem("e_hid"), sem("e_turn"), sem("e_thi"), sem("e_tlo")
        e_ye, e_scat, e_acc = sem("e_ye"), sem("e_scat"), sem("e_acc")
        stored = sem("stored")

        HD_D, HD_L = 29, 73
        HA_D, HA_L = 8, 19
        HP_D, HP_L = 6, 14

        def hdve(i, d, k):
            return HD_L * i + HD_D * d + k

        def hact(i, d, k):
            return HA_L * i + HA_D * d + k

        def hpe(i, d, k):
            return HP_L * i + HP_D * d + k

        def time_order(ap):
            return ap.rearrange("p (f i r) -> p f r i", f=4, r=4)

        def token_order(ap):
            return ap.rearrange("p (f r i) -> p f r i", f=4, r=4)

        def chunked(ap, n=16):
            return ap.rearrange("p (c t) -> p c t", c=n)

        def unit_w(w, k):
            return w[:, k % NSPL, :].rearrange("p (k n) -> p k n", k=4)

        def unit_done(eng, turns, k):
            eng.wait_ge(part_used, turns * (RING * PARTS) + PARTS * (k + 1))

        def fill_unit(f):
            return 2 * f + 1 if f < NCHK else U_GATE + 3 * ((f - NCHK) // 2) + 1 + (f - NCHK) % 2

        block = ctx.enter_context(nc.Block())

        @block.sync
        def _(sp):
            def load(turns, k, src, first=False):
                if not (isinstance(turns, int) and turns * RING + k < RING):
                    sp.wait_ge(lo_ready, turns * (RING * PARTS) + PARTS * (k - RING + 1))
                sp.dma_start(raw[:, k % RING, :].rearrange("p (k n) -> p k n", n=src.shape[-1]), src)\
                  .then_inc(raw_loaded[k % RING], 16)

            def tile4(w, r0, c0):
                return w[r0:r0 + 512, c0:c0 + UC].rearrange("(k p) n -> p k n", p=P)

            def mixer(i, k):
                for _, blk, _ in CHUNKS:
                    for kh in range(2):
                        load(0, k, tile4(io["w_in"][i], 512 * kh, UC * blk))
                        k += 1
                for n in BRANCH_ORDER:
                    for j in range(2):
                        for kh in range(2):
                            load(0, k, tile4(io["w_in"][i], 512 * kh, UC * (17 + 2 * n + j)))
                            k += 1
                        load(0, k, tile4(io["w_branch"][i, n], 0, UC * j))
                        k += 1
                for j in range(2):
                    for kh in range(2):
                        load(0, k, tile4(io["w_out"][i], 512 * kh, UC * j))
                        k += 1
                return k

            def dense(k):
                wg, wu, wd = io["dense_w_gate"][0], io["dense_w_up"][0], io["dense_w_down"][0]
                for w in (wg, wu):
                    for kh in range(2):
                        load(0, k, tile4(w, 512 * kh, 0))
                        k += 1
                turn0, k0 = k // RING, k % RING
                with sp.Fori(1, NFC) as c:
                    turns = c + (turn0 - 1)
                    kk = k0
                    for kh in range(2):
                        load(turns, kk, wg[512 * kh:512 * kh + 512, bass.ds(c * UC, UC)]
                             .rearrange("(k p) n -> p k n", p=P))
                        kk += 1
                    for j in range(2):
                        load(turns, kk, wd[bass.ds((c - 1) * UC, 512), UC * j:UC * j + UC]
                             .rearrange("(k p) n -> p k n", p=P))
                        kk += 1
                    for kh in range(2):
                        load(turns, kk, wu[512 * kh:512 * kh + 512, bass.ds(c * UC, UC)]
                             .rearrange("(k p) n -> p k n", p=P))
                        kk += 1
                k += 6 * (NFC - 1)
                f0 = NFC * UC
                load(0, k, wg[:, f0:FD].rearrange("(k p) n -> p k n", p=P))
                load(0, k + 1, tile4(wd, f0 - UC, 0))
                load(0, k + 2, tile4(wd, f0 - UC, UC))
                load(0, k + 3, wu[:, f0:FD].rearrange("(k p) n -> p k n", p=P))
                load(0, k + 4, wd[f0:FD, :].rearrange("(k p) n -> p k n", p=P))
                return k + 5

            def ple(i, turns, k):
                load(turns, k, io["ple_w_proj"][i].rearrange("(k p) n -> p k n", p=P))
                for j in range(2):
                    for kh in range(2):
                        k += 1
                        load(turns, k, tile4(io["ple_w_gate"][i], 512 * kh, UC * j))
                return k + 1

            k = mixer(0, 0)
            k = dense(k)
            k = ple(0, 0, k)
            k = mixer(1, k)
            turn0, k0 = k // RING, k % RING

            def sweep(s):
                with sp.Fori(0, NE) as e:
                    turns = e * TURNS_EXP + (s * (NE * TURNS_EXP) + turn0)
                    wg, wu, wd = (io[w][0, bass.ds(e, 1)] for w in ("moe_w_gate", "moe_w_up", "moe_w_down"))

                    def up(w, kk, c, kh):
                        load(turns, kk, w[:, 512 * kh:512 * kh + 512, UC * c:UC * c + UC]
                             .rearrange("a (k p) n -> p (a k) n", p=P))

                    def down(kk, c):
                        for j in range(2):
                            load(turns, kk + j, wd[:, UC * c:UC * c + 512, UC * j:UC * j + UC]
                                 .rearrange("a (k p) n -> p (a k) n", p=P))

                    kk = k0
                    for c in range(NEC):
                        for w in (wg, wu):
                            for kh in range(2):
                                up(w, kk, c, kh)
                                kk += 1
                        if c:
                            down(kk, c - 1)
                            kk += 2
                    down(kk, NEC - 1)

            sweep(0)
            sp.wait_ge(sweeps_ready, 1)
            sweeps = sp.value_load(nsw_i[0:1, 0:1], min_val=1, max_val=2)
            with sp.If(sweeps > 1):
                sweep(1)
            ple(1, sweeps * (NE * TURNS_EXP) + turn0, k0)
            sp.wait_ge(x_ready, 4 * 3)
            for r in range(4):
                sp.dma_start(out[0].rearrange("(i r) d -> r i d", r=4)[r],
                             x[64 * (r % 2):64 * (r % 2) + 64, r // 2, :]).then_inc(stored, 16)
            sp.wait_ge(stored, 64)

        @block.scalar
        def _(act):
            def split(turns, k):
                act.wait_ge(raw_loaded[k % RING], (turns + (k // RING + 1)) * 16)
                for h in range(PARTS):
                    if not (isinstance(turns, int) and turns * RING + k < NSPL):
                        act.wait_ge(part_used, turns * (RING * PARTS) + PARTS * (k - NSPL) + h + 1)
                    cols = slice(PC * h, PC * h + PC)
                    act.activation(w_hi[:, k % NSPL, cols], raw[:, k % RING, cols], ACT.Copy).then_inc(hi_ready, 1)

            def pre_norm(i, m):
                n = 3 * i + m
                if n:
                    act.wait_ge(x_ready, 2 * n)
                else:
                    act.wait_ge(x_loaded, 64)
                for t in range(NT):
                    if t:
                        act.wait_ge(ssq, NT * n + t)
                    act.activation(junk, x[:, t, :], ACT.Square,
                                   accum_out=small[:, t:t + 1]).then_inc(ssq, 1)
                if m:
                    gain_load(i, m)

            def gain_load(i, m):
                src = io[("g_mix_post", "g_ffn_post", "ple_g_post")[m]][i:i + 1, :]
                act.dma_start(gb, src.to_broadcast([P, DM]))\
                   .then_inc(gb_loaded, 16)

            def pre_norm_hi(i, m):
                n = 3 * i + m
                act.wait_ge(prm_ready, 1)
                for k in range(KT):
                    g = prm[:, (R_MIX, R_FFN, R_PLE)[m] + KT * i + k:][:, 0:1]
                    act.wait_ge(turned, 4 * n + k // 2 + 1)
                    act.activation(hT_hi[:, k, :], ps[:, S * k:S * k + S], ACT.Identity, scale=g)\
                       .then_inc(hT_hi_ready, 1)

            def post_norm(n, ys):
                for t in range(NT):
                    if t:
                        act.wait_ge(post_ssq, NT * n + t)
                    act.activation(junk, ys(t), ACT.Square, accum_out=small[:, 4 + t:5 + t])\
                       .then_inc(post_ssq, 1)

            def h_vec(i, d, step):
                z = B["zf" if d == 0 else "zb"]
                if step == 0:
                    act.wait_ge(evac_act, 23 * i + 2 + 1)
                    if d:
                        act.wait_ge(h_pe, hpe(i, 0, 6))
                        act.wait_ge(h_dve, hdve(i, 0, 29))
                    act.activation(hL, z, ACT.Sigmoid).then_inc(h_act, 1)
                    act.wait_ge(h_act, hact(i, d, 1))
                    act.activation(z, z, ACT.Sigmoid, scale=-1.0).then_inc(h_act, 1)
                if step == 1:
                    act.wait_ge(h_dve, hdve(i, d, 4))
                    act.activation(hL, hL, ACT.Ln).then_inc(h_act, 1)
                if step == 2:
                    act.wait_ge(h_dve, hdve(i, d, 8))
                    act.activation(h1, hL, ACT.Exp).then_inc(h_act, 1)
                    act.wait_ge(h_act, hact(i, d, 4))
                    act.activation(hL, hL, ACT.Exp, scale=-1.0).then_inc(h_act, 1)
                    act.activation(h2, h2, ACT.Exp).then_inc(h_act, 1)
                    act.activation(hC, hC, ACT.Exp).then_inc(h_act, 1)
                if step == 3:
                    act.wait_ge(h_pe, hpe(i, d, 2))
                    act.activation(kdT, ps[:, 2048:3072], ACT.Copy).then_inc(h_act, 1)

            def h_post(i, step):
                if step == 0:
                    act.wait_ge(h_pe, hpe(i, 2, 0))
                    act.wait_ge(h_dve, hdve(i, 2, 0))
                    act.activation(h1, ps[:, 512 * 6:512 * 8], ACT.Copy).then_inc(h_act, 1)
                    act.activation(hL, ps[:, 512 * 6:512 * 8], ACT.Square).then_inc(h_act, 1)
                else:
                    act.wait_ge(h_dve, hdve(i, 2, 14))
                    act.activation(token_order(br_hi[:, 1, :]), time_order(h2), ACT.Copy).then_inc(h_act, 1)

            def mixer(i):
                base = U_L0 * i
                pre_norm(i, 0)
                for k in range(LEAD):
                    if i == 0:
                        split(0, base + k)
                if i == 0:
                    preamble_tables()
                pre_norm_hi(i, 0)
                for u in range(U_MIX):
                    split(0, base + u + LEAD)
                    if u < U_GATE and u % 2 == 1:
                        c = u // 2
                        name = CHUNKS[c][0]
                        unit_done(act, 0, base + u)
                        if name in ("aq2", "ak2", "av2"):
                            act.wait_ge(conv_hi, i + 1)
                            act.wait_ge(conv_step, 15 * (i + 1))
                        if name == "inp" and i:
                            act.wait_ge(h_dve, hdve(i - 1, 2, 13))
                        dst, src = DEST[name], ps[:, 1024 * (c % 2):1024 * (c % 2) + 1024]
                        if name in IN_TIME:
                            dst, src = time_order(dst), token_order(src)
                        act.activation(dst, src, ACT.Silu if name == "gate" else ACT.Copy).then_inc(evac_act, 1)
                    if U_GATE <= u < U_OUT and (u - U_GATE) % 3 == 1:
                        m = (u - U_GATE) // 3
                        f = NCHK + 2 * m
                        unit_done(act, 0, base + u)
                        if m:
                            act.wait_ge(evac_dve, 6 * i + m)
                        else:
                            act.wait_ge(h_dve, hdve(i, 2, 15))
                            act.wait_ge(h_act, hact(i, 2, 3))
                        act.activation(gtile, ps[:, 1024 * (f % 2):1024 * (f % 2) + 1024], ACT.Sigmoid)\
                           .then_inc(evac_act, 1)
                    if u == 6:
                        h_vec(i, 0, 0)
                    if u == 8:
                        h_vec(i, 0, 1)
                        act.wait_ge(inp_turned, i + 1)
                        act.activation(B["inp"], ps[:, 2048:3072], ACT.Copy).then_inc(inp_ready, 1)
                    if u == 11:
                        h_vec(i, 0, 2)
                    if u == 17:
                        act.wait_ge(conv_step, 15 * i + 14)
                        act.activation(token_order(br_hi[:, 2, :]), time_order(conv["cc"]), ACT.Copy).then_inc(conv_hi, 1)
                    if u == 16:
                        h_vec(i, 0, 3)
                    if u == 21:
                        h_vec(i, 1, 0)
                    if u == 22:
                        h_vec(i, 1, 1)
                    if u == 23:
                        h_vec(i, 1, 2)
                    if u == 27:
                        h_vec(i, 1, 3)
                    if u == 32:
                        h_post(i, 0)
                    if u == 34:
                        h_post(i, 1)
                    if 35 <= u < 44:
                        attend(i, u - 35)
                    if u == 44:
                        act.wait_ge(h_pe, hpe(i, 2, 0))
                        gain_load(i, 0)
                    if u == U_OUT:
                        act.wait_ge(mg, 4 * (i + 1))
                        act.activation(hT_hi[:, :, :].rearrange("p k t -> p (k t)"), merged, ACT.Copy)\
                           .then_inc(m_hi, 1)

            def attend(i, g):
                h, odd = g // 2, g % 2
                if not odd and h >= 1:
                    hh = h - 1
                    act.wait_ge(at_v, NH * i + hh + 1)
                    act.activation(br_hi[:, 0, S * hh:S * hh + S], ps[:, 3072:3072 + S], ACT.Copy)\
                       .then_inc(at_hi, 1)
                if not odd and h < NH:
                    for q in range(2):
                        act.wait_ge(at_nm, NH * i + h + 1)
                        act.activation(aP[:, 512 * q:512 * q + 512], bank(4 + q), ACT.Exp, scale=SCALE,
                                       bias=small[:, 16 + q:17 + q], accum_out=small[:, 18 + q:19 + q])\
                           .then_inc(at_exp, 1)
                if odd:
                    act.wait_ge(at_t, 2 * (NH * i + h) + 1)
                    act.activation(aPT[:, 0:512], bank(6), ACT.Copy).then_inc(at_pt_act, 1)

            def preamble_tables():
                act.wait_ge(pre, PRE_LB)
                act.activation(small[:, 64:80], small[:, 48:64], ACT.Exp).then_inc(pre_act, 1)
                act.wait_ge(pre, PRE_ROPE)
                act.activation(rc[:, 0, :], rc[:, 0, :], ACT.Sin).then_inc(pre_act, 1)
                act.activation(rc[:, 1, :], rc[:, 1, :], ACT.Sin).then_inc(pre_act, 1)

            def p_load(i):
                for r in range(4):
                    act.dma_start(ptok[64 * (r % 2):64 * (r % 2) + 64, PLE * (r // 2):PLE * (r // 2) + PLE],
                                  io["p"][i, 0].rearrange("(i r) c -> r i c", r=4)[r]).then_inc(p_loaded, 16)

            def p_split(i):
                act.wait_ge(p_turned, i + 1)
                act.activation(br_hi[:, 2, 0:512], bank(7), ACT.Copy).then_inc(p_hi, 1)

            def dense(base):
                k = base + LEAD

                def gate(turns, kk, c, n=1024):
                    unit_done(act, turns, kk)
                    act.wait_ge(d_lo, c)
                    act.activation(dsg[:, 0:n], ps[:, 512 * 4:512 * 4 + n], ACT.Silu).then_inc(d_sg, 1)

                def hidden(c, n=1024):
                    act.wait_ge(d_hid, c + 1)
                    act.activation(br_hi[:, 0, 0:n], dsg[:, 0:n], ACT.Copy).then_inc(d_hi, 1)

                for u in range(4):
                    split(0, k)
                    if u == 1:
                        gate(0, base + 1, 0)
                    if u == 3:
                        hidden(0)
                    k += 1
                turn0, k0 = k // RING, k % RING
                with act.Fori(1, NFC) as c:
                    turns = c + (turn0 - 1)
                    for u in range(6):
                        split(turns, k0 + u)
                        if u == 1:
                            gate(turns, k0 - LEAD + 1, c)
                        if u == 5:
                            hidden(c)
                k += 6 * (NFC - 1)
                for u in range(5):
                    split(0, k + u)
                    if u == 0:
                        gate(0, k - LEAD, NFC, 512)
                    if u == 3:
                        hidden(NFC, 512)

            def experts(base):
                act.wait_ge(sweeps_ready, 1)
                sweeps = act.value_load(nsw_i[0:1, 0:1], min_val=1, max_val=2)
                k = base + LEAD
                turn0, k0 = k // RING, k % RING
                with act.Fori(0, sweeps) as s:
                    with act.Fori(0, NE) as e:
                        it = s * NE + e
                        turns = it * TURNS_EXP + turn0

                        def turn(c):
                            act.wait_ge(e_turn, it * NEC + (c + 1 + ONE))
                            act.activation(br_hi[:, 0, 0:512], bank(6), ACT.Copy).then_inc(e_thi, 1)

                        act.wait_ge(e_step, it * 4 + s + (3 + ONE))
                        act.activation(br_hi[:, 1, :], xg, ACT.Copy).then_inc(e_xhi, 1)
                        kk = k0
                        for c in range(NEC):
                            for u in range(4 if c == 0 else 6):
                                split(turns, kk)
                                kk += 1
                                if u == 1:
                                    unit_done(act, turns, kk - LEAD - 1)
                                    if c:
                                        act.wait_ge(e_hid, it * NEC + c)
                                    act.activation(msg, bank(4), ACT.Silu).then_inc(e_sg, 1)
                                    if c:
                                        turn(c - 1)
                        turn(NEC - 1)
                        split(turns, kk)
                        split(turns, kk + 1)
                        unit_done(act, turns, k0 - LEAD + U_EXP - 1)
                        act.activation(ye, ps[:, 0:1024], ACT.Copy).then_inc(e_ye, 1)
                return sweeps

            def ple(i, turns, k):
                n_units = (U_PLE - 1) if i == DEPTH - 1 else U_PLE
                k += LEAD
                for u in range(n_units):
                    split(turns, k + u)
                unit_done(act, turns, k - LEAD + U_PLE - 1)
                act.activation(sig, ps[:, 0:2048], ACT.Sigmoid).then_inc(pl_sig, 1)
                act.wait_ge(pl_prod, i + 1)
                post_norm(3 * i + 2, lambda t: eprod[:, DM * t:DM * t + DM])

            def y_psum(t):
                return ps[:, DM * t:DM * t + DM]

            for r in range(4):
                act.dma_start(x[64 * (r % 2):64 * (r % 2) + 64, r // 2, :],
                              io["x"][0].rearrange("(i r) d -> r i d", r=4)[r]).then_inc(x_loaded, 16)
            act.dma_start(cst[:, :], io["const"]).then_inc(const_loaded, 16)
            act.dma_start(maskb[:, :, :], io["maskb"]).then_inc(const_loaded, 16)
            act.dma_start(identb[:, :], io["identb"]).then_inc(const_loaded, 16)
            rows = arena[0:R_END, 2048:2048 + P]
            for r0, name, pat in ((R_MIX, "g_mix_pre", "i (k p) -> (i k) p"), (R_FFN, "g_ffn_pre", "i (k p) -> (i k) p"),
                                  (R_PLE, "ple_g_in", "i (k p) -> (i k) p"),
                                  (R_CONV, "conv_w", "i w (k p) -> (i w k) p"),
                                  (R_LB, "hgrn_lb_logits", "s i (k p) -> (s i k) p"),
                                  (R_NG, "hgrn_norm_g", "i (k p) -> (i k) p")):
                src = io[name].rearrange(pat, p=P)
                act.dma_start(rows[r0:r0 + src.shape[0], :], src).then_inc(const_loaded, 16)
            act.dma_start(arena[0:ROT, 3072:3072 + S].bitcast(I32),
                          io["positions"].partition_broadcast(ROT).rearrange("p a s -> p (a s)"))\
               .then_inc(pos_loaded, 16)

            mixer(0)
            unit_done(act, 0, U_MIX - 1)
            post_norm(0, y_psum)
            p_load(0)
            pre_norm(0, 1)
            pre_norm_hi(0, 1)
            p_split(0)
            dense(U_MIX)
            unit_done(act, 0, U_MIX + U_DENSE - 1)
            post_norm(1, y_psum)
            pre_norm(0, 2)
            pre_norm_hi(0, 2)
            ple(0, 0, U_MIX + U_DENSE)
            mixer(1)
            unit_done(act, 0, U_L0 + U_MIX - 1)
            post_norm(3, y_psum)
            p_load(1)
            act.dma_start(rout.rearrange("p (k e) -> p k e", k=KT),
                          io["moe_router"][0].rearrange("(k p) e -> p k e", p=P)).then_inc(rout_loaded, 16)
            pre_norm(1, 1)
            pre_norm_hi(1, 1)
            p_split(1)
            act.wait_ge(rout_loaded, 16)
            act.activation(r_hi[:, :], rout, ACT.Copy).then_inc(r_split, 1)
            act.wait_ge(r_step, R_DIFF)
            act.activation(rt[:, RT_EX:RT_EX + 16], rt[:, RT_DF:RT_DF + 16], ACT.Exp).then_inc(r_exp, 1)
            sweeps = experts(U_L0 + U_MIX)
            act.wait_ge(e_acc, sweeps * (NE * 2) + 1)
            post_norm(4, lambda t: yacc[:, DM * t:DM * t + DM])
            pre_norm(1, 2)
            pre_norm_hi(1, 2)
            k = U_L0 + U_MIX
            ple(1, sweeps * (NE * TURNS_EXP) + k // RING, k % RING)

        @block.vector
        def _(dve):
            def split(turns, k):
                for h in range(PARTS):
                    dve.wait_ge(hi_ready, turns * (RING * PARTS) + PARTS * k + h + 1)
                    cols = slice(PC * h, PC * h + PC)
                    dve.tensor_tensor(w_lo[:, k % NSPL, cols], raw[:, k % RING, cols],
                                      w_hi[:, k % NSPL, cols].bitcast(F32), ALU.subtract).then_inc(lo_ready, 1)

            def pre_norm(i, m):
                n = 3 * i + m
                dve.wait_ge(ssq, NT * (n + 1))
                dve.tensor_scalar(small[:, 2:4], small[:, 0:2], 1.0 / DM, EPS, ALU.mult, ALU.add)\
                   .then_inc(var_ready, 1)
                dve.wait_ge(rstd_ready, n + 1)
                for t in range(NT):
                    dve.tensor_scalar(xn[:, DM * t:DM * t + DM], x[:, t, :], small[:, 8 + t:9 + t], None, ALU.mult)\
                       .then_inc(xn_ready, 1)
                for k in range(KT):
                    g = prm[:, (R_MIX, R_FFN, R_PLE)[m] + KT * i + k:][:, 0:1]
                    dve.wait_ge(hT_hi_ready, KT * n + 2 * (k // 2) + 2)
                    dve.scalar_tensor_tensor(out=hT_lo[:, k, :], in0=ps[:, S * k:S * k + S], scalar=g,
                                             in1=hT_hi[:, k, :].bitcast(F32), op0=ALU.mult, op1=ALU.subtract)\
                       .then_inc(hT_lo_ready, 1)

            def post_norm(n, ys):
                dve.wait_ge(post_ssq, NT * (n + 1))
                dve.tensor_scalar(small[:, 6:8], small[:, 4:6], 1.0 / DM, EPS, ALU.mult, ALU.add)\
                   .then_inc(post_var, 1)
                dve.wait_ge(post_rstd, n + 1)
                dve.wait_ge(gb_loaded, 16 * (n + 1))
                for t in range(NT):
                    if n or t:
                        dve.wait_ge(x_ready, 2 * n + t)
                    dve.scalar_tensor_tensor(out=ptmp, in0=ys(t), scalar=small[:, 10 + t:11 + t], in1=gb,
                                             op0=ALU.mult, op1=ALU.mult).then_inc(post_tmp, 1)
                    dve.wait_ge(post_tmp, 2 * n + t + 1)
                    dve.tensor_tensor(x[:, t, :], x[:, t, :], ptmp, ALU.add).then_inc(x_ready, 1)

            def rope(i, r):
                name = ROPED[r]
                c = CIDX[name]
                n = 6 * i + r
                qr = A[name][0:ROT, :].rearrange("p (h t) -> p h t", h=NH)
                cos = rc[:, 0:1, :].to_broadcast([ROT, NH, S])
                sin = rc[:, 1:2, :].to_broadcast([ROT, NH, S])
                pq = ps[0:ROT, 1024 * (c % 2):1024 * (c % 2) + 1024].rearrange("p (h t) -> p h t", h=NH)
                dve.wait_ge(rot_done, n + 1)
                if n:
                    dve.wait_ge(rope_step, 2 * n)
                dve.tensor_tensor(pq, pq, sin, ALU.mult).then_inc(rope_t1, 1)
                dve.tensor_tensor(qr, qr, cos, ALU.mult).then_inc(rope_step, 1)
                dve.wait_ge(rope_t1, n + 1)
                dve.wait_ge(rope_step, 2 * n + 1)
                dve.tensor_tensor(qr, qr, pq, ALU.add).then_inc(rope_step, 1)

            def h_vec(i, d, step):
                z = B["zf" if d == 0 else "zb"]
                lbs = [lb[:, d, i, h:h + 1] for h in range(NH)]
                oms = [omlb[:, d, i, h:h + 1] for h in range(NH)]
                end, mid = (CH - 1, CH // 2 - 1) if d == 0 else (0, CH // 2)
                if step == 0:
                    dve.wait_ge(h_act, hact(i, d, 1))
                    for h in range(NH):
                        a = hL[:, S * h:S * h + S]
                        dve.tensor_scalar(a, a, oms[h], lbs[h], ALU.mult, ALU.add).then_inc(h_dve, 1)
                if step == 1:
                    dve.wait_ge(h_act, hact(i, d, 3))
                    for r in range(2):
                        a, c = hL[:, 512 * r:512 * r + 512], hC[:, 512 * r:512 * r + 512]
                        if d:
                            a, c = a[:, ::-1], c[:, ::-1]
                        dve.tensor_tensor_scan(out=c, data0=scan_keep, data1=a, initial=0.0,
                                               op0=ALU.mult, op1=ALU.add).then_inc(h_dve, 1)
                    dve.wait_ge(h_dve, hdve(i, d, 6))
                    cv = chunked(hC)
                    dve.tensor_tensor(chunked(hL), cv, cv[:, :, mid:mid + 1].to_broadcast([P, 16, CH]),
                                      ALU.subtract).then_inc(h_dve, 1)
                    dve.tensor_tensor(chunked(h2), cv[:, :, end:end + 1].to_broadcast([P, 16, CH]), cv,
                                      ALU.subtract).then_inc(h_dve, 1)
                if step == 2:
                    dve.wait_ge(evac_act, 23 * i + CIDX["q"] + 1)
                    dve.wait_ge(h_act, hact(i, d, 4))
                    dve.tensor_tensor(h1, h1, B["q"], ALU.mult).then_inc(h_dve, 1)
                    dve.wait_ge(h_act, hact(i, d, 5))
                    for h in range(NH):
                        a = hL[:, S * h:S * h + S]
                        dve.scalar_tensor_tensor(out=a, in0=z[:, S * h:S * h + S], scalar=oms[h], in1=a,
                                                 op0=ALU.mult, op1=ALU.mult).then_inc(h_dve, 1)
                    dve.wait_ge(h_act, hact(i, d, 7))
                    dve.tensor_copy(small[:, 32:48].rearrange("p (c a) -> p c a", a=1),
                                    chunked(hC)[:, :, end:end + 1]).then_inc(h_dve, 1)
                    for h in range(NH):
                        a = h2[:, S * h:S * h + S]
                        dve.scalar_tensor_tensor(out=a, in0=z[:, S * h:S * h + S], scalar=oms[h], in1=a,
                                                 op0=ALU.mult, op1=ALU.mult).then_inc(h_dve, 1)
                    dve.wait_ge(h_dve, hdve(i, d, 14))
                    dve.tensor_tensor(hC, hC, B["q"], ALU.mult).then_inc(h_dve, 1)
                if step == 3:
                    dve.wait_ge(h_pe, hpe(i, d, 1))
                    if d:
                        dve.wait_ge(h_dve, hdve(i, 1, 19))
                    dve.copy_predicated(attT.rearrange("p (c t) -> p c t", t=P),
                                        causal[d].rearrange("p (a t) -> p a t", a=1).to_broadcast([P, 8, P]),
                                        ps[:, 2048:3072].rearrange("p (c t) -> p c t", t=P)).then_inc(h_dve, 1)
                if step == 4:
                    dve.wait_ge(h_pe, hpe(i, d, 3))
                    dve.tensor_copy(hS, bank(4)).then_inc(h_dve, 1)
                if step in (5, 6):
                    c = step - 4
                    if d:
                        c = NCH - 1 - c
                    dve.wait_ge(h_pe, hpe(i, d, step - 1))
                    dve.wait_ge(h_dve, hdve(i, d, 21 + 4 * (step - 5)))
                    for h in range(NH):
                        a = hS[:, HD * h:HD * h + HD]
                        dve.scalar_tensor_tensor(out=a, in0=a, scalar=small[:, 32 + NCH * h + c:33 + NCH * h + c],
                                                 in1=ps[:, 2048 + HD * h:2048 + HD * h + HD],
                                                 op0=ALU.mult, op1=ALU.add).then_inc(h_dve, 1)

            def h_post(i, step):
                if step == 0:
                    dve.wait_ge(h_pe, hpe(i, 2, 1))
                    dve.tensor_scalar(small[:, 80:88], bank(4)[:, 0:8], 1.0 / HD, EPS, ALU.mult, ALU.add)\
                       .then_inc(h_dve, 1)
                    dve.wait_ge(h_pow, i + 1)
                    for j in range(8):
                        dve.tensor_scalar(hC[:, P * j:P * j + P], ident, small[:, 88 + j:89 + j], None, ALU.mult)\
                           .then_inc(h_dve, 1)
                if step == 1:
                    dve.wait_ge(h_pe, hpe(i, 2, 2))
                    dve.wait_ge(h_act, hact(i, 2, 1))
                    for h in range(NH):
                        dve.scalar_tensor_tensor(out=h2[:, S * h:S * h + S], in0=h1[:, S * h:S * h + S],
                                                 scalar=prm[:, R_NG + NH * i + h:R_NG + NH * i + h + 1],
                                                 in1=ps[:, 2048 + S * h:2048 + S * h + S],
                                                 op0=ALU.mult, op1=ALU.mult).then_inc(h_dve, 1)
                    dve.wait_ge(h_dve, hdve(i, 2, 13))
                    dve.wait_ge(evac_act, 23 * i + CIDX["gate"] + 1)
                    dve.tensor_tensor(h2, h2, B["gate"], ALU.mult).then_inc(h_dve, 1)
                    dve.wait_ge(h_act, hact(i, 2, 3))
                    dve.wait_ge(h_dve, hdve(i, 2, 14))
                    dve.tensor_tensor(token_order(br_lo[:, 1, :]), time_order(h2),
                                      token_order(br_hi[:, 1, :].bitcast(F32)), ALU.subtract)\
                       .then_inc(h_dve, 1)

            def convolve(i):
                cu, cb, cc = conv["cu"], conv["cb"], conv["cc"]
                n0 = 15 * i
                dve.wait_ge(evac_act, 23 * i + CIDX["cc"] + 1)
                dve.tensor_tensor(cu, cu, cc, ALU.mult).then_inc(conv_step, 1)
                dve.wait_ge(conv_step, n0 + 1)
                taps = [[prm[:, R_CONV + 12 * i + 4 * w + f:][:, 0:1] for w in range(3)] for f in range(4)]
                for f in range(4):
                    dve.tensor_scalar(cc[:, S * f:S * f + S], cu[:, S * f:S * f + S], taps[f][1], None, ALU.mult)\
                       .then_inc(conv_step, 1)
                for f in range(4):
                    y, s = cc[:, S * f:S * f + S], cu[:, S * f:S * f + S]
                    dve.wait_ge(conv_step, n0 + 2 + f)
                    dve.scalar_tensor_tensor(out=y[:, 1:S], in0=s[:, 0:S - 1], scalar=taps[f][0], in1=y[:, 1:S],
                                             op0=ALU.mult, op1=ALU.add).then_inc(conv_step, 1)
                for f in range(4):
                    y, s = cc[:, S * f:S * f + S], cu[:, S * f:S * f + S]
                    dve.wait_ge(conv_step, n0 + 6 + f)
                    dve.scalar_tensor_tensor(out=y[:, 0:S - 1], in0=s[:, 1:S], scalar=taps[f][2], in1=y[:, 0:S - 1],
                                             op0=ALU.mult, op1=ALU.add).then_inc(conv_step, 1)
                dve.wait_ge(conv_step, n0 + 13)
                dve.tensor_tensor(cc, cc, cb, ALU.mult).then_inc(conv_step, 1)

            def conv_lo(i):
                dve.wait_ge(conv_hi, i + 1)
                dve.wait_ge(conv_step, 15 * i + 14)
                dve.tensor_tensor(token_order(br_lo[:, 2, :]), time_order(conv["cc"]),
                                  token_order(br_hi[:, 2, :].bitcast(F32)), ALU.subtract)\
                   .then_inc(conv_step, 1)

            def attend(i, g):
                h, odd = g // 2, g % 2
                nh = NH * i + h
                if not odd and h >= 1:
                    hh = h - 1
                    dve.wait_ge(at_hi, NH * i + hh + 1)
                    dve.tensor_tensor(br_lo[:, 0, S * hh:S * hh + S], ps[:, 3072:3072 + S],
                                      br_hi[:, 0, S * hh:S * hh + S].bitcast(F32), ALU.subtract).then_inc(at_lo, 1)
                if not odd and h < NH:
                    dve.wait_ge(at_s, nh + 1)
                    if nh:
                        dve.wait_ge(at_exp, 2 * nh)
                    dve.tensor_reduce(small[:, 20:22], ps[:, 2048:3072].rearrange("p (q k) -> p q k", q=2),
                                      AX.X, ALU.max).then_inc(at_max, 1)
                    dve.wait_ge(at_max, nh + 1)
                    dve.tensor_scalar(small[:, 16:18], small[:, 20:22], -SCALE, None, ALU.mult).then_inc(at_nm, 1)
                    dve.wait_ge(at_exp, 2 * (nh + 1))
                    dve.reciprocal(small[:, 22:24], small[:, 18:20]).then_inc(at_dve, 1)
                    dve.wait_ge(at_dve, 3 * nh + 1)
                    if nh:
                        dve.wait_ge(at_t, 2 * nh)
                    for q in range(2):
                        dve.tensor_scalar(adiag[:, P * q:P * q + P], ident, small[:, 22 + q:23 + q], None, ALU.mult)\
                           .then_inc(at_dve, 1)
                if odd:
                    dve.wait_ge(at_t, 2 * nh + 2)
                    dve.tensor_copy(aPT[:, 512:1024], bank(7)).then_inc(at_pt_dve, 1)

            def merge(i, m):
                n, j = m // 2, m % 2
                f = NCHK + 2 * m + 1
                a = merged[:, 1024 * j:1024 * j + 1024]
                unit_done(dve, 0, U_L0 * i + fill_unit(f))
                dve.wait_ge(evac_act, 23 * i + NCHK + m + 1)
                if m > 2:
                    dve.wait_ge(mg, 4 * i + m - 2)
                src = ps[:, 1024 * (f % 2):1024 * (f % 2) + 1024]
                if n == 0:
                    dve.tensor_tensor(a, gtile, src, ALU.mult).then_inc(evac_dve, 1)
                else:
                    dve.tensor_tensor(utmp, gtile, src, ALU.mult).then_inc(evac_dve, 1)
                    dve.wait_ge(evac_dve, 6 * i + m + 1)
                    dve.tensor_tensor(a, a, utmp, ALU.add).then_inc(mg, 1)

            def mixer(i):
                base = U_L0 * i
                if i == 0:
                    for k in range(LEAD):
                        split(0, k)
                pre_norm(i, 0)
                for u in range(U_MIX):
                    split(0, base + u + LEAD)
                    if u == 7:
                        h_vec(i, 0, 0)
                    if u == 9:
                        h_vec(i, 0, 1)
                    if u == 12:
                        h_vec(i, 0, 2)
                    if u == 14:
                        dve.wait_ge(z_att, 2 * i + 1)
                        h_vec(i, 0, 3)
                    if u == 16:
                        convolve(i)
                    if u == 17:
                        conv_lo(i)
                        h_vec(i, 0, 4)
                    if u == 18:
                        h_vec(i, 0, 5)
                    if u == 19:
                        h_vec(i, 0, 6)
                    if u == 21:
                        h_vec(i, 1, 0)
                    if u == 22:
                        h_vec(i, 1, 1)
                    if u == 24:
                        h_vec(i, 1, 2)
                    if u == 26:
                        dve.wait_ge(z_att, 2 * i + 2)
                        h_vec(i, 1, 3)
                    if u == 28:
                        h_vec(i, 1, 4)
                    if u == 29:
                        h_vec(i, 1, 5)
                    if u == 30:
                        h_vec(i, 1, 6)
                    if u == 33:
                        h_post(i, 0)
                    if u == 34:
                        h_post(i, 1)
                    for r, name in enumerate(ROPED):
                        if u == 2 * CIDX[name] + 2:
                            rope(i, r)
                    if 35 <= u < 44:
                        attend(i, u - 35)
                    if u >= U_GATE + 3 and (u - U_GATE) % 3 == 0 and u < U_OUT + 1:
                        m = (u - U_GATE) // 3 - 1
                        merge(i, m)
                    if u == U_OUT:
                        dve.wait_ge(m_hi, i + 1)
                        dve.tensor_tensor(hT_lo[:, :, :].rearrange("p k t -> p (k t)"), merged,
                                          hT_hi[:, :, :].rearrange("p k t -> p (k t)").bitcast(F32),
                                          ALU.subtract).then_inc(m_lo, 1)

            def preamble():
                dve.wait_ge(prm_turned, 1)
                dve.tensor_copy(prm[:, :], bank(4)[:, 0:R_END]).then_inc(prm_ready, 1)
                dve.wait_ge(prm_ready, 1)
                n = 0

                def step(ins):
                    nonlocal n
                    n += 1
                    ins.then_inc(pre, 1)
                    dve.wait_ge(pre, n)

                lg = prm[:, R_LB:R_LB + 16].rearrange("p (s i k) -> p s i k", s=2, i=DEPTH)
                ex = small[:, 48:64].rearrange("p (s i k) -> p s i k", s=2, i=DEPTH)
                e2 = small[:, 64:80].rearrange("p (s i k) -> p s i k", s=2, i=DEPTH)
                mx = small[:, 24:32].rearrange("p (s a k) -> p s a k", s=2, a=1)
                step(dve.tensor_tensor(mx, lg[:, :, 0:1, :], lg[:, :, 1:2, :], ALU.max))
                for s in range(2):
                    step(dve.tensor_tensor(ex[:, s], lg[:, s], mx[:, s].to_broadcast([P, DEPTH, NH]), ALU.subtract))
                assert n == PRE_LB
                dve.wait_ge(pre_act, 1)
                step(dve.tensor_tensor(mx, e2[:, :, 0:1, :], e2[:, :, 1:2, :], ALU.add))
                step(dve.reciprocal(mx, mx))
                for s in range(2):
                    step(dve.tensor_tensor(e2[:, s], e2[:, s], mx[:, s].to_broadcast([P, DEPTH, NH]), ALU.mult))
                step(dve.tensor_tensor(ex[:, :, 1:2, :], e2[:, :, 0:1, :], e2[:, :, 1:2, :], ALU.add))
                step(dve.tensor_tensor(lb[:, :, 0:1, :], e2[:, :, 0:1, :], e2[:, :, 0:1, :], ALU.subtract))
                step(dve.tensor_tensor(lb[:, :, 1:2, :], ex[:, :, 1:2, :], e2[:, :, 0:1, :], ALU.subtract))
                step(dve.tensor_scalar(omlb[:, :, :, :], lb[:, :, :, :], -1.0, 1.0, ALU.mult, ALU.add))
                dve.wait_ge(pos_loaded, 16)
                pf = arena[0:ROT, 3584:3584 + S]
                kr = arena[0:ROT, 3840:3840 + S]
                step(dve.tensor_copy(pf.rearrange("p (r i) -> p r i", r=4),
                                     arena[0:ROT, 3072:3072 + S].bitcast(I32).rearrange("p (i r) -> p r i", r=4)))
                step(dve.tensor_scalar(pf, pf, inv_freq, None, ALU.mult))
                for w, (shift, turn) in enumerate(((HALF_PI, 0.25), (0.0, 0.0))):
                    r = rc[:, w, :]
                    step(dve.tensor_scalar(kr, pf, INV_2PI, turn, ALU.mult, ALU.add))
                    step(dve.tensor_scalar(kr, kr, ROUND, ROUND, ALU.add, ALU.subtract))
                    step(dve.scalar_tensor_tensor(out=r, in0=kr, scalar=-PI2[0], in1=pf, op0=ALU.mult, op1=ALU.add))
                    step(dve.scalar_tensor_tensor(out=r, in0=kr, scalar=-PI2[1], in1=r, op0=ALU.mult, op1=ALU.add))
                    step(dve.scalar_tensor_tensor(out=r, in0=kr, scalar=-PI2[2], in1=r, op0=ALU.mult, op1=ALU.add))
                    step(dve.tensor_scalar(r, r, shift, PI_IN, ALU.add, ALU.min))
                    step(dve.tensor_scalar(r, r, -PI_IN, None, ALU.max))
                assert n == PRE_ROPE

            def p_split(i):
                dve.wait_ge(p_hi, i + 1)
                dve.tensor_tensor(br_lo[:, 2, 0:512], bank(7), br_hi[:, 2, 0:512].bitcast(F32), ALU.subtract)\
                   .then_inc(p_lo, 1)

            def dense(base):
                k = base + LEAD

                def hidden(turns, kk, c, n=1024):
                    unit_done(dve, turns, kk)
                    dve.wait_ge(d_sg, c + 1)
                    dve.tensor_tensor(dsg[:, 0:n], dsg[:, 0:n], ps[:, 512 * 6:512 * 6 + n], ALU.mult)\
                       .then_inc(d_hid, 1)
                    dve.wait_ge(d_hi, c + 1)
                    dve.wait_ge(d_hid, c + 1)
                    dve.tensor_tensor(br_lo[:, 0, 0:n], dsg[:, 0:n], br_hi[:, 0, 0:n].bitcast(F32),
                                      ALU.subtract).then_inc(d_lo, 1)

                for u in range(4):
                    split(0, k)
                    k += 1
                hidden(0, base + 3, 0)
                turn0, k0 = k // RING, k % RING
                with dve.Fori(1, NFC) as c:
                    turns = c + (turn0 - 1)
                    for u in range(6):
                        split(turns, k0 + u)
                    hidden(turns, k0 - LEAD + 5, c)
                k += 6 * (NFC - 1)
                for u in range(5):
                    split(0, k + u)
                    if u == 3:
                        hidden(0, k - LEAD + 3, NFC, 512)

            def route():
                n = 0

                def step(ins):
                    nonlocal n
                    n += 1
                    ins.then_inc(r_step, 1)
                    dve.wait_ge(r_step, n)

                dve.wait_ge(r_split, 1)
                dve.tensor_tensor(r_lo[:, :], rout, r_hi[:, :].bitcast(F32), ALU.subtract).then_inc(r_split, 1)
                dve.wait_ge(r_log, 1)
                lg = rt[:, 0:16]
                step(dve.tensor_copy(lg, bank(4)[:, 0:16]))
                for t in range(NT):
                    m8, i8 = rt[:, 16:24], rt[:, 24:32].bitcast(U32)
                    cols = lg[:, 8 * t:8 * t + 8]
                    step(dve.max(out=m8, in_=cols))
                    step(dve.max_index(out=i8, in_max=m8, in_values=cols))
                    step(dve.tensor_copy(rt[:, 32:40], i8))
                    step(dve.tensor_scalar(rt[:, 40:48], iota8, rt[:, 32:33], None, ALU.is_equal))
                    step(dve.tensor_scalar(rt[:, 48:56], iota8, rt[:, 33:34], None, ALU.is_equal))
                    step(dve.tensor_tensor(rt[:, RT_M + 8 * t:RT_M + 8 * t + 8], rt[:, 40:48], rt[:, 48:56], ALU.add))
                    step(dve.tensor_scalar(rt[:, RT_DF + 8 * t:RT_DF + 8 * t + 8], cols, m8[:, 0:1], None,
                                           ALU.subtract))
                assert n == R_DIFF
                dve.wait_ge(r_exp, 1)
                step(dve.tensor_tensor(rt[:, RT_CB:RT_CB + 16], rt[:, RT_EX:RT_EX + 16], rt[:, RT_M:RT_M + 16],
                                       ALU.mult))
                step(dve.tensor_reduce(rt[:, 40:42], rt[:, RT_CB:RT_CB + 16].rearrange("p (t e) -> p t e", t=NT),
                                       AX.X, ALU.add))
                step(dve.reciprocal(rt[:, 42:44], rt[:, 40:42]))
                for t in range(NT):
                    c = rt[:, RT_CB + 8 * t:RT_CB + 8 * t + 8]
                    step(dve.tensor_scalar(c, c, rt[:, 42 + t:43 + t], None, ALU.mult))
                dve.wait_ge(r_rank, 1)
                re = rt[:, RT_RE:RT_RE + 16]
                step(dve.tensor_scalar(re, bank(5)[:, 0:16], 1.0, None, ALU.add))
                step(dve.tensor_tensor(re, re, rt[:, RT_M:RT_M + 16], ALU.mult))
                step(dve.tensor_scalar(re, re, -1.0, None, ALU.add))
                step(dve.tensor_reduce(rt[:, 44:45], bank(5)[:, 16:24], AX.X, ALU.max))
                step(dve.tensor_scalar(rt[:, 45:46], rt[:, 44:45], float(P), 1.0, ALU.is_gt, ALU.add))
                dve.tensor_copy(nsw_i[:, :], rt[:, 45:46]).then_inc(sweeps_ready, 1)
                dve.memset(yacc, 0.0).then_inc(e_acc, 1)

            def experts(base):
                dve.wait_ge(sweeps_ready, 1)
                sweeps = dve.value_load(nsw_i[0:1, 0:1], min_val=1, max_val=2)
                k = base + LEAD
                turn0, k0 = k // RING, k % RING
                gw = prm[:, R_FFN + KT:R_FFN + 2 * KT].rearrange("p (k a) -> p k a", a=1).to_broadcast([P, KT, P])
                rev = rt[:, RT_RE:RT_RE + 16].rearrange("p (t e) -> p t e", t=NT)
                cbv = rt[:, RT_CB:RT_CB + 16].rearrange("p (t e) -> p t e", t=NT)
                dve.sem_inc(e_step, ONE)
                with dve.Fori(0, sweeps) as s:
                    with dve.Fori(0, NE) as e:
                        it = s * NE + e
                        turns = it * TURNS_EXP + turn0
                        e0 = it * 4 + s + ONE

                        def turn(c):
                            dve.wait_ge(e_thi, it * NEC + c + 1)
                            dve.tensor_tensor(br_lo[:, 0, 0:512], bank(6), br_hi[:, 0, 0:512].bitcast(F32),
                                              ALU.subtract).then_inc(e_tlo, 1)

                        dve.wait_ge(e_step, e0)
                        dve.tensor_copy(rk[:, 0:2].rearrange("p (t a) -> p t a", a=1), rev[:, :, bass.ds(e, 1)])\
                           .then_inc(e_step, 1)
                        dve.tensor_copy(rk[:, 2:4].rearrange("p (t a) -> p t a", a=1), cbv[:, :, bass.ds(e, 1)])\
                           .then_inc(e_step, 1)
                        dve.wait_ge(e_step, e0 + 2)
                        dve.wait_ge(e_selc, it + ONE)
                        for t in range(NT):
                            dve.tensor_scalar(sel[:, P * t:P * t + P], iota, rk[:, t:t + 1], None, ALU.is_equal)\
                               .then_inc(e_sel, 1)
                            dve.tensor_scalar(selc[:, P * t:P * t + P], iota, rk[:, t:t + 1], rk[:, 2 + t:3 + t],
                                              ALU.is_equal, ALU.mult).then_inc(e_sel, 1)
                        dve.wait_ge(e_gath, it + 1)
                        dve.tensor_tensor(xg.rearrange("p (k t) -> p k t", k=KT),
                                          ps[:, 1024:2048].rearrange("p (k t) -> p k t", k=KT), gw, ALU.mult)\
                           .then_inc(e_step, 1)
                        dve.wait_ge(e_selc, it + (1 + ONE))
                        dve.tensor_copy(selct, bank(7)[:, 0:256]).then_inc(e_step, 1)
                        dve.wait_ge(e_xhi, it + 1)
                        dve.wait_ge(e_step, e0 + 3)
                        dve.tensor_tensor(br_lo[:, 1, :], xg, br_hi[:, 1, :].bitcast(F32), ALU.subtract)\
                           .then_inc(e_xlo, 1)
                        kk = k0
                        for c in range(NEC):
                            for u in range(4 if c == 0 else 6):
                                split(turns, kk)
                                kk += 1
                                if c and u == 1:
                                    turn(c - 1)
                                if u == 3:
                                    dve.wait_ge(e_sg, it * NEC + c + 1)
                                    unit_done(dve, turns, kk - LEAD - 1)
                                    dve.wait_ge(e_turn, it * NEC + (c + ONE))
                                    dve.tensor_tensor(hid, msg, bank(5), ALU.mult).then_inc(e_hid, 1)
                        turn(NEC - 1)
                        split(turns, kk)
                        split(turns, kk + 1)
                        for t in range(NT):
                            dve.wait_ge(e_scat, it + 1)
                            dve.wait_ge(e_acc, it * 2 + (1 + t))
                            a = yacc[:, DM * t:DM * t + DM]
                            dve.tensor_tensor(a, a, ps[:, 1024 * (1 + t):1024 * (2 + t)], ALU.add).then_inc(e_acc, 1)
                    dve.wait_ge(e_step, (s + 1) * (NE * 4) + s + ONE)
                    dve.tensor_scalar(rt[:, RT_RE:RT_RE + 16], rt[:, RT_RE:RT_RE + 16], -float(P), None, ALU.add)\
                       .then_inc(e_step, 1)
                return sweeps

            def ple(i, turns, k):
                n_units = (U_PLE - 1) if i == DEPTH - 1 else U_PLE
                k += LEAD
                for u in range(n_units):
                    split(turns, k + u)
                dve.wait_ge(pl_sig, i + 1)
                dve.tensor_tensor(eprod, sig, ps[:, 2048:4096], ALU.mult).then_inc(pl_prod, 1)
                post_norm(3 * i + 2, lambda t: eprod[:, DM * t:DM * t + DM])

            def y_psum(t):
                return ps[:, DM * t:DM * t + DM]

            preamble()
            mixer(0)
            post_norm(0, y_psum)
            pre_norm(0, 1)
            p_split(0)
            dense(U_MIX)
            post_norm(1, y_psum)
            pre_norm(0, 2)
            ple(0, 0, U_MIX + U_DENSE)
            mixer(1)
            post_norm(3, y_psum)
            pre_norm(1, 1)
            p_split(1)
            route()
            sweeps = experts(U_L0 + U_MIX)
            dve.wait_ge(e_acc, sweeps * (NE * 2) + 1)
            post_norm(4, lambda t: yacc[:, DM * t:DM * t + DM])
            pre_norm(1, 2)
            k = U_L0 + U_MIX
            ple(1, sweeps * (NE * TURNS_EXP) + k // RING, k % RING)

        @block.gpsimd
        def _(pool):
            pool.memset(minus_half[:, :], -0.5).then_inc(half_ready, 1)
            pool.wait_ge(half_ready, 1)
            for i in range(DEPTH):
                for m in range(3):
                    n = 3 * i + m
                    pool.wait_ge(var_ready, n + 1)
                    pool.tensor_tensor(small[:, 8:10], small[:, 2:4], minus_half[:, 0:2], ALU.pow).then_inc(rstd_ready, 1)
                    if m == 0:
                        for d in range(2):
                            if d:
                                pool.wait_ge(h_pe, hpe(i, 0, 3))
                            else:
                                pool.wait_ge(xn_ready, NT * (n + 1))
                            pool.memset(attT, 0.0).then_inc(z_att, 1)
                        pool.wait_ge(h_dve, hdve(i, 2, 1))
                        pool.tensor_tensor(small[:, 88:96], small[:, 80:88], minus_half[:, :], ALU.pow).then_inc(h_pow, 1)
                    pool.wait_ge(post_var, n + 1)
                    pool.tensor_tensor(small[:, 10:12], small[:, 6:8], minus_half[:, 0:2], ALU.pow).then_inc(post_rstd, 1)

        @block.tensor
        def _(pe):
            def mm3(o, l_hi, l_lo, r_hi_, r_lo_, start):
                pe.matmul(o, l_hi, r_hi_, start=start, stop=False, skip_group_check=True)
                pe.matmul(o, l_hi, r_lo_, start=False, stop=False, skip_group_check=True)
                return pe.matmul(o, l_lo, r_hi_, start=False, stop=True, skip_group_check=True)

            def take(turns, k, h):
                pe.wait_ge(lo_ready, turns * (RING * PARTS) + PARTS * k + h + 1)

            def feat_unit(turns, k, b0, kh, a_hi, a_lo, nk=4):
                wh, wl = unit_w(w_hi, k), unit_w(w_lo, k)
                for h in range(PARTS):
                    take(turns, k, h)
                    for f in range(4):
                        o = ps[:, 512 * b0 + S * f:512 * b0 + S * f + S]
                        for kk in (2 * h, 2 * h + 1):
                            ins = mm3(o, wh[:, kk, P * f:P * f + P], wl[:, kk, P * f:P * f + P],
                                      a_hi[:, 4 * kh + kk, :], a_lo[:, 4 * kh + kk, :],
                                      start=(kh == 0 and kk == 0 and f % 2 == 0))
                    ins.then_inc(part_used, 1)

            def tok_unit(turns, k, outs, kh, a, starts):
                wh, wl = unit_w(w_hi, k), unit_w(w_lo, k)
                for h in range(PARTS):
                    take(turns, k, h)
                    for t, o in enumerate(outs):
                        for kk in (2 * h, 2 * h + 1):
                            ah, al = a(t, 4 * kh + kk)
                            ins = mm3(o, ah, al, wh[:, kk, :], wl[:, kk, :], start=(starts and kk == 0))
                    ins.then_inc(part_used, 1)

            def hT_nat(t, k):
                return hT_hi[:, k, P * t:P * t + P], hT_lo[:, k, P * t:P * t + P]

            def pre_norm(i, m):
                n = 3 * i + m
                pe.wait_ge(xn_ready, NT * (n + 1))
                for k in range(KT):
                    for t in range(NT):
                        ins = pe.transpose(ps[:, S * k + P * t:S * k + P * t + P],
                                           xn[:, DM * t + P * k:DM * t + P * k + P], ident)
                    if k % 2:
                        ins.then_inc(turned, 1)
                pe.wait_ge(hT_lo_ready, KT * (n + 1))

            def fill_wait(i, f):
                f -= 2
                if f < 0:
                    return
                if f < NCHK:
                    if CHUNKS[f][0] in ROPED:
                        pe.wait_ge(rope_step, 12 * i + 2 * ROPED.index(CHUNKS[f][0]) + 2)
                    pe.wait_ge(evac_act, 23 * i + f + 1)
                elif (f - NCHK) % 2 == 0:
                    pe.wait_ge(evac_act, 23 * i + NCHK + (f - NCHK) // 2 + 1)
                else:
                    pe.wait_ge(evac_dve, 6 * i + (f - NCHK) // 2 + 1)

            def rotate(i, r):
                name = ROPED[r]
                c = CIDX[name]
                pe.wait_ge(evac_act, 23 * i + c + 1)
                for j in range(2):
                    ins = pe.matmul(ps[0:ROT, 1024 * (c % 2) + 512 * j:1024 * (c % 2) + 512 * j + 512], rotm,
                                    A[name][0:ROT, 512 * j:512 * j + 512], start=True, stop=True)
                ins.then_inc(rot_done, 1)

            def h_step(i, d, step):
                chunks = range(NCH) if d == 0 else range(NCH - 1, -1, -1)
                v = B["inp"]

                def inter(c):
                    for h in range(NH):
                        ins = pe.matmul(ps[:, 3072 + S * h + CH * c:3072 + S * h + CH * c + CH],
                                        hS[:, HD * h:HD * h + HD], hC[:, S * h + CH * c:S * h + CH * c + CH],
                                        start=False, stop=True, skip_group_check=True)
                    return ins

                def outer(c):
                    p0, t = CH * (c % 2), c // 2
                    for h in range(NH):
                        ins = pe.matmul(bank(4)[:, HD * h:HD * h + HD],
                                        kdT[p0:p0 + CH, 256 * h + P * t:256 * h + P * t + P],
                                        v[p0:p0 + CH, 512 * t + HD * h:512 * t + HD * h + HD], start=True, stop=True)
                    return ins

                if step == 1:
                    pe.wait_ge(h_dve, hdve(i, d, 13))
                    for j in range(NH * NT):
                        cols = slice(P * j, P * j + P)
                        ins = pe.matmul(ps[:, 2048 + P * j:2048 + P * j + P], hL[:, cols], h1[:, cols],
                                        start=True, stop=True)
                    ins.then_inc(h_pe, 1)
                if step == 2:
                    pe.wait_ge(h_dve, hdve(i, d, 20))
                    for j in range(NH * NT):
                        ins = pe.transpose(ps[:, 2048 + P * j:2048 + P * j + P], h2[:, P * j:P * j + P], ident)
                    ins.then_inc(h_pe, 1)
                if step == 3:
                    pe.wait_ge(h_act, hact(i, d, 8))
                    for h in range(NH):
                        for t in range(NT):
                            j = NT * h + t
                            pe.matmul(ps[:, 3072 + P * j:3072 + P * j + P],
                                      B["inp"][:, 512 * t + HD * h:512 * t + HD * h + HD], attT[:, P * j:P * j + P],
                                      start=(d == 0 and t == 0 and h % 2 == 0), stop=True, skip_group_check=True)
                    outer(chunks[0]).then_inc(h_pe, 1)
                if step in (4, 5):
                    pe.wait_ge(h_dve, hdve(i, d, 21 + 4 * (step - 4)))
                    if step == 4:
                        pe.wait_ge(h_dve, hdve(i, d, 19))
                    inter(chunks[step - 3])
                    outer(chunks[step - 3]).then_inc(h_pe, 1)
                if step == 6:
                    pe.wait_ge(h_dve, hdve(i, d, 29))
                    inter(chunks[3]).then_inc(h_pe, 1)

            def h_post(i, step):
                if step == 0:
                    pe.wait_ge(h_act, hact(i, 2, 2))
                    for j in range(8):
                        ins = pe.matmul(bank(4)[:, j:j + 1], hL[:, P * j:P * j + P], ones[:, 0:1], start=True, stop=True)
                    ins.then_inc(h_pe, 1)
                else:
                    pe.wait_ge(h_dve, hdve(i, 2, 9))
                    for j in range(2):
                        ins = pe.matmul(bank(4 + j), ones, hC[:, 512 * j:512 * j + 512], start=True, stop=True)
                    ins.then_inc(h_pe, 1)

            def attend(i, g):
                h, odd = g // 2, g % 2
                nh = NH * i + h
                if not odd and h >= 1:
                    hh = h - 1
                    pe.wait_ge(at_pt_act, NH * i + hh + 1)
                    pe.wait_ge(at_pt_dve, NH * i + hh + 1)
                    for q in range(2):
                        o = ps[:, 3072 + P * q:3072 + P * q + P]
                        for j, (grp, t) in enumerate(((0, 0), (0, 1), (1, q), (2, q))):
                            ins = pe.matmul(o, A[f"av{grp}"][:, 512 * t + HD * hh:512 * t + HD * hh + HD],
                                            aPT[:, 512 * q + P * j:512 * q + P * j + P], start=(j == 0), stop=(j == 3))
                    ins.then_inc(at_v, 1)
                if not odd and h < NH:
                    if h == 0:
                        pe.wait_ge(rope_step, 12 * (i + 1))
                        pe.wait_ge(evac_act, 23 * i + NCHK)
                        pe.wait_ge(h_dve, hdve(i, 2, 13))
                    else:
                        pe.wait_ge(at_exp, 2 * nh)
                    hs = slice(S * h, S * h + S)
                    for q in range(2):
                        pe.matmul(bank(4 + q), identb[:, :], maskb[:, q, :], start=True, stop=False,
                                  skip_group_check=True)
                        for grp in range(NG):
                            qT = A[f"aq{grp}"][:, S * h + P * q:S * h + P * q + P]
                            kT = A[f"ak{grp}"][:, hs]
                            if grp == 0:
                                o = ps[:, 2048 + 512 * q:2048 + 512 * q + S]
                            else:
                                kT = A[f"ak{grp}"][:, S * h + P * q:S * h + P * q + P]
                                o = ps[:, 2048 + 512 * q + P * (grp + 1):2048 + 512 * q + P * (grp + 2)]
                            ins = pe.matmul(o, qT, kT, start=False, stop=True, skip_group_check=True)
                    ins.then_inc(at_s, 1)
                if odd:
                    pe.wait_ge(at_dve, 3 * (nh + 1))
                    if h:
                        pe.wait_ge(at_lo, NH * i + h)
                    else:
                        pe.wait_ge(h_act, hact(i, 2, 2))
                    for q in range(2):
                        for j in range(4):
                            ins = pe.matmul(bank(6 + q)[:, P * j:P * j + P], aP[:, 512 * q + P * j:512 * q + P * j + P],
                                            adiag[:, P * q:P * q + P], start=True, stop=True)
                        ins.then_inc(at_t, 1)

            def mixer(i):
                base = U_L0 * i
                pre_norm(i, 0)
                for u in range(U_MIX):
                    k = base + u
                    if u < U_GATE:
                        c, kh = u // 2, u % 2
                        name, _, layout = CHUNKS[c]
                        if kh == 0:
                            fill_wait(i, c)
                        b0 = 2 * (c % 2)
                        if layout == "feat":
                            feat_unit(0, k, b0, kh, hT_hi, hT_lo)
                        else:
                            tok_unit(0, k, [bank(b0), bank(b0 + 1)], kh, hT_nat, kh == 0)
                    elif u < U_OUT:
                        m, r = divmod(u - U_GATE, 3)
                        f = NCHK + 2 * m + (r == 2)
                        if r != 1:
                            fill_wait(i, f)
                        b0 = 2 * (f % 2)
                        if r < 2:
                            feat_unit(0, k, b0, r, hT_hi, hT_lo)
                        else:
                            n = BRANCH_ORDER[m // 2]
                            if n == 2:
                                pe.wait_ge(conv_step, 15 * (i + 1))
                            elif n == 1:
                                pe.wait_ge(h_dve, hdve(i, 2, 15))
                            else:
                                pe.wait_ge(at_lo, NH * (i + 1))
                            feat_unit(0, k, b0, 0, br_hi[:, n, :].rearrange("p (k t) -> p k t", k=4),
                                      br_lo[:, n, :].rearrange("p (k t) -> p k t", k=4))
                    else:
                        j, kh = divmod(u - U_OUT, 2)
                        if u == U_OUT:
                            pe.wait_ge(m_lo, i + 1)
                        tok_unit(0, k, [bank(j), bank(2 + j)], kh, hT_nat, kh == 0)
                    for r, name in enumerate(ROPED):
                        if u == 2 * CIDX[name] + 2:
                            rotate(i, r)
                    if u == 8:
                        pe.wait_ge(evac_act, 23 * i + CIDX["inp"] + 1)
                        for t in range(NT):
                            for h in range(NH):
                                ins = pe.transpose(bank(4 + t)[:, HD * h:HD * h + HD],
                                                   h1[:, S * h + P * t:S * h + P * t + P], ident)
                        ins.then_inc(inp_turned, 1)
                    if u == 14:
                        h_step(i, 0, 1)
                    if u == 15:
                        h_step(i, 0, 2)
                    if u == 16:
                        h_step(i, 0, 3)
                    if u == 17:
                        h_step(i, 0, 4)
                    if u == 18:
                        h_step(i, 0, 5)
                    if u == 20:
                        h_step(i, 0, 6)
                    if u == 25:
                        h_step(i, 1, 1)
                    if u == 26:
                        h_step(i, 1, 2)
                    if u == 27:
                        h_step(i, 1, 3)
                    if u == 28:
                        h_step(i, 1, 4)
                    if u == 29:
                        h_step(i, 1, 5)
                    if u == 31:
                        h_step(i, 1, 6)
                    if u == 32:
                        h_post(i, 0)
                    if u == 33:
                        h_post(i, 1)
                    if 35 <= u < 44:
                        attend(i, u - 35)

            def p_turn(i):
                pe.wait_ge(p_loaded, 64 * (i + 1))
                for kk in range(2):
                    for t in range(NT):
                        ins = pe.transpose(bank(7)[:, S * kk + P * t:S * kk + P * t + P],
                                           ptok[:, PLE * t + P * kk:PLE * t + P * kk + P], ident)
                ins.then_inc(p_turned, 1)

            def dense(base):
                k = base

                def feats(turns, kk, b0, kh):
                    feat_unit(turns, kk, b0, kh, hT_hi, hT_lo)

                def hT4(t, kk):
                    return (br_hi[:, 0, S * kk + P * t:S * kk + P * t + P],
                            br_lo[:, 0, S * kk + P * t:S * kk + P * t + P])

                def down(turns, kk, c, first=False):
                    for j in range(2):
                        tok_unit(turns, kk + j, [bank(j), bank(2 + j)], 0, hT4, first)

                pe.wait_ge(p_lo, 1)
                for kh in range(2):
                    feats(0, k + kh, 4, kh)
                for kh in range(2):
                    feats(0, k + 2 + kh, 6, kh)
                k += 4

                def body(turns, kk, c, first):
                    pe.wait_ge(d_sg, c)
                    for kh in range(2):
                        feats(turns, kk + kh, 4, kh)
                        pe.wait_ge(d_lo, c)
                    down(turns, kk + 2, c - 1, first)
                    for kh in range(2):
                        feats(turns, kk + 4 + kh, 6, kh)
    
                body(0, k, 1, True)
                k += 6
                turn0, k0 = k // RING, k % RING
                with pe.Fori(2, NFC) as c:
                    body(c + (turn0 - 2), k0, c, False)
                k += 6 * (NFC - 2)
                def half(kk, b):
                    wh, wl = (w[:, kk % NSPL, :].rearrange("p (k n) -> p k n", k=KT) for w in (w_hi, w_lo))
                    for h in range(PARTS):
                        take(0, kk, h)
                        for f in range(2):
                            for kx in range(4 * h, 4 * h + 4):
                                ins = mm3(ps[:, 512 * b + S * f:512 * b + S * f + S], wh[:, kx, P * f:P * f + P],
                                          wl[:, kx, P * f:P * f + P], hT_hi[:, kx, :], hT_lo[:, kx, :],
                                          start=(kx == 0 and f == 0))
                        ins.then_inc(part_used, 1)

                pe.wait_ge(d_sg, NFC)
                half(k, 4)
                pe.wait_ge(d_lo, NFC)
                down(0, k + 1, NFC - 1)
                half(k + 3, 6)
                pe.wait_ge(d_lo, NFC + 1)
                kk = k + 4
                wh, wl = (w[:, kk % NSPL, :].rearrange("p (k n) -> p k n", k=2) for w in (w_hi, w_lo))
                for kx in range(2):
                    take(0, kk, kx)
                    for t in range(NT):
                        for j in range(2):
                            ah, al = hT4(t, kx)
                            ins = mm3(bank(2 * t + j), ah, al, wh[:, kx, 512 * j:512 * j + 512],
                                      wl[:, kx, 512 * j:512 * j + 512], start=False)
                    ins.then_inc(part_used, 1)

            def route():
                pe.wait_ge(r_split, 2)
                for t in range(NT):
                    for k in range(KT):
                        ah, al = hT_nat(t, k)
                        ins = mm3(bank(4)[:, NE * t:NE * t + NE], ah, al, r_hi[:, NE * k:NE * k + NE],
                                  r_lo[:, NE * k:NE * k + NE], start=(t == 0 and k == 0))
                ins.then_inc(r_log, 1)
                pe.wait_ge(r_step, R_DIFF)
                mk = [rt[:, RT_M + NE * t:RT_M + NE * t + NE] for t in range(NT)]
                b = bank(5)
                pe.matmul(b[:, 0:8], lower, mk[0], start=True, stop=True)
                pe.matmul(b[:, 8:16], lower, mk[1], start=True, stop=False)
                pe.matmul(b[:, 8:16], ones, mk[0], start=False, stop=True)
                pe.matmul(b[:, 16:24], ones, mk[0], start=True, stop=False)
                pe.matmul(b[:, 16:24], ones, mk[1], start=False, stop=True).then_inc(r_rank, 1)

            def experts(base):
                pe.wait_ge(sweeps_ready, 1)
                sweeps = pe.value_load(nsw_i[0:1, 0:1], min_val=1, max_val=2)
                turn0, k0 = base // RING, base % RING
                pe.sem_inc(e_selc, ONE)
                pe.sem_inc(e_turn, ONE)
                with pe.Fori(0, sweeps) as s:
                    with pe.Fori(0, NE) as e:
                        it = s * NE + e
                        turns = it * TURNS_EXP + turn0

                        def xg4(t, k):
                            return br_hi[:, 1, P * k:P * k + P], br_lo[:, 1, P * k:P * k + P]

                        def hid4(t, k):
                            return br_hi[:, 0, P * k:P * k + P], br_lo[:, 0, P * k:P * k + P]

                        def turn(c):
                            pe.wait_ge(e_hid, it * NEC + c + 1)
                            if c:
                                pe.wait_ge(e_tlo, it * NEC + c)
                            for f in range(4):
                                ins = pe.transpose(bank(6)[:, P * f:P * f + P], hid[:, P * f:P * f + P], ident)
                            ins.then_inc(e_turn, 1)

                        pe.wait_ge(e_sel, (it + 1) * 4)
                        pe.wait_ge(e_acc, it * 2 + 1)
                        for k in range(KT):
                            for t in range(NT):
                                ins = pe.matmul(ps[:, 1024 + P * k:1024 + P * k + P],
                                                xn[:, DM * t + P * k:DM * t + P * k + P], sel[:, P * t:P * t + P],
                                                start=(t == 0), stop=(t == NT - 1))
                        ins.then_inc(e_gath, 1)
                        for t in range(NT):
                            ins = pe.transpose(bank(7)[:, P * t:P * t + P], selc[:, P * t:P * t + P], ident)
                        ins.then_inc(e_selc, 1)
                        pe.wait_ge(e_xlo, it + 1)
                        kk = k0
                        for c in range(NEC):
                            if c:
                                pe.wait_ge(e_sg, it * NEC + c)
                            for kh in range(2):
                                tok_unit(turns, kk, [bank(4)], kh, xg4, kh == 0)
                                kk += 1
                            if c:
                                turn(c - 1)
                            for kh in range(2):
                                tok_unit(turns, kk, [bank(5)], kh, xg4, kh == 0)
                                kk += 1
                            if c:
                                pe.wait_ge(e_tlo, it * NEC + c)
                                for j in range(2):
                                    tok_unit(turns, kk, [bank(j)], 0, hid4, c == 1)
                                    kk += 1
                        turn(NEC - 1)
                        pe.wait_ge(e_tlo, it * NEC + NEC)
                        for j in range(2):
                            tok_unit(turns, kk, [bank(j)], 0, hid4, False)
                            kk += 1
                        pe.wait_ge(e_ye, it + 1)
                        pe.wait_ge(e_step, it * 4 + s + (4 + ONE))
                        for t in range(NT):
                            for j in range(2):
                                ins = pe.matmul(bank(2 + 2 * t + j), selct[:, P * t:P * t + P],
                                                ye[:, 512 * j:512 * j + 512], start=True, stop=True)
                        ins.then_inc(e_scat, 1)
                return sweeps

            def ple(i, turns, k):
                pe.wait_ge(p_lo, i + 1)
                wh, wl = (w[:, k % NSPL, :].rearrange("p (k n) -> p k n", k=2) for w in (w_hi, w_lo))
                for kx in range(2):
                    take(turns, k, kx)
                    for t in range(NT):
                        for j in range(2):
                            ins = mm3(bank(4 + 2 * t + j), br_hi[:, 2, S * kx + P * t:S * kx + P * t + P],
                                      br_lo[:, 2, S * kx + P * t:S * kx + P * t + P],
                                      wh[:, kx, 512 * j:512 * j + 512], wl[:, kx, 512 * j:512 * j + 512],
                                      start=(kx == 0))
                    ins.then_inc(part_used, 1)
                pre_norm(i, 2)
                for j in range(2):
                    for kh in range(2):
                        k += 1
                        tok_unit(turns, k, [bank(j), bank(2 + j)], kh, hT_nat, kh == 0)

            pe.wait_ge(const_loaded, 16 * 9)
            pe.transpose(bank(4)[:, 0:R_END], arena[0:R_END, 2048:2048 + P], cst[0:R_END, C_ID:C_ID + R_END])\
              .then_inc(prm_turned, 1)
            mixer(0)
            pre_norm(0, 1)
            p_turn(0)
            dense(U_MIX)
            ple(0, 0, U_MIX + U_DENSE)
            mixer(1)
            pre_norm(1, 1)
            p_turn(1)
            route()
            sweeps = experts(U_L0 + U_MIX)
            pe.wait_ge(e_acc, sweeps * (NE * 2) + 1)
            k = U_L0 + U_MIX
            ple(1, sweeps * (NE * TURNS_EXP) + k // RING, k % RING)


ONE = 1
RT_M, RT_DF, RT_EX, RT_CB, RT_RE = 56, 72, 88, 104, 120
R_DIFF = 1 + 7 * NT
PRE_LB = 3
PRE_ROPE = PRE_LB + 8 + 2 + 14
INV_2PI = 0.15915494309189535
HALF_PI = 1.5707963267948966
PI_IN = 3.1415925
PI2 = (6.28125, 0.0019350051879882812, 3.0199159819567e-07)
ROUND = 12582912.0


def shape_constants(np):
    c = np.zeros((P, C_END), np.float32)
    r = np.arange(P)
    c[:, C_ID:C_ID + P] = np.eye(P)
    c[:, C_ONE:C_ONE + P] = 1.0
    c[:, C_LT:C_LT + P] = r[:, None] < r[None, :]
    c[:, C_IOTA:C_IOTA + P] = r[None, :]
    c[:, C_SCAN:C_SCAN + 512] = np.arange(512)[None, :] % CH != 0
    s, t = r[:, None], r[None, :]
    c[:, C_MASK:C_MASK + P] = (s <= t) & (s // CH == t // CH)
    c[:, C_MASK + P:C_MASK + 2 * P] = (s >= t) & (s // CH == t // CH)
    half = ROT // 2
    for m in range(half):
        c[m + half, C_ROT + m] = -1.0
        c[m, C_ROT + half + m] = 1.0
    c[0:ROT, C_INV] = (500000.0 ** (-(np.arange(ROT) % half) * 2.0 / ROT)).astype(np.float32)
    c[:, C_I8:C_I8 + NE] = np.arange(NE)[None, :]
    order = np.array([4 * i + res for res in range(4) for i in range(S // 4)])
    mask = np.zeros((P, 2, 512), np.float32)
    for q in range(2):
        tq = order[P * q:P * q + P][:, None]
        own = order[P * q:P * q + P][None, :]
        mask[:, q, 0:S] = np.where(np.abs(tq - order[None, :]) <= 64, 0.0, -1e30)
        mask[:, q, S:S + P] = np.where((tq - own) % 4 == 0, 0.0, -1e30)
        mask[:, q, S + P:S + 2 * P] = np.where((tq - own) % 16 == 0, 0.0, -1e30)
    return c, mask, np.eye(P)


_INS = ["x", "p", "positions", "w_in", "conv_w", "hgrn_lb_logits", "hgrn_norm_g", "w_branch", "w_out",
        "g_mix_pre", "g_mix_post", "g_ffn_pre", "g_ffn_post", "dense_w_gate", "dense_w_up", "dense_w_down",
        "moe_router", "moe_w_gate", "moe_w_up", "moe_w_down", "ple_w_proj", "ple_w_gate", "ple_g_in", "ple_g_post"]


def kernel(**inputs):
    import ml_dtypes as _ml
    import numpy as _np
    import concourse.bacc as _bacc
    from concourse import mybir as _mybir
    from concourse.bass_utils import run_bass_kernel_spmd as _run

    nc = _bacc.Bacc("TRN2", target_bir_lowering=False, num_devices=1, dynamic_dma_scratch_size=1024)
    arrays, io = {}, {}

    def give(name, a):
        arrays[f"in_{name}_dram"] = a
        io[name] = nc.dram_tensor(f"in_{name}_dram", a.shape, _mybir.dt.from_np(a.dtype), kind="ExternalInput").ap()

    for name in _INS:
        give(name, _np.ascontiguousarray(inputs[name]))
    const, mask, eye = shape_constants(_np)
    give("const", const)
    give("maskb", mask.astype(_ml.bfloat16))
    give("identb", eye.astype(_ml.bfloat16))
    out = nc.dram_tensor("out_0_dram", (1, S, DM), F32, kind="ExternalOutput").ap()
    build(nc, io, out)
    r = _run(nc, [arrays], core_ids=[0])
    return r.results[0]["out_0_dram"]
```

```python
from contextlib import ExitStack

import concourse.bass as bass
from concourse import mybir

F32 = mybir.dt.float32
F32R = mybir.dt.float32r
BF16 = mybir.dt.bfloat16
I32 = mybir.dt.int32
U32 = mybir.dt.uint32
ALU = mybir.AluOpType
ACT = mybir.ActivationFunctionType
AX = mybir.AxisListType

P = 128
DM = 1024
S = 256
NT = S // P
KT = DM // P
DEPTH = 2
EPS = 1e-6
NH = 4
HD = 128
ROT = HD // 4
NG = 3
CH = 64
NCH = S // CH
BW = 512
FD = 2816
NE = 8
FE = 3584
PLE = 256
SCALE = float(HD) ** -0.5
UC = 512
UN = 2048
RING = 6
NSPL = 2
LEAD = NSPL - 1
PARTS = 2
PC = UN // PARTS

CHUNKS = [("zf", 10, "feat"), ("zb", 11, "feat"), ("q", 9, "feat"), ("inp", 12, "feat"), ("gate", 13, "feat"),
          ("cu", 14, "feat"), ("cb", 15, "feat"), ("cc", 16, "feat")]
for _g in range(NG):
    CHUNKS += [(f"aq{_g}", 3 * _g, "feat"), (f"ak{_g}", 3 * _g + 1, "feat"), (f"av{_g}", 3 * _g + 2, "tok")]
NCHK = len(CHUNKS)
BRANCH_ORDER = [2, 1, 0]
U_GATE = 2 * NCHK
U_OUT = U_GATE + 3 * 6
U_MIX = U_OUT + 4
NFC = FD // UC
U_DENSE = 6 * NFC + 3
U_PLE = 5
NEC = FE // UC
U_EXP = 6 * NEC
TURNS_EXP = U_EXP // RING
U_L0 = U_MIX + U_DENSE + U_PLE
N_FILL = NCHK + 12
CIDX = {name: n for n, (name, _, _) in enumerate(CHUNKS)}
ROPED = [f"a{x}{g}" for g in range(NG) for x in "qk"]

C_ID, C_ONE, C_LT, C_IOTA, C_SCAN = 0, 128, 256, 384, 512
C_MASK, C_SIGN, C_INV, C_I8, C_END = 1024, 1280, 1281, 1282, 1290
R_MIX, R_FFN, R_PLE, R_CONV, R_LB, R_NG, R_END = 0, 16, 32, 48, 72, 88, 96


def build(nc, io, out):
    ctx = ExitStack()
    with ctx:
        def sb(name, shape, dt=F32):
            return ctx.enter_context(nc.sbuf_tensor(name, shape, dt))

        def sem(name):
            return ctx.enter_context(nc.semaphore(name))

        x = sb("x", [P, NT, DM])
        raw = sb("raw", [P, RING, UN])
        w_hi = sb("w_hi", [P, NSPL, UN], F32R)
        w_lo = sb("w_lo", [P, NSPL, UN], F32R)
        hT_hi = sb("hT_hi", [P, KT, S], F32R)
        hT_lo = sb("hT_lo", [P, KT, S], F32R)
        br_hi = sb("br_hi", [P, 3, 1024], F32R)
        br_lo = sb("br_lo", [P, 3, 1024], F32R)
        cst = sb("cst", [P, C_END])
        prm = sb("prm", [P, R_END])
        maskb = sb("maskb", [P, 2, 512], BF16)
        identb = sb("identb", [P, P], BF16)
        rc = sb("rc", [ROT, 2, S])
        lb = sb("lb", [P, 2, DEPTH, NH])
        omlb = sb("omlb", [P, 2, DEPTH, NH])
        small = sb("small", [P, 96])
        arena = sb("arena", [P, 20 * 1024])

        ident = cst[:, C_ID:C_ID + P]
        ones = cst[:, C_ONE:C_ONE + P]
        lower = cst[:, C_LT:C_LT + P]
        iota = cst[:, C_IOTA:C_IOTA + P]
        scan_keep = cst[:, C_SCAN:C_SCAN + 512]
        causal = [cst[:, C_MASK + P * d:C_MASK + P * d + P].bitcast(U32) for d in range(2)]
        rot_sign = cst[0:ROT, C_SIGN:C_SIGN + 1]
        inv_freq = cst[0:ROT, C_INV:C_INV + 1]
        iota8 = cst[:, C_I8:C_I8 + NE]

        def area(k, n=1024):
            return arena[:, 1024 * k:1024 * k + n]

        A = {f"a{x}{g}": area(3 * g + j) for g in range(NG) for j, x in enumerate("qkv")}
        B = {"zf": area(9), "zb": area(10), "q": area(11), "inp": area(12), "gate": area(13)}
        hL, hC, h1, h2 = area(14), area(15), area(16), area(17)
        kdT = area(18)
        attT = area(19)
        hS = sb("hS", [P, NH * HD])[:, :]
        conv = {"cu": A["aq2"], "cb": A["ak2"], "cc": A["av2"]}
        DEST = {**A, **B, **conv, "inp": h1}
        IN_TIME = (*B, *conv)
        merged = arena[:, 1024 * 9:1024 * 11]
        swapped = arena[0:ROT, 1024 * 9:1024 * 10]
        gtile = area(11)
        aP, aPT = area(12), area(13)
        adiag = area(14, 256)
        utmp = area(15)
        xn = arena[:, 0:2048]
        gained = arena[:, 1024 * 14:1024 * 16]
        junk = area(17)
        gb = area(18)
        dsg = area(4)
        yacc = arena[:, 1024 * 2:1024 * 4]
        gfull = area(4)
        hid = area(6, 512)
        msg = arena[:, 1024 * 6 + 512:1024 * 7]
        sel = area(7, 256)
        cslot = arena[:, 1024 * 7 + 256:1024 * 7 + 257]
        rout = arena[:, 1024 * 7 + 768:1024 * 7 + 832]
        rt = arena[:, 1024 * 7 + 832:1024 * 8]
        ye_hi = hT_hi[:, 0:4, :].rearrange("p k t -> p (k t)")
        ye_lo = hT_lo[:, 0:4, :].rearrange("p k t -> p (k t)")
        selct = hT_hi[:, 4, :]
        rk = sb("rk", [P, 4])
        minus_half = sb("minus_half", [P, 8])
        nsw_i = sb("nsw_i", [P, 1], I32)
        r_hi = sb("r_hi", [P, KT * NE], F32R)
        r_lo = sb("r_lo", [P, KT * NE], F32R)
        ptok = area(8, 512)
        sig = arena[:, 1024 * 10:1024 * 12]
        eprod = arena[:, 1024 * 12:1024 * 14]

        ps = ctx.enter_context(nc.psum_tensor("ps", [P, 8 * 512], F32))

        def bank(b, n=512):
            return ps[:, 512 * b:512 * b + n]

        raw_loaded = [sem(f"raw_loaded{n}") for n in range(RING)]
        hi_ready, lo_ready, part_used = sem("hi_ready"), sem("lo_ready"), sem("part_used")
        x_loaded, const_loaded, pos_loaded = sem("x_loaded"), sem("const_loaded"), sem("pos_loaded")
        gb_loaded, p_loaded, rout_loaded = sem("gb_loaded"), sem("p_loaded"), sem("rout_loaded")
        prm_turned, prm_ready, pre = sem("prm_turned"), sem("prm_ready"), sem("pre")
        pre_act = sem("pre_act")
        ssq, var_ready, rstd_ready, xn_ready = sem("ssq"), sem("var_ready"), sem("rstd_ready"), sem("xn_ready")
        turned, hT_hi_ready, hT_lo_ready = sem("turned"), sem("hT_hi_ready"), sem("hT_lo_ready")
        post_ssq, post_var, post_rstd, post_gain, x_ready = (
            sem("post_ssq"), sem("post_var"), sem("post_rstd"), sem("post_gain"), sem("x_ready"))
        evac_act, evac_dve = sem("evac_act"), sem("evac_dve")
        half_ready, z_att = sem("half_ready"), sem("z_att")
        inp_turned, inp_ready = sem("inp_turned"), sem("inp_ready")
        half_swapped, rope_step, rope_done = sem("half_swapped"), sem("rope_step"), sem("rope_done")
        h_pe, h_act, h_dve, h_pow = sem("h_pe"), sem("h_act"), sem("h_dve"), sem("h_pow")
        conv_step, conv_hi = sem("conv_step"), sem("conv_hi")
        at_s, at_t, at_v = sem("at_s"), sem("at_t"), sem("at_v")
        at_max, at_nm, at_exp, at_dve, at_pt_act, at_pt_dve = (
            sem("at_max"), sem("at_nm"), sem("at_exp"), sem("at_dve"), sem("at_pt_act"), sem("at_pt_dve"))
        at_hi, at_lo = sem("at_hi"), sem("at_lo")
        mg, m_hi, m_lo = sem("mg"), sem("m_hi"), sem("m_lo")
        d_sg, d_hid, d_hi, d_lo = sem("d_sg"), sem("d_hid"), sem("d_hi"), sem("d_lo")
        p_turned, p_hi, p_lo = sem("p_turned"), sem("p_hi"), sem("p_lo")
        pl_sig, pl_prod = sem("pl_sig"), sem("pl_prod")
        r_split, r_log, r_step, r_exp, r_rank = (
            sem("r_split"), sem("r_log"), sem("r_step"), sem("r_exp"), sem("r_rank"))
        sweeps_ready = sem("sweeps_ready")
        gfull_loaded, xn_scaled = sem("gfull_loaded"), sem("xn_scaled")
        e_rank, e_sel, e_gath, e_slots, e_xhi, e_xlo = (
            sem("e_rank"), sem("e_sel"), sem("e_gath"), sem("e_slots"), sem("e_xhi"), sem("e_xlo"))
        e_sg, e_hid, e_turn, e_thi, e_tlo = sem("e_sg"), sem("e_hid"), sem("e_turn"), sem("e_thi"), sem("e_tlo")
        e_yhi, e_ylo, e_scat, e_acc = sem("e_yhi"), sem("e_ylo"), sem("e_scat"), sem("e_acc")
        stored = sem("stored")

        HD_D, HD_L = 29, 73
        HA_D, HA_L = 8, 19
        HP_D, HP_L = 6, 14

        def hdve(i, d, k):
            return HD_L * i + HD_D * d + k

        def hact(i, d, k):
            return HA_L * i + HA_D * d + k

        def hpe(i, d, k):
            return HP_L * i + HP_D * d + k

        def time_order(ap):
            return ap.rearrange("p (f i r) -> p f r i", f=4, r=4)

        def token_order(ap):
            return ap.rearrange("p (f r i) -> p f r i", f=4, r=4)

        def chunked(ap, n=16):
            return ap.rearrange("p (c t) -> p c t", c=n)

        def h_turned(m, k):
            b = 2048 if m == 0 else 0
            return ps[:, b + S * k:b + S * k + S]

        def y_mixer(t):
            return ps[:, 2048 + DM * t:2048 + DM * t + DM]

        def y_dense(t):
            return ps[:, DM * t:DM * t + DM]

        def y_experts(t):
            return yacc[:, DM * t:DM * t + DM]

        def y_ple(t):
            return eprod[:, DM * t:DM * t + DM]

        def unit_w(w, k):
            return w[:, k % NSPL, :].rearrange("p (k n) -> p k n", k=4)

        def unit_done(eng, turns, k):
            eng.wait_ge(part_used, turns * (RING * PARTS) + PARTS * (k + 1))

        def fill_unit(f):
            return 2 * f + 1 if f < NCHK else U_GATE + 3 * ((f - NCHK) // 2) + 1 + (f - NCHK) % 2

        block = ctx.enter_context(nc.Block())

        @block.sync
        def _(sp):
            def load(turns, k, src, first=False):
                if not (isinstance(turns, int) and turns * RING + k < RING):
                    sp.wait_ge(lo_ready, turns * (RING * PARTS) + PARTS * (k - RING + 1))
                sp.dma_start(raw[:, k % RING, :].rearrange("p (k n) -> p k n", n=src.shape[-1]), src)\
                  .then_inc(raw_loaded[k % RING], 16)

            def tile4(w, r0, c0):
                return w[r0:r0 + 512, c0:c0 + UC].rearrange("(k p) n -> p k n", p=P)

            def mixer(i, k):
                for _, blk, _ in CHUNKS:
                    for kh in range(2):
                        load(0, k, tile4(io["w_in"][i], 512 * kh, UC * blk))
                        k += 1
                for n in BRANCH_ORDER:
                    for j in range(2):
                        for kh in range(2):
                            load(0, k, tile4(io["w_in"][i], 512 * kh, UC * (17 + 2 * n + j)))
                            k += 1
                        load(0, k, tile4(io["w_branch"][i, n], 0, UC * j))
                        k += 1
                for kh in range(2):
                    for j in range(2):
                        load(0, k, tile4(io["w_out"][i], 512 * kh, UC * j))
                        k += 1
                return k

            def dense(k):
                wg, wu, wd = io["dense_w_gate"][0], io["dense_w_up"][0], io["dense_w_down"][0]
                for w in (wg, wu):
                    for kh in range(2):
                        load(0, k, tile4(w, 512 * kh, 0))
                        k += 1
                turn0, k0 = k // RING, k % RING
                with sp.Fori(1, NFC) as c:
                    turns = c + (turn0 - 1)
                    kk = k0
                    for kh in range(2):
                        load(turns, kk, wg[512 * kh:512 * kh + 512, bass.ds(c * UC, UC)]
                             .rearrange("(k p) n -> p k n", p=P))
                        kk += 1
                    for j in range(2):
                        load(turns, kk, wd[bass.ds((c - 1) * UC, 512), UC * j:UC * j + UC]
                             .rearrange("(k p) n -> p k n", p=P))
                        kk += 1
                    for kh in range(2):
                        load(turns, kk, wu[512 * kh:512 * kh + 512, bass.ds(c * UC, UC)]
                             .rearrange("(k p) n -> p k n", p=P))
                        kk += 1
                k += 6 * (NFC - 1)
                f0 = NFC * UC
                load(0, k, wg[:, f0:FD].rearrange("(k p) n -> p k n", p=P))
                load(0, k + 1, tile4(wd, f0 - UC, 0))
                load(0, k + 2, tile4(wd, f0 - UC, UC))
                load(0, k + 3, wu[:, f0:FD].rearrange("(k p) n -> p k n", p=P))
                load(0, k + 4, wd[f0:FD, :].rearrange("(k p) n -> p k n", p=P))
                return k + 5

            def ple(i, turns, k):
                load(turns, k, io["ple_w_proj"][i].rearrange("(k p) n -> p k n", p=P))
                for j in range(2):
                    for kh in range(2):
                        k += 1
                        load(turns, k, tile4(io["ple_w_gate"][i], 512 * kh, UC * j))
                return k + 1

            for r in range(4):
                sp.dma_start(x[64 * (r % 2):64 * (r % 2) + 64, r // 2, :],
                             io["x"][0].rearrange("(i r) d -> r i d", r=4)[r]).then_inc(x_loaded, 16)
            sp.wait_ge(x_loaded, 64)
            k = mixer(0, 0)
            k = dense(k)
            k = ple(0, 0, k)
            k = mixer(1, k)
            turn0, k0 = k // RING, k % RING

            def sweep(s):
                with sp.Fori(0, NE) as e:
                    turns = e * TURNS_EXP + (s * (NE * TURNS_EXP) + turn0)
                    wg, wu, wd = (io[w][0, bass.ds(e, 1)] for w in ("moe_w_gate", "moe_w_up", "moe_w_down"))

                    def up(w, kk, c, kh):
                        load(turns, kk, w[:, 512 * kh:512 * kh + 512, UC * c:UC * c + UC]
                             .rearrange("a (k p) n -> p (a k) n", p=P))

                    def down(kk, c):
                        for j in range(2):
                            load(turns, kk + j, wd[:, UC * c:UC * c + 512, UC * j:UC * j + UC]
                                 .rearrange("a (k p) n -> p (a k) n", p=P))

                    kk = k0
                    for c in range(NEC):
                        for w in (wg, wu):
                            for kh in range(2):
                                up(w, kk, c, kh)
                                kk += 1
                        if c:
                            down(kk, c - 1)
                            kk += 2
                    down(kk, NEC - 1)

            sweep(0)
            sp.wait_ge(sweeps_ready, 1)
            sweeps = sp.value_load(nsw_i[0:1, 0:1], min_val=1, max_val=2)
            with sp.If(sweeps > 1):
                sweep(1)
            ple(1, sweeps * (NE * TURNS_EXP) + turn0, k0)
            for r in range(4):
                sp.wait_ge(x_ready, 2 * 5 + r // 2 + 1)
                sp.dma_start(out[0].rearrange("(i r) d -> r i d", r=4)[r],
                             x[64 * (r % 2):64 * (r % 2) + 64, r // 2, :]).then_inc(stored, 16)
            sp.wait_ge(stored, 64)

        @block.scalar
        def _(act):
            def split(turns, k):
                act.wait_ge(raw_loaded[k % RING], (turns + (k // RING + 1)) * 16)
                for h in range(PARTS):
                    if not (isinstance(turns, int) and turns * RING + k < NSPL):
                        act.wait_ge(part_used, turns * (RING * PARTS) + PARTS * (k - NSPL) + h + 1)
                    cols = slice(PC * h, PC * h + PC)
                    act.activation(w_hi[:, k % NSPL, cols], raw[:, k % RING, cols], ACT.Copy).then_inc(hi_ready, 1)

            def pre_norm(i, m):
                n = 3 * i + m
                for t in range(NT):
                    if n:
                        act.wait_ge(x_ready, 2 * (n - 1) + t + 1)
                    else:
                        act.wait_ge(x_loaded, 64)
                    if n or t:
                        act.wait_ge(ssq, NT * n + t)
                    act.activation(junk, x[:, t, :], ACT.Square,
                                   accum_out=small[:, t:t + 1]).then_inc(ssq, 1)
                if m:
                    gain_load(i, m)

            def gain_load(i, m):
                src = io[("g_mix_post", "g_ffn_post", "ple_g_post")[m]][i:i + 1, :]
                act.dma_start(gb, src.to_broadcast([P, DM]))\
                   .then_inc(gb_loaded, 16)

            def pre_norm_hi(i, m):
                n = 3 * i + m
                act.wait_ge(prm_ready, 1)
                for k in range(KT):
                    g = prm[:, (R_MIX, R_FFN, R_PLE)[m] + KT * i + k:][:, 0:1]
                    act.wait_ge(turned, 4 * n + k // 2 + 1)
                    act.activation(hT_hi[:, k, :], h_turned(m, k), ACT.Identity, scale=g)\
                       .then_inc(hT_hi_ready, 1)

            def post_norm(n, ys, ready=None):
                for t in range(NT):
                    if ready:
                        ready(t)
                    if n or t:
                        act.wait_ge(post_ssq, NT * n + t)
                    if t:
                        act.wait_ge(post_gain, NT * n + 1)
                    act.activation(junk, ys(t), ACT.Square, accum_out=small[:, 4 + t:5 + t])\
                       .then_inc(post_ssq, 1)

            def h_vec(i, d, step):
                z = B["zf" if d == 0 else "zb"]
                if step == 0:
                    act.wait_ge(evac_act, 23 * i + 2 + 1)
                    if d:
                        act.wait_ge(h_pe, hpe(i, 0, 6))
                        act.wait_ge(h_dve, hdve(i, 0, 29))
                    act.activation(hL, z, ACT.Sigmoid).then_inc(h_act, 1)
                    act.wait_ge(h_act, hact(i, d, 1))
                    act.activation(z, z, ACT.Sigmoid, scale=-1.0).then_inc(h_act, 1)
                if step == 1:
                    act.wait_ge(h_dve, hdve(i, d, 4))
                    act.activation(hL, hL, ACT.Ln).then_inc(h_act, 1)
                if step == 2:
                    act.wait_ge(h_dve, hdve(i, d, 8))
                    act.activation(h1, hL, ACT.Exp).then_inc(h_act, 1)
                    act.wait_ge(h_act, hact(i, d, 4))
                    act.activation(hL, hL, ACT.Exp, scale=-1.0).then_inc(h_act, 1)
                    act.activation(h2, h2, ACT.Exp).then_inc(h_act, 1)
                    act.activation(hC, hC, ACT.Exp).then_inc(h_act, 1)
                if step == 3:
                    act.wait_ge(h_pe, hpe(i, d, 2))
                    act.activation(kdT, ps[:, 2048:3072], ACT.Copy).then_inc(h_act, 1)

            def h_post(i, step):
                if step == 0:
                    act.wait_ge(h_pe, hpe(i, 2, 0))
                    act.wait_ge(h_dve, hdve(i, 2, 0))
                    act.activation(h1, ps[:, 512 * 6:512 * 8], ACT.Copy).then_inc(h_act, 1)
                    act.activation(hL, ps[:, 512 * 6:512 * 8], ACT.Square).then_inc(h_act, 1)
                else:
                    act.wait_ge(h_dve, hdve(i, 2, 14))
                    act.activation(token_order(br_hi[:, 1, :]), time_order(h2), ACT.Copy).then_inc(h_act, 1)

            def mixer(i):
                base = U_L0 * i
                pre_norm(i, 0)
                for k in range(LEAD):
                    if i == 0:
                        split(0, base + k)
                pre_norm_hi(i, 0)
                for u in range(U_MIX):
                    split(0, base + u + LEAD)
                    if i == 0 and u == 2:
                        preamble_tables()
                    if u < U_GATE and u % 2 == 1:
                        c = u // 2
                        name = CHUNKS[c][0]
                        unit_done(act, 0, base + u)
                        if name in ("aq2", "ak2", "av2"):
                            act.wait_ge(conv_hi, i + 1)
                            act.wait_ge(conv_step, 15 * (i + 1))
                        if name == "inp" and i:
                            act.wait_ge(h_dve, hdve(i - 1, 2, 13))
                        dst, src = DEST[name], ps[:, 1024 * (c % 2):1024 * (c % 2) + 1024]
                        if name in IN_TIME:
                            dst, src = time_order(dst), token_order(src)
                        act.activation(dst, src, ACT.Silu if name == "gate" else ACT.Copy).then_inc(evac_act, 1)
                        if name in ROPED:
                            swap_halves(i, ROPED.index(name))
                    if U_GATE <= u < U_OUT and (u - U_GATE) % 3 == 1:
                        m = (u - U_GATE) // 3
                        f = NCHK + 2 * m
                        unit_done(act, 0, base + u)
                        if m:
                            act.wait_ge(evac_dve, 6 * i + m)
                        else:
                            act.wait_ge(h_dve, hdve(i, 2, 15))
                            act.wait_ge(h_act, hact(i, 2, 3))
                        act.activation(gtile, ps[:, 1024 * (f % 2):1024 * (f % 2) + 1024], ACT.Sigmoid)\
                           .then_inc(evac_act, 1)
                    if u == 6:
                        h_vec(i, 0, 0)
                    if u == 8:
                        h_vec(i, 0, 1)
                        act.wait_ge(inp_turned, i + 1)
                        act.activation(B["inp"], ps[:, 2048:3072], ACT.Copy).then_inc(inp_ready, 1)
                    if u == 11:
                        h_vec(i, 0, 2)
                    if u == 17:
                        act.wait_ge(conv_step, 15 * i + 14)
                        act.activation(token_order(br_hi[:, 2, :]), time_order(conv["cc"]), ACT.Copy).then_inc(conv_hi, 1)
                    if u == 16:
                        h_vec(i, 0, 3)
                    if u == 21:
                        h_vec(i, 1, 0)
                    if u == 22:
                        h_vec(i, 1, 1)
                    if u == 23:
                        h_vec(i, 1, 2)
                    if u == 27:
                        h_vec(i, 1, 3)
                    if u == 32:
                        h_post(i, 0)
                    if u == 34:
                        h_post(i, 1)
                    if 35 <= u < 44:
                        attend(i, u - 35)
                    if u == 44:
                        act.wait_ge(h_pe, hpe(i, 2, 0))
                        gain_load(i, 0)
                    if u in (U_OUT - 2, U_OUT):
                        j = int(u == U_OUT)
                        act.wait_ge(mg, 4 * i + 3 + j)
                        act.activation(br_hi[:, 1 + j, :], merged[:, 1024 * j:1024 * j + 1024], ACT.Copy)\
                           .then_inc(m_hi, 1)

            def swap_halves(i, r):
                n, a = 6 * i + r, A[ROPED[r]]
                act.wait_ge(evac_act, 23 * i + CIDX[ROPED[r]] + 1)
                if r:
                    act.wait_ge(rope_done, n)
                else:
                    act.wait_ge(h_dve, hdve(i, 0, 18))
                half = ROT // 2
                for p in range(2):
                    act.dma_start(swapped[half * p:half * p + half, :], a[half * (1 - p):half * (2 - p), :])\
                       .then_inc(half_swapped, 16)

            def attend(i, g):
                h, odd = g // 2, g % 2
                if not odd and h >= 1:
                    hh = h - 1
                    act.wait_ge(at_v, NH * i + hh + 1)
                    act.activation(br_hi[:, 0, S * hh:S * hh + S], ps[:, 3072:3072 + S], ACT.Copy)\
                       .then_inc(at_hi, 1)
                if not odd and h < NH:
                    for q in range(2):
                        act.wait_ge(at_nm, NH * i + h + 1)
                        act.activation(aP[:, 512 * q:512 * q + 512], bank(4 + q), ACT.Exp, scale=SCALE,
                                       bias=small[:, 16 + q:17 + q], accum_out=small[:, 18 + q:19 + q])\
                           .then_inc(at_exp, 1)
                if odd:
                    act.wait_ge(at_t, 2 * (NH * i + h) + 1)
                    act.activation(aPT[:, 0:512], bank(6), ACT.Copy).then_inc(at_pt_act, 1)

            def preamble_tables():
                act.wait_ge(pre, PRE_ANGLES)
                act.activation(small[:, 64:80], small[:, 48:64], ACT.Exp).then_inc(pre_act, 1)
                act.activation(rc[:, 0, :], rc[:, 0, :], ACT.Sin).then_inc(pre_act, 1)
                act.activation(rc[:, 1, :], rc[:, 1, :], ACT.Sin).then_inc(pre_act, 1)

            def p_load(i):
                for r in range(4):
                    act.dma_start(ptok[64 * (r % 2):64 * (r % 2) + 64, PLE * (r // 2):PLE * (r // 2) + PLE],
                                  io["p"][i, 0].rearrange("(i r) c -> r i c", r=4)[r]).then_inc(p_loaded, 16)

            def p_split(i):
                act.wait_ge(p_turned, i + 1)
                act.activation(br_hi[:, 2, 0:512], bank(7), ACT.Copy).then_inc(p_hi, 1)

            def dense(base):
                k = base + LEAD

                def gate(turns, kk, c, n=1024):
                    unit_done(act, turns, kk)
                    act.wait_ge(d_lo, c)
                    act.activation(dsg[:, 0:n], ps[:, 512 * 4:512 * 4 + n], ACT.Silu).then_inc(d_sg, 1)

                def hidden(c, n=1024):
                    act.wait_ge(d_hid, c + 1)
                    act.activation(br_hi[:, 0, 0:n], dsg[:, 0:n], ACT.Copy).then_inc(d_hi, 1)

                for u in range(4):
                    split(0, k)
                    if u == 1:
                        gate(0, base + 1, 0)
                    if u == 3:
                        hidden(0)
                    k += 1
                turn0, k0 = k // RING, k % RING
                with act.Fori(1, NFC) as c:
                    turns = c + (turn0 - 1)
                    for u in range(6):
                        split(turns, k0 + u)
                        if u == 1:
                            gate(turns, k0 - LEAD + 1, c)
                        if u == 5:
                            hidden(c)
                k += 6 * (NFC - 1)
                for u in range(5):
                    split(0, k + u)
                    if u == 0:
                        gate(0, k - LEAD, NFC, 512)
                    if u == 3:
                        hidden(NFC, 512)

            def gathered(it):
                act.wait_ge(e_gath, it + 1)
                act.activation(br_hi[:, 1, :], ps[:, 1024:2048], ACT.Copy).then_inc(e_xhi, 1)

            def experts(base):
                turn0, k0 = base // RING, base % RING
                split(0, base + 1)
                gathered(0)
                act.wait_ge(sweeps_ready, 1)
                sweeps = act.value_load(nsw_i[0:1, 0:1], min_val=1, max_val=2)
                with act.Fori(0, sweeps) as s:
                    with act.Fori(0, NE) as e:
                        it = s * NE + e
                        turns = it * TURNS_EXP + turn0

                        def turn(c):
                            act.wait_ge(e_turn, it * NEC + (c + 1 + ONE))
                            act.activation(br_hi[:, 0, 0:512], bank(6), ACT.Copy).then_inc(e_thi, 1)

                        for u in range(2, U_EXP):
                            split(turns, k0 + u)
                            c, step = divmod(u + 2, 6)
                            if step == 3 and c < NEC or u == 3:
                                c = 0 if u == 3 else c
                                unit_done(act, turns, k0 + (1 if u == 3 else u - 2))
                                if c:
                                    act.wait_ge(e_hid, it * NEC + c)
                                act.activation(msg, bank(4), ACT.Silu).then_inc(e_sg, 1)
                                if c:
                                    turn(c - 1)
                        turn(NEC - 1)
                        gathered(it + 1)
                        split(turns, k0 + U_EXP)
                        split(turns, k0 + U_EXP + 1)
                        unit_done(act, turns, k0 + U_EXP - 1)
                        act.wait_ge(e_slots, it + 1)
                        act.activation(ye_hi, ps[:, 0:1024], ACT.Identity, scale=cslot).then_inc(e_yhi, 1)
                return sweeps

            def ple(i, turns, k):
                for u in range(2, U_PLE) if i == DEPTH - 1 else range(LEAD, U_PLE + LEAD):
                    split(turns, k + u)
                unit_done(act, turns, k + U_PLE - 1)
                for t in range(NT):
                    act.activation(sig[:, DM * t:DM * t + DM], y_dense(t), ACT.Sigmoid).then_inc(pl_sig, 1)
                post_norm(3 * i + 2, y_ple, lambda t: act.wait_ge(pl_prod, 2 * i + t + 1))

            act.dma_start(cst[:, :], io["const"]).then_inc(const_loaded, 16)
            act.dma_start(maskb[:, :, :], io["maskb"]).then_inc(const_loaded, 16)
            act.dma_start(identb[:, :], io["identb"]).then_inc(const_loaded, 16)
            rows = arena[0:R_END, 2048:2048 + P]
            for r0, name, pat in ((R_MIX, "g_mix_pre", "i (k p) -> (i k) p"), (R_FFN, "g_ffn_pre", "i (k p) -> (i k) p"),
                                  (R_PLE, "ple_g_in", "i (k p) -> (i k) p"),
                                  (R_CONV, "conv_w", "i w (k p) -> (i w k) p"),
                                  (R_LB, "hgrn_lb_logits", "s i (k p) -> (s i k) p"),
                                  (R_NG, "hgrn_norm_g", "i (k p) -> (i k) p")):
                src = io[name].rearrange(pat, p=P)
                act.dma_start(rows[r0:r0 + src.shape[0], :], src).then_inc(const_loaded, 16)
            act.dma_start(arena[0:ROT, 3072:3072 + S].bitcast(I32),
                          io["positions"].partition_broadcast(ROT).rearrange("p a s -> p (a s)"))\
               .then_inc(pos_loaded, 16)

            mixer(0)
            unit_done(act, 0, U_MIX - 1)
            post_norm(0, y_mixer)
            p_load(0)
            pre_norm(0, 1)
            pre_norm_hi(0, 1)
            p_split(0)
            dense(U_MIX)
            unit_done(act, 0, U_MIX + U_DENSE - 1)
            post_norm(1, y_dense)
            pre_norm(0, 2)
            pre_norm_hi(0, 2)
            ple(0, 0, U_MIX + U_DENSE)
            mixer(1)
            unit_done(act, 0, U_L0 + U_MIX - 1)
            post_norm(3, y_mixer)
            p_load(1)
            act.dma_start(rout.rearrange("p (k e) -> p k e", k=KT),
                          io["moe_router"][0].rearrange("(k p) e -> p k e", p=P)).then_inc(rout_loaded, 16)
            act.dma_start(gfull, io["g_ffn_pre"][1:2, :].to_broadcast([P, DM])).then_inc(gfull_loaded, 16)
            pre_norm(1, 1)
            pre_norm_hi(1, 1)
            p_split(1)
            act.wait_ge(rout_loaded, 16)
            act.activation(r_hi[:, :], rout, ACT.Copy).then_inc(r_split, 1)
            act.wait_ge(r_step, R_DIFF)
            act.activation(rt[:, RT_EX:RT_EX + 16], rt[:, RT_DF:RT_DF + 16], ACT.Exp).then_inc(r_exp, 1)
            sweeps = experts(U_L0 + U_MIX)
            act.wait_ge(e_acc, sweeps * (NE * 2) + 3)
            post_norm(4, y_experts)
            pre_norm(1, 2)
            pre_norm_hi(1, 2)
            k = U_L0 + U_MIX
            ple(1, sweeps * (NE * TURNS_EXP) + k // RING, k % RING)

        @block.vector
        def _(dve):
            def split(turns, k):
                for h in range(PARTS):
                    dve.wait_ge(hi_ready, turns * (RING * PARTS) + PARTS * k + h + 1)
                    cols = slice(PC * h, PC * h + PC)
                    dve.tensor_tensor(w_lo[:, k % NSPL, cols], raw[:, k % RING, cols],
                                      w_hi[:, k % NSPL, cols].bitcast(F32), ALU.subtract).then_inc(lo_ready, 1)

            def pre_norm(i, m):
                n = 3 * i + m
                for t in range(NT):
                    dve.wait_ge(ssq, NT * n + t + 1)
                    dve.tensor_scalar(small[:, 2 + t:3 + t], small[:, t:t + 1], 1.0 / DM, EPS, ALU.mult, ALU.add)\
                       .then_inc(var_ready, 1)
                    dve.wait_ge(rstd_ready, NT * n + t + 1)
                    dve.tensor_scalar(xn[:, DM * t:DM * t + DM], x[:, t, :], small[:, 8 + t:9 + t], None, ALU.mult)\
                       .then_inc(xn_ready, 1)
                for k in range(KT):
                    g = prm[:, (R_MIX, R_FFN, R_PLE)[m] + KT * i + k:][:, 0:1]
                    dve.wait_ge(hT_hi_ready, KT * n + 2 * (k // 2) + 2)
                    dve.scalar_tensor_tensor(out=hT_lo[:, k, :], in0=h_turned(m, k), scalar=g,
                                             in1=hT_hi[:, k, :].bitcast(F32), op0=ALU.mult, op1=ALU.subtract)\
                       .then_inc(hT_lo_ready, 1)

            def post_norm(n, ys):
                dve.wait_ge(gb_loaded, 16 * (n + 1))
                if n:
                    dve.wait_ge(x_ready, 2 * n)
                for t in (1, 0):
                    if t == 0:
                        dve.wait_ge(post_ssq, NT * n + 1)
                        dve.tensor_scalar(small[:, 6:7], small[:, 4:5], 1.0 / DM, EPS, ALU.mult, ALU.add)\
                           .then_inc(post_var, 1)
                    dve.tensor_tensor(gained[:, DM * t:DM * t + DM], ys(t), gb, ALU.mult).then_inc(post_gain, 1)
                dve.wait_ge(post_ssq, NT * n + 2)
                dve.tensor_scalar(small[:, 7:8], small[:, 5:6], 1.0 / DM, EPS, ALU.mult, ALU.add)\
                   .then_inc(post_var, 1)
                dve.wait_ge(post_gain, NT * (n + 1))
                for t in range(NT):
                    dve.wait_ge(post_rstd, NT * n + t + 1)
                    dve.scalar_tensor_tensor(out=x[:, t, :], in0=gained[:, DM * t:DM * t + DM],
                                             scalar=small[:, 10 + t:11 + t], in1=x[:, t, :],
                                             op0=ALU.mult, op1=ALU.add).then_inc(x_ready, 1)

            def h_vec(i, d, step):
                z = B["zf" if d == 0 else "zb"]
                lbs = [lb[:, d, i, h:h + 1] for h in range(NH)]
                oms = [omlb[:, d, i, h:h + 1] for h in range(NH)]
                end, mid = (CH - 1, CH // 2 - 1) if d == 0 else (0, CH // 2)
                if step == 0:
                    dve.wait_ge(h_act, hact(i, d, 1))
                    for h in range(NH):
                        a = hL[:, S * h:S * h + S]
                        dve.tensor_scalar(a, a, oms[h], lbs[h], ALU.mult, ALU.add).then_inc(h_dve, 1)
                if step == 1:
                    dve.wait_ge(h_act, hact(i, d, 3))
                    for r in range(2):
                        a, c = hL[:, 512 * r:512 * r + 512], hC[:, 512 * r:512 * r + 512]
                        if d:
                            a, c = a[:, ::-1], c[:, ::-1]
                        dve.tensor_tensor_scan(out=c, data0=scan_keep, data1=a, initial=0.0,
                                               op0=ALU.mult, op1=ALU.add).then_inc(h_dve, 1)
                    dve.wait_ge(h_dve, hdve(i, d, 6))
                    cv = chunked(hC)
                    dve.tensor_tensor(chunked(hL), cv, cv[:, :, mid:mid + 1].to_broadcast([P, 16, CH]),
                                      ALU.subtract).then_inc(h_dve, 1)
                    dve.tensor_tensor(chunked(h2), cv[:, :, end:end + 1].to_broadcast([P, 16, CH]), cv,
                                      ALU.subtract).then_inc(h_dve, 1)
                if step == 2:
                    dve.wait_ge(evac_act, 23 * i + CIDX["q"] + 1)
                    dve.wait_ge(h_act, hact(i, d, 4))
                    dve.tensor_tensor(h1, h1, B["q"], ALU.mult).then_inc(h_dve, 1)
                    dve.wait_ge(h_act, hact(i, d, 5))
                    for h in range(NH):
                        a = hL[:, S * h:S * h + S]
                        dve.scalar_tensor_tensor(out=a, in0=z[:, S * h:S * h + S], scalar=oms[h], in1=a,
                                                 op0=ALU.mult, op1=ALU.mult).then_inc(h_dve, 1)
                    dve.wait_ge(h_act, hact(i, d, 7))
                    dve.tensor_copy(small[:, 32:48].rearrange("p (c a) -> p c a", a=1),
                                    chunked(hC)[:, :, end:end + 1]).then_inc(h_dve, 1)
                    for h in range(NH):
                        a = h2[:, S * h:S * h + S]
                        dve.scalar_tensor_tensor(out=a, in0=z[:, S * h:S * h + S], scalar=oms[h], in1=a,
                                                 op0=ALU.mult, op1=ALU.mult).then_inc(h_dve, 1)
                    dve.wait_ge(h_dve, hdve(i, d, 14))
                    dve.tensor_tensor(hC, hC, B["q"], ALU.mult).then_inc(h_dve, 1)
                if step == 3:
                    dve.wait_ge(h_pe, hpe(i, d, 1))
                    if d:
                        dve.wait_ge(h_dve, hdve(i, 1, 19))
                    dve.copy_predicated(attT.rearrange("p (c t) -> p c t", t=P),
                                        causal[d].rearrange("p (a t) -> p a t", a=1).to_broadcast([P, 8, P]),
                                        ps[:, 2048:3072].rearrange("p (c t) -> p c t", t=P)).then_inc(h_dve, 1)
                if step == 4:
                    dve.wait_ge(h_pe, hpe(i, d, 3))
                    dve.tensor_copy(hS, bank(4)).then_inc(h_dve, 1)
                if step in (5, 6):
                    c = step - 4
                    if d:
                        c = NCH - 1 - c
                    dve.wait_ge(h_pe, hpe(i, d, step - 1))
                    dve.wait_ge(h_dve, hdve(i, d, 21 + 4 * (step - 5)))
                    for h in range(NH):
                        a = hS[:, HD * h:HD * h + HD]
                        dve.scalar_tensor_tensor(out=a, in0=a, scalar=small[:, 32 + NCH * h + c:33 + NCH * h + c],
                                                 in1=ps[:, 2048 + HD * h:2048 + HD * h + HD],
                                                 op0=ALU.mult, op1=ALU.add).then_inc(h_dve, 1)

            def h_post(i, step):
                if step == 0:
                    dve.wait_ge(h_pe, hpe(i, 2, 1))
                    dve.tensor_scalar(small[:, 80:88], bank(4)[:, 0:8], 1.0 / HD, EPS, ALU.mult, ALU.add)\
                       .then_inc(h_dve, 1)
                    dve.wait_ge(h_pow, i + 1)
                    for j in range(8):
                        dve.tensor_scalar(hC[:, P * j:P * j + P], ident, small[:, 88 + j:89 + j], None, ALU.mult)\
                           .then_inc(h_dve, 1)
                if step == 1:
                    dve.wait_ge(h_pe, hpe(i, 2, 2))
                    dve.wait_ge(h_act, hact(i, 2, 1))
                    for h in range(NH):
                        dve.scalar_tensor_tensor(out=h2[:, S * h:S * h + S], in0=h1[:, S * h:S * h + S],
                                                 scalar=prm[:, R_NG + NH * i + h:R_NG + NH * i + h + 1],
                                                 in1=ps[:, 2048 + S * h:2048 + S * h + S],
                                                 op0=ALU.mult, op1=ALU.mult).then_inc(h_dve, 1)
                    dve.wait_ge(h_dve, hdve(i, 2, 13))
                    dve.wait_ge(evac_act, 23 * i + CIDX["gate"] + 1)
                    dve.tensor_tensor(h2, h2, B["gate"], ALU.mult).then_inc(h_dve, 1)
                    dve.wait_ge(h_act, hact(i, 2, 3))
                    dve.wait_ge(h_dve, hdve(i, 2, 14))
                    dve.tensor_tensor(token_order(br_lo[:, 1, :]), time_order(h2),
                                      token_order(br_hi[:, 1, :].bitcast(F32)), ALU.subtract)\
                       .then_inc(h_dve, 1)

            def convolve(i):
                cu, cb, cc = conv["cu"], conv["cb"], conv["cc"]
                n0 = 15 * i
                dve.wait_ge(evac_act, 23 * i + CIDX["cc"] + 1)
                dve.tensor_tensor(cu, cu, cc, ALU.mult).then_inc(conv_step, 1)
                dve.wait_ge(conv_step, n0 + 1)
                taps = [[prm[:, R_CONV + 12 * i + 4 * w + f:][:, 0:1] for w in range(3)] for f in range(4)]
                for f in range(4):
                    dve.tensor_scalar(cc[:, S * f:S * f + S], cu[:, S * f:S * f + S], taps[f][1], None, ALU.mult)\
                       .then_inc(conv_step, 1)
                for f in range(4):
                    y, s = cc[:, S * f:S * f + S], cu[:, S * f:S * f + S]
                    dve.wait_ge(conv_step, n0 + 2 + f)
                    dve.scalar_tensor_tensor(out=y[:, 1:S], in0=s[:, 0:S - 1], scalar=taps[f][0], in1=y[:, 1:S],
                                             op0=ALU.mult, op1=ALU.add).then_inc(conv_step, 1)
                for f in range(4):
                    y, s = cc[:, S * f:S * f + S], cu[:, S * f:S * f + S]
                    dve.wait_ge(conv_step, n0 + 6 + f)
                    dve.scalar_tensor_tensor(out=y[:, 0:S - 1], in0=s[:, 1:S], scalar=taps[f][2], in1=y[:, 0:S - 1],
                                             op0=ALU.mult, op1=ALU.add).then_inc(conv_step, 1)
                dve.wait_ge(conv_step, n0 + 13)
                dve.tensor_tensor(cc, cc, cb, ALU.mult).then_inc(conv_step, 1)

            def conv_lo(i):
                dve.wait_ge(conv_hi, i + 1)
                dve.wait_ge(conv_step, 15 * i + 14)
                dve.tensor_tensor(token_order(br_lo[:, 2, :]), time_order(conv["cc"]),
                                  token_order(br_hi[:, 2, :].bitcast(F32)), ALU.subtract)\
                   .then_inc(conv_step, 1)

            def attend(i, g):
                h, odd = g // 2, g % 2
                nh = NH * i + h
                if not odd and h >= 1:
                    hh = h - 1
                    dve.wait_ge(at_hi, NH * i + hh + 1)
                    dve.tensor_tensor(br_lo[:, 0, S * hh:S * hh + S], ps[:, 3072:3072 + S],
                                      br_hi[:, 0, S * hh:S * hh + S].bitcast(F32), ALU.subtract).then_inc(at_lo, 1)
                if not odd and h < NH:
                    dve.wait_ge(at_s, nh + 1)
                    if nh:
                        dve.wait_ge(at_exp, 2 * nh)
                    dve.tensor_reduce(small[:, 20:22], ps[:, 2048:3072].rearrange("p (q k) -> p q k", q=2),
                                      AX.X, ALU.max).then_inc(at_max, 1)
                    dve.wait_ge(at_max, nh + 1)
                    dve.tensor_scalar(small[:, 16:18], small[:, 20:22], -SCALE, None, ALU.mult).then_inc(at_nm, 1)
                    dve.wait_ge(at_exp, 2 * (nh + 1))
                    dve.reciprocal(small[:, 22:24], small[:, 18:20]).then_inc(at_dve, 1)
                    dve.wait_ge(at_dve, 3 * nh + 1)
                    if nh:
                        dve.wait_ge(at_t, 2 * nh)
                    for q in range(2):
                        dve.tensor_scalar(adiag[:, P * q:P * q + P], ident, small[:, 22 + q:23 + q], None, ALU.mult)\
                           .then_inc(at_dve, 1)
                if odd:
                    dve.wait_ge(at_t, 2 * nh + 2)
                    dve.tensor_copy(aPT[:, 512:1024], bank(7)).then_inc(at_pt_dve, 1)

            def merge(i, m):
                n, j = m // 2, m % 2
                f = NCHK + 2 * m + 1
                a = merged[:, 1024 * j:1024 * j + 1024]
                unit_done(dve, 0, U_L0 * i + fill_unit(f))
                dve.wait_ge(evac_act, 23 * i + NCHK + m + 1)
                if m > 2:
                    dve.wait_ge(mg, 4 * i + m - 2)
                src = ps[:, 1024 * (f % 2):1024 * (f % 2) + 1024]
                if m == 0:
                    dve.wait_ge(rope_done, 6 * (i + 1))
                if n == 0:
                    dve.tensor_tensor(a, gtile, src, ALU.mult).then_inc(evac_dve, 1)
                else:
                    dve.tensor_tensor(utmp, gtile, src, ALU.mult).then_inc(evac_dve, 1)
                    dve.wait_ge(evac_dve, 6 * i + m + 1)
                    dve.tensor_tensor(a, a, utmp, ALU.add).then_inc(mg, 1)

            def mixer(i):
                base = U_L0 * i
                if i == 0:
                    for k in range(LEAD):
                        split(0, k)
                pre_norm(i, 0)
                for u in range(U_MIX):
                    split(0, base + u + LEAD)
                    if i == 0 and u in (1, 3):
                        preamble(u)
                    if u == 7:
                        h_vec(i, 0, 0)
                    if u == 9:
                        h_vec(i, 0, 1)
                    if u == 12:
                        h_vec(i, 0, 2)
                    if u == 14:
                        dve.wait_ge(z_att, 2 * i + 1)
                        h_vec(i, 0, 3)
                    if u == 16:
                        convolve(i)
                    if u == 17:
                        conv_lo(i)
                        h_vec(i, 0, 4)
                    if u == 18:
                        h_vec(i, 0, 5)
                    if u == 19:
                        h_vec(i, 0, 6)
                    if u == 21:
                        h_vec(i, 1, 0)
                    if u == 22:
                        h_vec(i, 1, 1)
                    if u == 24:
                        h_vec(i, 1, 2)
                    if u == 26:
                        dve.wait_ge(z_att, 2 * i + 2)
                        h_vec(i, 1, 3)
                    if u == 28:
                        h_vec(i, 1, 4)
                    if u == 29:
                        h_vec(i, 1, 5)
                    if u == 30:
                        h_vec(i, 1, 6)
                    if u == 33:
                        h_post(i, 0)
                    if u == 34:
                        h_post(i, 1)
                    if 35 <= u < 44:
                        attend(i, u - 35)
                    if u >= U_GATE + 3 and (u - U_GATE) % 3 == 0 and u < U_OUT + 1:
                        m = (u - U_GATE) // 3 - 1
                        merge(i, m)
                    if u in (U_OUT - 2, U_OUT):
                        j = int(u == U_OUT)
                        dve.wait_ge(m_hi, 2 * i + j + 1)
                        dve.tensor_tensor(br_lo[:, 1 + j, :], merged[:, 1024 * j:1024 * j + 1024],
                                          br_hi[:, 1 + j, :].bitcast(F32), ALU.subtract).then_inc(m_lo, 1)

            preamble_steps = [0]

            def preamble(u):

                def step(ins):
                    preamble_steps[0] += 1
                    ins.then_inc(pre, 1)
                    dve.wait_ge(pre, preamble_steps[0])

                lg = prm[:, R_LB:R_LB + 16].rearrange("p (s i k) -> p s i k", s=2, i=DEPTH)
                ex = small[:, 48:64].rearrange("p (s i k) -> p s i k", s=2, i=DEPTH)
                e2 = small[:, 64:80].rearrange("p (s i k) -> p s i k", s=2, i=DEPTH)
                mx = small[:, 24:32].rearrange("p (s a k) -> p s a k", s=2, a=1)
                if u == 1:
                    step(dve.tensor_tensor(mx, lg[:, :, 0:1, :], lg[:, :, 1:2, :], ALU.max))
                    for s in range(2):
                        step(dve.tensor_tensor(ex[:, s], lg[:, s], mx[:, s].to_broadcast([P, DEPTH, NH]), ALU.subtract))
                    dve.wait_ge(pos_loaded, 16)
                    pf = arena[0:ROT, 3584:3584 + S]
                    kr = arena[0:ROT, 3840:3840 + S]
                    step(dve.tensor_copy(pf.rearrange("p (r i) -> p r i", r=4),
                                         arena[0:ROT, 3072:3072 + S].bitcast(I32).rearrange("p (i r) -> p r i", r=4)))
                    step(dve.tensor_scalar(pf, pf, inv_freq, None, ALU.mult))
                    for w, (shift, turn) in enumerate(((HALF_PI, 0.25), (0.0, 0.0))):
                        r = rc[:, w, :]
                        step(dve.tensor_scalar(kr, pf, INV_2PI, turn, ALU.mult, ALU.add))
                        step(dve.tensor_scalar(kr, kr, ROUND, ROUND, ALU.add, ALU.subtract))
                        for part in range(3):
                            step(dve.scalar_tensor_tensor(out=r, in0=kr, scalar=-PI2[part], in1=r if part else pf,
                                                          op0=ALU.mult, op1=ALU.add))
                        step(dve.tensor_scalar(r, r, shift, PI_IN, ALU.add, ALU.min))
                        step(dve.tensor_scalar(r, r, -PI_IN, None, ALU.max))
                    assert preamble_steps[0] == PRE_ANGLES
                else:
                    dve.wait_ge(pre_act, 3)
                    step(dve.tensor_tensor(mx, e2[:, :, 0:1, :], e2[:, :, 1:2, :], ALU.add))
                    step(dve.reciprocal(mx, mx))
                    for s in range(2):
                        step(dve.tensor_tensor(e2[:, s], e2[:, s], mx[:, s].to_broadcast([P, DEPTH, NH]), ALU.mult))
                    step(dve.tensor_tensor(ex[:, :, 1:2, :], e2[:, :, 0:1, :], e2[:, :, 1:2, :], ALU.add))
                    step(dve.tensor_tensor(lb[:, :, 0:1, :], e2[:, :, 0:1, :], e2[:, :, 0:1, :], ALU.subtract))
                    step(dve.tensor_tensor(lb[:, :, 1:2, :], ex[:, :, 1:2, :], e2[:, :, 0:1, :], ALU.subtract))
                    step(dve.tensor_scalar(omlb[:, :, :, :], lb[:, :, :, :], -1.0, 1.0, ALU.mult, ALU.add))
                    step(dve.tensor_scalar(rc[:, 1, :], rc[:, 1, :], rot_sign, None, ALU.mult))
                    assert preamble_steps[0] == PRE_END

            def p_split(i):
                dve.wait_ge(p_hi, i + 1)
                dve.tensor_tensor(br_lo[:, 2, 0:512], bank(7), br_hi[:, 2, 0:512].bitcast(F32), ALU.subtract)\
                   .then_inc(p_lo, 1)

            def dense(base):
                k = base + LEAD

                def hidden(turns, kk, c, n=1024):
                    unit_done(dve, turns, kk)
                    dve.wait_ge(d_sg, c + 1)
                    dve.tensor_tensor(dsg[:, 0:n], dsg[:, 0:n], ps[:, 512 * 6:512 * 6 + n], ALU.mult)\
                       .then_inc(d_hid, 1)
                    dve.wait_ge(d_hi, c + 1)
                    dve.wait_ge(d_hid, c + 1)
                    dve.tensor_tensor(br_lo[:, 0, 0:n], dsg[:, 0:n], br_hi[:, 0, 0:n].bitcast(F32),
                                      ALU.subtract).then_inc(d_lo, 1)

                for u in range(4):
                    split(0, k)
                    k += 1
                hidden(0, base + 3, 0)
                turn0, k0 = k // RING, k % RING
                with dve.Fori(1, NFC) as c:
                    turns = c + (turn0 - 1)
                    for u in range(6):
                        split(turns, k0 + u)
                    hidden(turns, k0 - LEAD + 5, c)
                k += 6 * (NFC - 1)
                for u in range(5):
                    split(0, k + u)
                    if u == 3:
                        hidden(0, k - LEAD + 3, NFC, 512)

            def route():
                n = 0

                def step(ins):
                    nonlocal n
                    n += 1
                    ins.then_inc(r_step, 1)
                    dve.wait_ge(r_step, n)

                dve.wait_ge(r_split, 1)
                dve.tensor_tensor(r_lo[:, :], rout, r_hi[:, :].bitcast(F32), ALU.subtract).then_inc(r_split, 1)
                dve.wait_ge(r_log, 1)
                lg = rt[:, 0:16]
                step(dve.tensor_copy(lg, bank(4)[:, 0:16]))
                for t in range(NT):
                    m8, i8 = rt[:, 16:24], rt[:, 24:32].bitcast(U32)
                    cols = lg[:, 8 * t:8 * t + 8]
                    step(dve.max(out=m8, in_=cols))
                    step(dve.max_index(out=i8, in_max=m8, in_values=cols))
                    step(dve.tensor_copy(rt[:, 32:40], i8))
                    step(dve.tensor_scalar(rt[:, 40:48], iota8, rt[:, 32:33], None, ALU.is_equal))
                    step(dve.tensor_scalar(rt[:, 48:56], iota8, rt[:, 33:34], None, ALU.is_equal))
                    step(dve.tensor_tensor(rt[:, RT_M + 8 * t:RT_M + 8 * t + 8], rt[:, 40:48], rt[:, 48:56], ALU.add))
                    step(dve.tensor_scalar(rt[:, RT_DF + 8 * t:RT_DF + 8 * t + 8], cols, m8[:, 0:1], None,
                                           ALU.subtract))
                assert n == R_DIFF
                dve.wait_ge(r_exp, 1)
                step(dve.tensor_tensor(rt[:, RT_CB:RT_CB + 16], rt[:, RT_EX:RT_EX + 16], rt[:, RT_M:RT_M + 16],
                                       ALU.mult))
                step(dve.tensor_reduce(rt[:, 40:42], rt[:, RT_CB:RT_CB + 16].rearrange("p (t e) -> p t e", t=NT),
                                       AX.X, ALU.add))
                step(dve.reciprocal(rt[:, 42:44], rt[:, 40:42]))
                for t in range(NT):
                    c = rt[:, RT_CB + 8 * t:RT_CB + 8 * t + 8]
                    step(dve.tensor_scalar(c, c, rt[:, 42 + t:43 + t], None, ALU.mult))
                dve.wait_ge(r_rank, 1)
                re = rt[:, RT_RE:RT_RE + 16]
                step(dve.tensor_scalar(re, bank(5)[:, 0:16], 1.0, None, ALU.add))
                step(dve.tensor_tensor(re, re, rt[:, RT_M:RT_M + 16], ALU.mult))
                step(dve.tensor_scalar(re, re, -1.0, None, ALU.add))
                step(dve.memset(rt[:, RT_TAB:RT_TAB + 4 * TAB], -1.0))
                for s in range(2):
                    for t in range(NT):
                        step(dve.tensor_scalar(rt[:, RT_TAB + TAB * t + NE * s:][:, 0:NE], re[:, NE * t:NE * t + NE],
                                               -float(P) * s, None, ALU.add))
                        step(dve.tensor_copy(rt[:, RT_TAB + TAB * (2 + t) + NE * s:][:, 0:NE],
                                             rt[:, RT_CB + NE * t:RT_CB + NE * t + NE]))
                step(dve.tensor_reduce(rt[:, 44:45], bank(5)[:, 16:24], AX.X, ALU.max))
                step(dve.tensor_scalar(rt[:, 45:46], rt[:, 44:45], float(P), 1.0, ALU.is_gt, ALU.add))
                dve.tensor_copy(nsw_i[:, :], rt[:, 45:46]).then_inc(sweeps_ready, 1)

            def select(it):
                tab = rt[:, RT_TAB:RT_TAB + 4 * TAB].rearrange("p (r c) -> p r c", r=4)
                dve.tensor_copy(rk[:, :].rearrange("p (r a) -> p r a", a=1), tab[:, :, bass.ds(it, 1)])\
                   .then_inc(e_rank, 1)
                dve.wait_ge(e_rank, it + 1)
                for t in range(NT):
                    dve.tensor_scalar(sel[:, P * t:P * t + P], iota, rk[:, t:t + 1], None, ALU.is_equal)\
                       .then_inc(e_sel, 1)

            def gathered(it):
                dve.wait_ge(e_xhi, it + 1)
                dve.tensor_tensor(br_lo[:, 1, :], ps[:, 1024:2048], br_hi[:, 1, :].bitcast(F32), ALU.subtract)\
                   .then_inc(e_xlo, 1)

            def accumulate(it, t):
                dve.wait_ge(e_scat, it * 2 + (t + 1))
                dve.wait_ge(e_acc, it * 2 + (1 + t))
                a = yacc[:, DM * t:DM * t + DM]
                dve.tensor_tensor(a, a, ps[:, 1024:2048], ALU.add).then_inc(e_acc, 1)

            def experts(base):
                turn0, k0 = base // RING, base % RING
                select(0)
                dve.wait_ge(gfull_loaded, 16)
                for t in range(NT):
                    a = xn[:, DM * t:DM * t + DM]
                    dve.tensor_tensor(a, a, gfull, ALU.mult).then_inc(xn_scaled, 1)
                split(0, base + 1)
                gathered(0)
                dve.memset(ye_hi.bitcast(F32), 0.0).then_inc(e_ylo, 1)
                dve.memset(ye_lo.bitcast(F32), 0.0).then_inc(e_ylo, 1)
                dve.memset(selct.bitcast(F32), 0.0).then_inc(e_ylo, 1)
                dve.memset(yacc, 0.0).then_inc(e_acc, 1)
                sweeps = dve.value_load(nsw_i[0:1, 0:1], min_val=1, max_val=2)
                with dve.Fori(0, sweeps) as s:
                    with dve.Fori(0, NE) as e:
                        it = s * NE + e
                        turns = it * TURNS_EXP + turn0

                        def turn(c):
                            dve.wait_ge(e_thi, it * NEC + c + 1)
                            dve.tensor_tensor(br_lo[:, 0, 0:512], bank(6), br_hi[:, 0, 0:512].bitcast(F32),
                                              ALU.subtract).then_inc(e_tlo, 1)

                        def hidden(c):
                            dve.wait_ge(e_sg, it * NEC + c + 1)
                            unit_done(dve, turns, k0 + 6 * c + (1 if c else 3))
                            dve.wait_ge(e_turn, it * NEC + (c + ONE))
                            dve.tensor_tensor(hid, msg, bank(5), ALU.mult).then_inc(e_hid, 1)

                        for u in range(2, U_EXP):
                            split(turns, k0 + u)
                            if u == 3:
                                accumulate(it, 0)
                            if u == 5:
                                hidden(0)
                                accumulate(it, 1)
                                dve.tensor_copy(selct, bank(7)[:, 0:256])
                                dve.tensor_copy(cslot, bank(7)[:, 256:257]).then_inc(e_slots, 1)
                            c, step = divmod(u + 2, 6)
                            if step == 3 and 0 < c < NEC:
                                turn(c - 1)
                            if step == 5 and c:
                                hidden(c)
                            if step == 5 and c == 3:
                                select(it + 1)
                        turn(NEC - 1)
                        gathered(it + 1)
                        split(turns, k0 + U_EXP)
                        split(turns, k0 + U_EXP + 1)
                        dve.wait_ge(e_yhi, it + 1)
                        dve.scalar_tensor_tensor(out=ye_lo, in0=ps[:, 0:1024], scalar=cslot, in1=ye_hi.bitcast(F32),
                                                 op0=ALU.mult, op1=ALU.subtract).then_inc(e_ylo, 1)
                accumulate(sweeps * NE, 0)
                accumulate(sweeps * NE, 1)
                return sweeps

            def ple(i, turns, k):
                for u in range(2, U_PLE) if i == DEPTH - 1 else range(LEAD, U_PLE + LEAD):
                    split(turns, k + u)
                for t in range(NT):
                    dve.wait_ge(pl_sig, 2 * i + t + 1)
                    dve.tensor_tensor(y_ple(t), sig[:, DM * t:DM * t + DM], ps[:, 2048 + DM * t:2048 + DM * t + DM],
                                      ALU.mult).then_inc(pl_prod, 1)
                dve.wait_ge(pl_prod, 2 * i + 2)
                post_norm(3 * i + 2, y_ple)

            dve.wait_ge(prm_turned, 1)
            dve.tensor_copy(prm[:, :], bank(0)[:, 0:R_END]).then_inc(prm_ready, 1)
            mixer(0)
            unit_done(dve, 0, U_MIX - 1)
            post_norm(0, y_mixer)
            pre_norm(0, 1)
            p_split(0)
            dense(U_MIX)
            unit_done(dve, 0, U_MIX + U_DENSE - 1)
            post_norm(1, y_dense)
            pre_norm(0, 2)
            ple(0, 0, U_MIX + U_DENSE)
            mixer(1)
            unit_done(dve, 0, U_L0 + U_MIX - 1)
            post_norm(3, y_mixer)
            pre_norm(1, 1)
            p_split(1)
            route()
            sweeps = experts(U_L0 + U_MIX)
            dve.wait_ge(e_acc, sweeps * (NE * 2) + 3)
            post_norm(4, y_experts)
            pre_norm(1, 2)
            k = U_L0 + U_MIX
            ple(1, sweeps * (NE * TURNS_EXP) + k // RING, k % RING)

        @block.gpsimd
        def _(pool):
            pool.memset(minus_half[:, :], -0.5).then_inc(half_ready, 1)
            pool.wait_ge(half_ready, 1)

            def root(src, dst, ready, count, done):
                pool.wait_ge(ready, count)
                pool.tensor_tensor(small[:, dst:dst + 1], small[:, src:src + 1], minus_half[:, 0:1], ALU.pow)\
                    .then_inc(done, 1)

            def rope(i, r):
                n = 6 * i + r
                qr = A[ROPED[r]][0:ROT, :].rearrange("p (h t) -> p h t", h=NH)
                sw = swapped.rearrange("p (h t) -> p h t", h=NH)
                cos = rc[:, 0:1, :].to_broadcast([ROT, NH, S])
                sin = rc[:, 1:2, :].to_broadcast([ROT, NH, S])
                pool.wait_ge(half_swapped, 32 * (n + 1))
                pool.tensor_tensor(sw, sw, sin, ALU.mult).then_inc(rope_step, 1)
                pool.tensor_tensor(qr, qr, cos, ALU.mult).then_inc(rope_step, 1)
                pool.wait_ge(rope_step, 2 * (n + 1))
                pool.tensor_tensor(qr, qr, sw, ALU.add).then_inc(rope_done, 1)

            for i in range(DEPTH):
                for m in range(3):
                    n = 3 * i + m
                    for t in range(NT):
                        root(2 + t, 8 + t, var_ready, NT * n + t + 1, rstd_ready)
                    if m == 0:
                        for d in range(2):
                            if d:
                                pool.wait_ge(h_pe, hpe(i, 0, 3))
                            else:
                                pool.wait_ge(xn_ready, NT * (n + 1))
                            pool.memset(attT, 0.0).then_inc(z_att, 1)
                        if i == 0:
                            pool.wait_ge(pre, PRE_END)
                        for r in range(len(ROPED)):
                            rope(i, r)
                        pool.wait_ge(h_dve, hdve(i, 2, 1))
                        pool.tensor_tensor(small[:, 88:96], small[:, 80:88], minus_half[:, :], ALU.pow).then_inc(h_pow, 1)
                    for t in range(NT):
                        root(6 + t, 10 + t, post_var, NT * n + t + 1, post_rstd)

        @block.tensor
        def _(pe):
            def mm3(o, l_hi, l_lo, r_hi_, r_lo_, start):
                pe.matmul(o, l_hi, r_hi_, start=start, stop=False, skip_group_check=True)
                pe.matmul(o, l_hi, r_lo_, start=False, stop=False, skip_group_check=True)
                return pe.matmul(o, l_lo, r_hi_, start=False, stop=True, skip_group_check=True)

            def take(turns, k, h):
                pe.wait_ge(lo_ready, turns * (RING * PARTS) + PARTS * k + h + 1)

            def feat_unit(turns, k, b0, kh, a_hi, a_lo, norm=None):
                wh, wl = unit_w(w_hi, k), unit_w(w_lo, k)
                for h in range(PARTS):
                    take(turns, k, h)
                    if norm is not None:
                        h_split(norm, 4 * kh + 2 * h + 2)
                    for f in range(4):
                        o = ps[:, 512 * b0 + S * f:512 * b0 + S * f + S]
                        for kk in (2 * h, 2 * h + 1):
                            ins = mm3(o, wh[:, kk, P * f:P * f + P], wl[:, kk, P * f:P * f + P],
                                      a_hi[:, 4 * kh + kk, :], a_lo[:, 4 * kh + kk, :],
                                      start=(kh == 0 and kk == 0 and f % 2 == 0))
                    ins.then_inc(part_used, 1)

            def tok_unit(turns, k, outs, kh, a, starts):
                wh, wl = unit_w(w_hi, k), unit_w(w_lo, k)
                for h in range(PARTS):
                    take(turns, k, h)
                    for t, o in enumerate(outs):
                        for kk in (2 * h, 2 * h + 1):
                            ah, al = a(t, 4 * kh + kk)
                            ins = mm3(o, ah, al, wh[:, kk, :], wl[:, kk, :], start=(starts and kk == 0))
                    ins.then_inc(part_used, 1)

            def merged_nat(t, k):
                b, c = 1 + k // 4, S * (k % 4) + P * t
                return br_hi[:, b, c:c + P], br_lo[:, b, c:c + P]

            def hT_nat(t, k):
                return hT_hi[:, k, P * t:P * t + P], hT_lo[:, k, P * t:P * t + P]

            def pre_norm(i, m):
                n = 3 * i + m
                for t in range(NT):
                    pe.wait_ge(xn_ready, NT * n + t + 1)
                    for k in range(KT):
                        ins = pe.transpose(h_turned(m, k)[:, P * t:P * t + P],
                                           xn[:, DM * t + P * k:DM * t + P * k + P], ident)
                        if t and k % 2:
                            ins.then_inc(turned, 1)

            def h_split(n, tiles=KT):
                pe.wait_ge(hT_lo_ready, KT * n + tiles)

            def fill_wait(i, f):
                f -= 2
                if f < 0:
                    return
                if f < NCHK:
                    pe.wait_ge(evac_act, 23 * i + f + 1)
                elif (f - NCHK) % 2 == 0:
                    pe.wait_ge(evac_act, 23 * i + NCHK + (f - NCHK) // 2 + 1)
                else:
                    pe.wait_ge(evac_dve, 6 * i + (f - NCHK) // 2 + 1)

            def h_step(i, d, step):
                chunks = range(NCH) if d == 0 else range(NCH - 1, -1, -1)
                v = B["inp"]

                def inter(c):
                    for h in range(NH):
                        ins = pe.matmul(ps[:, 3072 + S * h + CH * c:3072 + S * h + CH * c + CH],
                                        hS[:, HD * h:HD * h + HD], hC[:, S * h + CH * c:S * h + CH * c + CH],
                                        start=False, stop=True, skip_group_check=True)
                    return ins

                def outer(c):
                    p0, t = CH * (c % 2), c // 2
                    for h in range(NH):
                        ins = pe.matmul(bank(4)[:, HD * h:HD * h + HD],
                                        kdT[p0:p0 + CH, 256 * h + P * t:256 * h + P * t + P],
                                        v[p0:p0 + CH, 512 * t + HD * h:512 * t + HD * h + HD], start=True, stop=True)
                    return ins

                if step == 1:
                    pe.wait_ge(h_dve, hdve(i, d, 13))
                    for j in range(NH * NT):
                        cols = slice(P * j, P * j + P)
                        ins = pe.matmul(ps[:, 2048 + P * j:2048 + P * j + P], hL[:, cols], h1[:, cols],
                                        start=True, stop=True)
                    ins.then_inc(h_pe, 1)
                if step == 2:
                    pe.wait_ge(h_dve, hdve(i, d, 20))
                    for j in range(NH * NT):
                        ins = pe.transpose(ps[:, 2048 + P * j:2048 + P * j + P], h2[:, P * j:P * j + P], ident)
                    ins.then_inc(h_pe, 1)
                if step == 3:
                    pe.wait_ge(h_act, hact(i, d, 8))
                    for h in range(NH):
                        for t in range(NT):
                            j = NT * h + t
                            pe.matmul(ps[:, 3072 + P * j:3072 + P * j + P],
                                      B["inp"][:, 512 * t + HD * h:512 * t + HD * h + HD], attT[:, P * j:P * j + P],
                                      start=(d == 0 and t == 0 and h % 2 == 0), stop=True, skip_group_check=True)
                    outer(chunks[0]).then_inc(h_pe, 1)
                if step in (4, 5):
                    pe.wait_ge(h_dve, hdve(i, d, 21 + 4 * (step - 4)))
                    if step == 4:
                        pe.wait_ge(h_dve, hdve(i, d, 19))
                    inter(chunks[step - 3])
                    outer(chunks[step - 3]).then_inc(h_pe, 1)
                if step == 6:
                    pe.wait_ge(h_dve, hdve(i, d, 29))
                    inter(chunks[3]).then_inc(h_pe, 1)

            def h_post(i, step):
                if step == 0:
                    pe.wait_ge(h_act, hact(i, 2, 2))
                    for j in range(8):
                        ins = pe.matmul(bank(4)[:, j:j + 1], hL[:, P * j:P * j + P], ones[:, 0:1], start=True, stop=True)
                    ins.then_inc(h_pe, 1)
                else:
                    pe.wait_ge(h_dve, hdve(i, 2, 9))
                    for j in range(2):
                        ins = pe.matmul(bank(4 + j), ones, hC[:, 512 * j:512 * j + 512], start=True, stop=True)
                    ins.then_inc(h_pe, 1)

            def attend(i, g):
                h, odd = g // 2, g % 2
                nh = NH * i + h
                if not odd and h >= 1:
                    hh = h - 1
                    pe.wait_ge(at_pt_act, NH * i + hh + 1)
                    pe.wait_ge(at_pt_dve, NH * i + hh + 1)
                    for q in range(2):
                        o = ps[:, 3072 + P * q:3072 + P * q + P]
                        for j, (grp, t) in enumerate(((0, 0), (0, 1), (1, q), (2, q))):
                            ins = pe.matmul(o, A[f"av{grp}"][:, 512 * t + HD * hh:512 * t + HD * hh + HD],
                                            aPT[:, 512 * q + P * j:512 * q + P * j + P], start=(j == 0), stop=(j == 3))
                    ins.then_inc(at_v, 1)
                if not odd and h < NH:
                    if h == 0:
                        pe.wait_ge(rope_done, 6 * (i + 1))
                        pe.wait_ge(evac_act, 23 * i + NCHK)
                        pe.wait_ge(h_dve, hdve(i, 2, 13))
                    else:
                        pe.wait_ge(at_exp, 2 * nh)
                    hs = slice(S * h, S * h + S)
                    for q in range(2):
                        pe.matmul(bank(4 + q), identb[:, :], maskb[:, q, :], start=True, stop=False,
                                  skip_group_check=True)
                        for grp in range(NG):
                            qT = A[f"aq{grp}"][:, S * h + P * q:S * h + P * q + P]
                            kT = A[f"ak{grp}"][:, hs]
                            if grp == 0:
                                o = ps[:, 2048 + 512 * q:2048 + 512 * q + S]
                            else:
                                kT = A[f"ak{grp}"][:, S * h + P * q:S * h + P * q + P]
                                o = ps[:, 2048 + 512 * q + P * (grp + 1):2048 + 512 * q + P * (grp + 2)]
                            ins = pe.matmul(o, qT, kT, start=False, stop=True, skip_group_check=True)
                    ins.then_inc(at_s, 1)
                if odd:
                    pe.wait_ge(at_dve, 3 * (nh + 1))
                    if h:
                        pe.wait_ge(at_lo, NH * i + h)
                    else:
                        pe.wait_ge(h_act, hact(i, 2, 2))
                    for q in range(2):
                        for j in range(4):
                            ins = pe.matmul(bank(6 + q)[:, P * j:P * j + P], aP[:, 512 * q + P * j:512 * q + P * j + P],
                                            adiag[:, P * q:P * q + P], start=True, stop=True)
                        ins.then_inc(at_t, 1)

            def mixer(i):
                base = U_L0 * i
                pre_norm(i, 0)
                for u in range(U_MIX):
                    k = base + u
                    if u < U_GATE:
                        c, kh = u // 2, u % 2
                        name, _, layout = CHUNKS[c]
                        if kh == 0:
                            fill_wait(i, c)
                        b0 = 2 * (c % 2)
                        if layout == "feat":
                            feat_unit(0, k, b0, kh, hT_hi, hT_lo, norm=3 * i if c == 0 else None)
                        else:
                            tok_unit(0, k, [bank(b0), bank(b0 + 1)], kh, hT_nat, kh == 0)
                    elif u < U_OUT:
                        m, r = divmod(u - U_GATE, 3)
                        f = NCHK + 2 * m + (r == 2)
                        if r != 1:
                            fill_wait(i, f)
                        b0 = 2 * (f % 2)
                        if r < 2:
                            feat_unit(0, k, b0, r, hT_hi, hT_lo)
                        else:
                            n = BRANCH_ORDER[m // 2]
                            if n == 2:
                                pe.wait_ge(conv_step, 15 * (i + 1))
                            elif n == 1:
                                pe.wait_ge(h_dve, hdve(i, 2, 15))
                            else:
                                pe.wait_ge(at_lo, NH * (i + 1))
                            feat_unit(0, k, b0, 0, br_hi[:, n, :].rearrange("p (k t) -> p k t", k=4),
                                      br_lo[:, n, :].rearrange("p (k t) -> p k t", k=4))
                    else:
                        kh, j = divmod(u - U_OUT, 2)
                        if j == 0:
                            pe.wait_ge(m_lo, 2 * i + kh + 1)
                        tok_unit(0, k, [bank(4 + j), bank(6 + j)], kh, merged_nat, kh == 0)
                    if u == 8:
                        pe.wait_ge(evac_act, 23 * i + CIDX["inp"] + 1)
                        for t in range(NT):
                            for h in range(NH):
                                ins = pe.transpose(bank(4 + t)[:, HD * h:HD * h + HD],
                                                   h1[:, S * h + P * t:S * h + P * t + P], ident)
                        ins.then_inc(inp_turned, 1)
                    if u == 14:
                        h_step(i, 0, 1)
                    if u == 15:
                        h_step(i, 0, 2)
                    if u == 16:
                        h_step(i, 0, 3)
                    if u == 17:
                        h_step(i, 0, 4)
                    if u == 18:
                        h_step(i, 0, 5)
                    if u == 20:
                        h_step(i, 0, 6)
                    if u == 25:
                        h_step(i, 1, 1)
                    if u == 26:
                        h_step(i, 1, 2)
                    if u == 27:
                        h_step(i, 1, 3)
                    if u == 28:
                        h_step(i, 1, 4)
                    if u == 29:
                        h_step(i, 1, 5)
                    if u == 31:
                        h_step(i, 1, 6)
                    if u == 32:
                        h_post(i, 0)
                    if u == 33:
                        h_post(i, 1)
                    if 35 <= u < 44:
                        attend(i, u - 35)

            def p_turn(i):
                pe.wait_ge(p_loaded, 64 * (i + 1))
                for kk in range(2):
                    for t in range(NT):
                        ins = pe.transpose(bank(7)[:, S * kk + P * t:S * kk + P * t + P],
                                           ptok[:, PLE * t + P * kk:PLE * t + P * kk + P], ident)
                ins.then_inc(p_turned, 1)

            def dense(base):
                k = base

                def feats(turns, kk, b0, kh, norm=None):
                    feat_unit(turns, kk, b0, kh, hT_hi, hT_lo, norm)

                def hT4(t, kk):
                    return (br_hi[:, 0, S * kk + P * t:S * kk + P * t + P],
                            br_lo[:, 0, S * kk + P * t:S * kk + P * t + P])

                def down(turns, kk, c, first=False):
                    for j in range(2):
                        tok_unit(turns, kk + j, [bank(j), bank(2 + j)], 0, hT4, first)

                for kh in range(2):
                    feats(0, k + kh, 4, kh, norm=1)
                pe.wait_ge(p_lo, 1)
                for kh in range(2):
                    feats(0, k + 2 + kh, 6, kh)
                k += 4

                def body(turns, kk, c, first):
                    pe.wait_ge(d_sg, c)
                    for kh in range(2):
                        feats(turns, kk + kh, 4, kh)
                        pe.wait_ge(d_lo, c)
                    down(turns, kk + 2, c - 1, first)
                    for kh in range(2):
                        feats(turns, kk + 4 + kh, 6, kh)
    
                body(0, k, 1, True)
                k += 6
                turn0, k0 = k // RING, k % RING
                with pe.Fori(2, NFC) as c:
                    body(c + (turn0 - 2), k0, c, False)
                k += 6 * (NFC - 2)
                def half(kk, b):
                    wh, wl = (w[:, kk % NSPL, :].rearrange("p (k n) -> p k n", k=KT) for w in (w_hi, w_lo))
                    for h in range(PARTS):
                        take(0, kk, h)
                        for f in range(2):
                            for kx in range(4 * h, 4 * h + 4):
                                ins = mm3(ps[:, 512 * b + S * f:512 * b + S * f + S], wh[:, kx, P * f:P * f + P],
                                          wl[:, kx, P * f:P * f + P], hT_hi[:, kx, :], hT_lo[:, kx, :],
                                          start=(kx == 0 and f == 0))
                        ins.then_inc(part_used, 1)

                pe.wait_ge(d_sg, NFC)
                half(k, 4)
                pe.wait_ge(d_lo, NFC)
                down(0, k + 1, NFC - 1)
                half(k + 3, 6)
                pe.wait_ge(d_lo, NFC + 1)
                kk = k + 4
                wh, wl = (w[:, kk % NSPL, :].rearrange("p (k n) -> p k n", k=2) for w in (w_hi, w_lo))
                for kx in range(2):
                    take(0, kk, kx)
                    for t in range(NT):
                        for j in range(2):
                            ah, al = hT4(t, kx)
                            ins = mm3(bank(2 * t + j), ah, al, wh[:, kx, 512 * j:512 * j + 512],
                                      wl[:, kx, 512 * j:512 * j + 512], start=False)
                    ins.then_inc(part_used, 1)

            def route():
                h_split(4)
                pe.wait_ge(r_split, 2)
                for t in range(NT):
                    for k in range(KT):
                        ah, al = hT_nat(t, k)
                        ins = mm3(bank(4)[:, NE * t:NE * t + NE], ah, al, r_hi[:, NE * k:NE * k + NE],
                                  r_lo[:, NE * k:NE * k + NE], start=(t == 0 and k == 0))
                ins.then_inc(r_log, 1)
                pe.wait_ge(r_step, R_DIFF)
                mk = [rt[:, RT_M + NE * t:RT_M + NE * t + NE] for t in range(NT)]
                b = bank(5)
                pe.matmul(b[:, 0:8], lower, mk[0], start=True, stop=True)
                pe.matmul(b[:, 8:16], lower, mk[1], start=True, stop=False)
                pe.matmul(b[:, 8:16], ones, mk[0], start=False, stop=True)
                pe.matmul(b[:, 16:24], ones, mk[0], start=True, stop=False)
                pe.matmul(b[:, 16:24], ones, mk[1], start=False, stop=True).then_inc(r_rank, 1)

            def gather(it):
                pe.wait_ge(e_sel, (it + 1) * 2)
                for k in range(KT):
                    for t in range(NT):
                        ins = pe.matmul(ps[:, 1024 + P * k:1024 + P * k + P],
                                        xn[:, DM * t + P * k:DM * t + P * k + P], sel[:, P * t:P * t + P],
                                        start=(t == 0), stop=(t == NT - 1))
                for t in range(NT):
                    pe.transpose(bank(7)[:, P * t:P * t + P], sel[:, P * t:P * t + P], ident)
                for t in range(NT):
                    ins = pe.matmul(bank(7)[:, 256:257], sel[:, P * t:P * t + P], rk[:, 2 + t:3 + t],
                                    start=(t == 0), stop=(t == NT - 1))
                ins.then_inc(e_gath, 1)

            def scatter(it, t):
                pe.wait_ge(e_ylo, it + 3)
                if t:
                    pe.wait_ge(e_acc, it * 2 + 2)
                for j in range(2):
                    cols = slice(512 * j, 512 * j + 512)
                    pe.matmul(bank(2 + j), selct[:, P * t:P * t + P], ye_hi[:, cols], start=True, stop=False)
                    ins = pe.matmul(bank(2 + j), selct[:, P * t:P * t + P], ye_lo[:, cols], start=False, stop=True)
                ins.then_inc(e_scat, 1)

            def experts(base):
                turn0, k0 = base // RING, base % RING
                pe.sem_inc(e_turn, ONE)
                pe.wait_ge(xn_scaled, NT)
                gather(0)
                pe.wait_ge(sweeps_ready, 1)
                sweeps = pe.value_load(nsw_i[0:1, 0:1], min_val=1, max_val=2)
                with pe.Fori(0, sweeps) as s:
                    with pe.Fori(0, NE) as e:
                        it = s * NE + e
                        turns = it * TURNS_EXP + turn0

                        def xg4(t, k):
                            return br_hi[:, 1, P * k:P * k + P], br_lo[:, 1, P * k:P * k + P]

                        def hid4(t, k):
                            return br_hi[:, 0, P * k:P * k + P], br_lo[:, 0, P * k:P * k + P]

                        def turn(c):
                            pe.wait_ge(e_hid, it * NEC + c + 1)
                            for f in range(4):
                                ins = pe.transpose(bank(6)[:, P * f:P * f + P], hid[:, P * f:P * f + P], ident)
                            ins.then_inc(e_turn, 1)

                        pe.wait_ge(e_xlo, it + 1)
                        kk = k0
                        for c in range(NEC):
                            if c:
                                pe.wait_ge(e_sg, it * NEC + c)
                            for kh in range(2):
                                tok_unit(turns, kk, [bank(4)], kh, xg4, kh == 0)
                                kk += 1
                            if c:
                                turn(c - 1)
                            else:
                                scatter(it, 0)
                            for kh in range(2):
                                tok_unit(turns, kk, [bank(5)], kh, xg4, kh == 0)
                                kk += 1
                            if c:
                                pe.wait_ge(e_tlo, it * NEC + c)
                                for j in range(2):
                                    tok_unit(turns, kk, [bank(j)], 0, hid4, c == 1)
                                    kk += 1
                            else:
                                scatter(it, 1)
                        turn(NEC - 1)
                        pe.wait_ge(e_slots, it + 1)
                        pe.wait_ge(e_acc, it * 2 + 3)
                        gather(it + 1)
                        pe.wait_ge(e_tlo, it * NEC + NEC)
                        for j in range(2):
                            tok_unit(turns, kk, [bank(j)], 0, hid4, False)
                            kk += 1
                pe.wait_ge(e_xlo, sweeps * NE + 1)
                scatter(sweeps * NE, 0)
                scatter(sweeps * NE, 1)
                return sweeps

            def ple(i, turns, k):
                pe.wait_ge(p_lo, i + 1)
                wh, wl = (w[:, k % NSPL, :].rearrange("p (k n) -> p k n", k=2) for w in (w_hi, w_lo))
                for kx in range(2):
                    take(turns, k, kx)
                    for t in range(NT):
                        for j in range(2):
                            ins = mm3(bank(4 + 2 * t + j), br_hi[:, 2, S * kx + P * t:S * kx + P * t + P],
                                      br_lo[:, 2, S * kx + P * t:S * kx + P * t + P],
                                      wh[:, kx, 512 * j:512 * j + 512], wl[:, kx, 512 * j:512 * j + 512],
                                      start=(kx == 0))
                    ins.then_inc(part_used, 1)
                pre_norm(i, 2)
                h_split(3 * i + 2)
                for j in range(2):
                    for kh in range(2):
                        k += 1
                        tok_unit(turns, k, [bank(j), bank(2 + j)], kh, hT_nat, kh == 0)

            pe.wait_ge(const_loaded, 16 * 9)
            pe.transpose(bank(0)[:, 0:R_END], arena[0:R_END, 2048:2048 + P], cst[0:R_END, C_ID:C_ID + R_END])\
              .then_inc(prm_turned, 1)
            mixer(0)
            pre_norm(0, 1)
            p_turn(0)
            dense(U_MIX)
            ple(0, 0, U_MIX + U_DENSE)
            mixer(1)
            pre_norm(1, 1)
            p_turn(1)
            route()
            sweeps = experts(U_L0 + U_MIX)
            k = U_L0 + U_MIX
            ple(1, sweeps * (NE * TURNS_EXP) + k // RING, k % RING)


ONE = 1
RT_M, RT_DF, RT_EX, RT_CB, RT_RE, RT_TAB = 56, 72, 88, 104, 72, 120
TAB = 2 * NE + 1
R_DIFF = 1 + 7 * NT
PRE_ANGLES = 3 + 2 + 14
PRE_END = PRE_ANGLES + 9
INV_2PI = 0.15915494309189535
HALF_PI = 1.5707963267948966
PI_IN = 3.1415925
PI2 = (6.28125, 0.0019350051879882812, 3.0199159819567e-07)
ROUND = 12582912.0


def shape_constants(np):
    c = np.zeros((P, C_END), np.float32)
    r = np.arange(P)
    c[:, C_ID:C_ID + P] = np.eye(P)
    c[:, C_ONE:C_ONE + P] = 1.0
    c[:, C_LT:C_LT + P] = r[:, None] < r[None, :]
    c[:, C_IOTA:C_IOTA + P] = r[None, :]
    c[:, C_SCAN:C_SCAN + 512] = np.arange(512)[None, :] % CH != 0
    s, t = r[:, None], r[None, :]
    c[:, C_MASK:C_MASK + P] = (s <= t) & (s // CH == t // CH)
    c[:, C_MASK + P:C_MASK + 2 * P] = (s >= t) & (s // CH == t // CH)
    half = ROT // 2
    c[0:ROT, C_SIGN] = np.where(np.arange(ROT) < half, -1.0, 1.0)
    c[0:ROT, C_INV] = (500000.0 ** (-(np.arange(ROT) % half) * 2.0 / ROT)).astype(np.float32)
    c[:, C_I8:C_I8 + NE] = np.arange(NE)[None, :]
    order = np.array([4 * i + res for res in range(4) for i in range(S // 4)])
    mask = np.zeros((P, 2, 512), np.float32)
    for q in range(2):
        tq = order[P * q:P * q + P][:, None]
        own = order[P * q:P * q + P][None, :]
        mask[:, q, 0:S] = np.where(np.abs(tq - order[None, :]) <= 64, 0.0, -1e30)
        mask[:, q, S:S + P] = np.where((tq - own) % 4 == 0, 0.0, -1e30)
        mask[:, q, S + P:S + 2 * P] = np.where((tq - own) % 16 == 0, 0.0, -1e30)
    return c, mask, np.eye(P)


_INS = ["x", "p", "positions", "w_in", "conv_w", "hgrn_lb_logits", "hgrn_norm_g", "w_branch", "w_out",
        "g_mix_pre", "g_mix_post", "g_ffn_pre", "g_ffn_post", "dense_w_gate", "dense_w_up", "dense_w_down",
        "moe_router", "moe_w_gate", "moe_w_up", "moe_w_down", "ple_w_proj", "ple_w_gate", "ple_g_in", "ple_g_post"]


def kernel(**inputs):
    import ml_dtypes as _ml
    import numpy as _np
    import concourse.bacc as _bacc
    from concourse import mybir as _mybir
    from concourse.bass_utils import run_bass_kernel_spmd as _run

    nc = _bacc.Bacc("TRN2", target_bir_lowering=False, num_devices=1, dynamic_dma_scratch_size=1024)
    arrays, io = {}, {}

    def give(name, a):
        arrays[f"in_{name}_dram"] = a
        io[name] = nc.dram_tensor(f"in_{name}_dram", a.shape, _mybir.dt.from_np(a.dtype), kind="ExternalInput").ap()

    for name in _INS:
        give(name, _np.ascontiguousarray(inputs[name]))
    const, mask, eye = shape_constants(_np)
    give("const", const)
    give("maskb", mask.astype(_ml.bfloat16))
    give("identb", eye.astype(_ml.bfloat16))
    out = nc.dram_tensor("out_0_dram", (1, S, DM), F32, kind="ExternalOutput").ap()
    build(nc, io, out)
    r = _run(nc, [arrays], core_ids=[0])
    return r.results[0]["out_0_dram"]
```

```python
from contextlib import ExitStack

import concourse.bass as bass
from concourse import mybir

F32 = mybir.dt.float32
F32R = mybir.dt.float32r
BF16 = mybir.dt.bfloat16
I32 = mybir.dt.int32
U32 = mybir.dt.uint32
ALU = mybir.AluOpType
ACT = mybir.ActivationFunctionType
AX = mybir.AxisListType

P = 128
DM = 1024
S = 256
NT = S // P
KT = DM // P
DEPTH = 2
EPS = 1e-6
NH = 4
HD = 128
ROT = HD // 4
NG = 3
CH = 64
NCH = S // CH
FD = 2816
NE = 8
FE = 3584
PLE = 256
SCALE = float(HD) ** -0.5
UC = 512
UN = 2048
RING = 6
NSPL = 2
LEAD = NSPL - 1
PARTS = 2
PC = UN // PARTS

CHUNKS = [("zf", 10, "feat"), ("zb", 11, "feat"), ("q", 9, "feat"), ("inp", 12, "feat"), ("gate", 13, "feat"),
          ("cu", 14, "feat"), ("cb", 15, "feat"), ("cc", 16, "feat")]
for _g in range(NG):
    CHUNKS += [(f"aq{_g}", 3 * _g, "feat"), (f"ak{_g}", 3 * _g + 1, "feat"), (f"av{_g}", 3 * _g + 2, "tok")]
NCHK = len(CHUNKS)
BRANCH_ORDER = [2, 1, 0]
U_GATE = 2 * NCHK
U_OUT = U_GATE + 3 * 6
U_MIX = U_OUT + 4
NFC = FD // UC
U_DENSE = 6 * NFC + 3
U_PLE = 5
NEC = FE // UC
U_EXP = 6 * NEC
TURNS_EXP = U_EXP // RING
U_L0 = U_MIX + U_DENSE + U_PLE
CIDX = {name: n for n, (name, _, _) in enumerate(CHUNKS)}
ROPED = [f"a{x}{g}" for g in range(NG) for x in "qk"]

C_ID, C_ONE, C_LT, C_IOTA, C_SCAN = 0, 128, 256, 384, 512
C_MASK, C_SIGN, C_INV, C_I8, C_END = 1024, 1280, 1281, 1282, 1290
R_MIX, R_FFN, R_PLE, R_CONV, R_LB, R_NG, R_END = 0, 16, 32, 48, 72, 88, 96


def build(nc, io, out):
    ctx = ExitStack()
    with ctx:
        def sb(name, shape, dt=F32):
            return ctx.enter_context(nc.sbuf_tensor(name, shape, dt))

        def sem(name):
            return ctx.enter_context(nc.semaphore(name))

        x = sb("x", [P, NT, DM])
        raw = sb("raw", [P, RING, UN])
        w_hi = sb("w_hi", [P, NSPL, UN], F32R)
        w_lo = sb("w_lo", [P, NSPL, UN], F32R)
        hT_hi = sb("hT_hi", [P, KT, S], F32R)
        hT_lo = sb("hT_lo", [P, KT, S], F32R)
        br_hi = sb("br_hi", [P, 3, 1024], F32R)
        br_lo = sb("br_lo", [P, 3, 1024], F32R)
        cst = sb("cst", [P, C_END])
        prm = sb("prm", [P, R_END])
        maskb = sb("maskb", [P, 2, 512], BF16)
        identb = sb("identb", [P, P], BF16)
        rc = sb("rc", [ROT, 2, S])
        lb = sb("lb", [P, 2, DEPTH, NH])
        omlb = sb("omlb", [P, 2, DEPTH, NH])
        small = sb("small", [P, 96])
        arena = sb("arena", [P, 20 * 1024])

        ident = cst[:, C_ID:C_ID + P]
        ones = cst[:, C_ONE:C_ONE + P]
        lower = cst[:, C_LT:C_LT + P]
        iota = cst[:, C_IOTA:C_IOTA + P]
        scan_keep = cst[:, C_SCAN:C_SCAN + 512]
        causal = [cst[:, C_MASK + P * d:C_MASK + P * d + P].bitcast(U32) for d in range(2)]
        rot_sign = cst[0:ROT, C_SIGN:C_SIGN + 1]
        inv_freq = cst[0:ROT, C_INV:C_INV + 1]
        iota8 = cst[:, C_I8:C_I8 + NE]

        def area(k, n=1024):
            return arena[:, 1024 * k:1024 * k + n]

        A = {f"a{x}{g}": area(3 * g + j) for g in range(NG) for j, x in enumerate("qkv")}
        B = {"zf": area(9), "zb": area(10), "q": area(11), "inp": area(12), "gate": area(13)}
        hL, hC, h1, h2 = area(14), area(15), area(16), area(17)
        kdT = area(18)
        attT = area(19)
        hS = sb("hS", [P, NH * HD])[:, :]
        conv = {"cu": A["aq2"], "cb": A["ak2"], "cc": A["av2"]}
        DEST = {**A, **B, **conv, "inp": h1}
        IN_TIME = (*B, *conv)
        merged = arena[:, 1024 * 9:1024 * 11]
        swapped = arena[0:ROT, 1024 * 9:1024 * 10]
        gtile = area(11)
        aP, aPT = area(12), area(13)
        adiag = area(14, 256)
        utmp = area(15)
        xn = arena[:, 0:2048]
        gained = arena[:, 1024 * 14:1024 * 16]
        junk = area(17)
        gb = area(18)
        dsg = area(4)
        yacc = arena[:, 1024 * 2:1024 * 4]
        gfull = area(4)
        hid = area(6, 512)
        msg = arena[:, 1024 * 6 + 512:1024 * 7]
        sel = area(7, 256)
        cslot = arena[:, 1024 * 7 + 256:1024 * 7 + 257]
        rout = area(6)
        logT = area(10)[0:NE, 0:S]
        rt = arena[:, 1024 * 7 + 832:1024 * 8]
        ye_hi = hT_hi[:, 0:4, :].rearrange("p k t -> p (k t)")
        ye_lo = hT_lo[:, 0:4, :].rearrange("p k t -> p (k t)")
        selct = hT_hi[:, 4, :]
        rk = sb("rk", [P, 4])
        minus_half = sb("minus_half", [P, 8])
        nsw_i = sb("nsw_i", [P, 1], I32)
        r_hi, r_lo = br_hi[:, 1, :], br_lo[:, 1, :]
        ptok = area(8, 512)
        sig = arena[:, 1024 * 10:1024 * 12]
        eprod = arena[:, 1024 * 12:1024 * 14]

        ps = ctx.enter_context(nc.psum_tensor("ps", [P, 8 * 512], F32))

        def bank(b, n=512):
            return ps[:, 512 * b:512 * b + n]

        raw_loaded = [sem(f"raw_loaded{n}") for n in range(RING)]
        hi_ready, lo_ready, part_used = sem("hi_ready"), sem("lo_ready"), sem("part_used")
        x_loaded = [sem(f"x_loaded{t}") for t in range(NT)]
        ident_loaded, const_loaded, tables_loaded = sem("ident_loaded"), sem("const_loaded"), sem("tables_loaded")
        gb_loaded, p_loaded, rout_loaded = sem("gb_loaded"), sem("p_loaded"), sem("rout_loaded")
        prm_turned, prm_ready, pre = sem("prm_turned"), sem("prm_ready"), sem("pre")
        pre_act = sem("pre_act")
        ssq, var_ready, rstd_ready, xn_ready = sem("ssq"), sem("var_ready"), sem("rstd_ready"), sem("xn_ready")
        turned, hT_hi_ready, hT_lo_ready = sem("turned"), sem("hT_hi_ready"), sem("hT_lo_ready")
        post_ssq, post_var, post_rstd, post_gain, x_ready = (
            sem("post_ssq"), sem("post_var"), sem("post_rstd"), sem("post_gain"), sem("x_ready"))
        y0_done = sem("y0_done")
        evac_act, evac_dve = sem("evac_act"), sem("evac_dve")
        half_ready, z_att = sem("half_ready"), sem("z_att")
        inp_turned, inp_ready = sem("inp_turned"), sem("inp_ready")
        half_swapped, rope_step, rope_done = sem("half_swapped"), sem("rope_step"), sem("rope_done")
        h_pe, h_act, h_dve, h_pow = sem("h_pe"), sem("h_act"), sem("h_dve"), sem("h_pow")
        conv_step, conv_hi = sem("conv_step"), sem("conv_hi")
        at_s, at_t, at_v = sem("at_s"), sem("at_t"), sem("at_v")
        at_max, at_nm, at_exp, at_dve, at_pt_act, at_pt_dve = (
            sem("at_max"), sem("at_nm"), sem("at_exp"), sem("at_dve"), sem("at_pt_act"), sem("at_pt_dve"))
        at_hi, at_lo = sem("at_hi"), sem("at_lo")
        mg, m_hi, m_lo = sem("mg"), sem("m_hi"), sem("m_lo")
        d_sg, d_hid, d_hi, d_lo = sem("d_sg"), sem("d_hid"), sem("d_hi"), sem("d_lo")
        p_turned, p_hi, p_lo = sem("p_turned"), sem("p_hi"), sem("p_lo")
        pl_sig, pl_prod = sem("pl_sig"), sem("pl_prod")
        rout_zeroed, r_split, r_log, r_copied, r_turned, r_step, r_exp, r_rank = (
            sem("rout_zeroed"), sem("r_split"), sem("r_log"), sem("r_copied"), sem("r_turned"), sem("r_step"),
            sem("r_exp"), sem("r_rank"))
        sweeps_ready = sem("sweeps_ready")
        gfull_loaded, xn_scaled = sem("gfull_loaded"), sem("xn_scaled")
        e_rank, e_sel, e_gath, e_slots, e_xhi, e_xlo = (
            sem("e_rank"), sem("e_sel"), sem("e_gath"), sem("e_slots"), sem("e_xhi"), sem("e_xlo"))
        e_sg, e_hid, e_turn, e_thi, e_tlo = sem("e_sg"), sem("e_hid"), sem("e_turn"), sem("e_thi"), sem("e_tlo")
        e_yhi, e_ylo, e_scat, e_acc = sem("e_yhi"), sem("e_ylo"), sem("e_scat"), sem("e_acc")
        stored = sem("stored")

        HD_D, HD_L = 29, 73
        HA_D, HA_L = 8, 19
        HP_D, HP_L = 6, 14

        def hdve(i, d, k):
            return HD_L * i + HD_D * d + k

        def hact(i, d, k):
            return HA_L * i + HA_D * d + k

        def hpe(i, d, k):
            return HP_L * i + HP_D * d + k

        def time_order(ap):
            return ap.rearrange("p (f i r) -> p f r i", f=4, r=4)

        def token_order(ap):
            return ap.rearrange("p (f r i) -> p f r i", f=4, r=4)

        def chunked(ap, n=16):
            return ap.rearrange("p (c t) -> p c t", c=n)

        def h_turned(m, k):
            b = (2048, 0, (0, 512, -512, 0)[k // 2])[m]
            return ps[:, b + S * k:b + S * k + S]

        def y_done(eng, n, t, turns, k):
            if t:
                unit_done(eng, turns, k)
            else:
                eng.wait_ge(y0_done, n - n // 4 + 1)

        def y_mixer(t):
            return ps[:, 2048 + DM * t:2048 + DM * t + DM]

        def y_dense(t):
            return ps[:, DM * t:DM * t + DM]

        def y_experts(t):
            return yacc[:, DM * t:DM * t + DM]

        def y_ple(t):
            return eprod[:, DM * t:DM * t + DM]

        def unit_w(w, k):
            return w[:, k % NSPL, :].rearrange("p (k n) -> p k n", k=4)

        def unit_done(eng, turns, k):
            eng.wait_ge(part_used, turns * (RING * PARTS) + PARTS * (k + 1))

        def fill_unit(f):
            return 2 * f + 1 if f < NCHK else U_GATE + 3 * ((f - NCHK) // 2) + 1 + (f - NCHK) % 2

        block = ctx.enter_context(nc.Block())

        @block.sync
        def _(sp):
            def load(turns, k, src):
                if not (isinstance(turns, int) and turns * RING + k < RING):
                    sp.wait_ge(lo_ready, turns * (RING * PARTS) + PARTS * (k - RING + 1))
                sp.dma_start(raw[:, k % RING, :].rearrange("p (k n) -> p k n", n=src.shape[-1]), src)\
                  .then_inc(raw_loaded[k % RING], 16)

            def parameters():
                rows = arena[0:R_END, 2048:2048 + P]
                for r0, name, pat in ((R_MIX, "g_mix_pre", "i (k p) -> (i k) p"),
                                      (R_FFN, "g_ffn_pre", "i (k p) -> (i k) p"),
                                      (R_PLE, "ple_g_in", "i (k p) -> (i k) p"),
                                      (R_CONV, "conv_w", "i w (k p) -> (i w k) p"),
                                      (R_LB, "hgrn_lb_logits", "s i (k p) -> (s i k) p"),
                                      (R_NG, "hgrn_norm_g", "i (k p) -> (i k) p")):
                    src = io[name].rearrange(pat, p=P)
                    sp.dma_start(rows[r0:r0 + src.shape[0], :], src).then_inc(const_loaded, 16)

            def tables():
                sp.dma_start(cst[:, C_ONE:C_END], io["const"][:, C_ONE:C_END]).then_inc(tables_loaded, 16)
                sp.dma_start(maskb[:, :, :], io["maskb"]).then_inc(tables_loaded, 16)
                sp.dma_start(identb[:, :], io["identb"]).then_inc(tables_loaded, 16)
                sp.dma_start(arena[0:ROT, 3072:3072 + S].bitcast(I32),
                             io["positions"].partition_broadcast(ROT).rearrange("p a s -> p (a s)"))\
                  .then_inc(tables_loaded, 16)

            def tile4(w, r0, c0):
                return w[r0:r0 + 512, c0:c0 + UC].rearrange("(k p) n -> p k n", p=P)

            def mixer(i, k):
                for _, blk, _ in CHUNKS:
                    for kh in range(2):
                        load(0, k, tile4(io["w_in"][i], 512 * kh, UC * blk))
                        if k == 0:
                            parameters()
                        if k == 1:
                            tables()
                        k += 1
                for n in BRANCH_ORDER:
                    for j in range(2):
                        for kh in range(2):
                            load(0, k, tile4(io["w_in"][i], 512 * kh, UC * (17 + 2 * n + j)))
                            k += 1
                        load(0, k, tile4(io["w_branch"][i, n], 0, UC * j))
                        k += 1
                for kh in range(2):
                    for j in range(2):
                        load(0, k, tile4(io["w_out"][i], 512 * kh, UC * j))
                        k += 1
                return k

            def dense(k):
                wg, wu, wd = io["dense_w_gate"][0], io["dense_w_up"][0], io["dense_w_down"][0]
                for w in (wg, wu):
                    for kh in range(2):
                        load(0, k, tile4(w, 512 * kh, 0))
                        k += 1
                turn0, k0 = k // RING, k % RING
                with sp.Fori(1, NFC) as c:
                    turns = c + (turn0 - 1)
                    kk = k0
                    for kh in range(2):
                        load(turns, kk, wg[512 * kh:512 * kh + 512, bass.ds(c * UC, UC)]
                             .rearrange("(k p) n -> p k n", p=P))
                        kk += 1
                    for j in range(2):
                        load(turns, kk, wd[bass.ds((c - 1) * UC, 512), UC * j:UC * j + UC]
                             .rearrange("(k p) n -> p k n", p=P))
                        kk += 1
                    for kh in range(2):
                        load(turns, kk, wu[512 * kh:512 * kh + 512, bass.ds(c * UC, UC)]
                             .rearrange("(k p) n -> p k n", p=P))
                        kk += 1
                k += 6 * (NFC - 1)
                f0 = NFC * UC
                load(0, k, wg[:, f0:FD].rearrange("(k p) n -> p k n", p=P))
                load(0, k + 1, wu[:, f0:FD].rearrange("(k p) n -> p k n", p=P))
                load(0, k + 2, tile4(wd, f0 - UC, 0))
                load(0, k + 3, tile4(wd, f0 - UC, UC))
                load(0, k + 4, wd[f0:FD, :].rearrange("(k p) n -> p k n", p=P))
                return k + 5

            def ple(i, turns, k):
                load(turns, k, io["ple_w_proj"][i].rearrange("(k p) n -> p k n", p=P))
                for j in range(2):
                    for kh in range(2):
                        k += 1
                        load(turns, k, tile4(io["ple_w_gate"][i], 512 * kh, UC * j))
                return k + 1

            for r in range(4):
                sp.dma_start(x[64 * (r % 2):64 * (r % 2) + 64, r // 2, :],
                             io["x"][0].rearrange("(i r) d -> r i d", r=4)[r]).then_inc(x_loaded[r // 2], 16)
            sp.dma_start(cst[:, 0:C_ONE], io["const"][:, 0:C_ONE]).then_inc(ident_loaded, 16)
            k = mixer(0, 0)
            k = dense(k)
            k = ple(0, 0, k)
            k = mixer(1, k)
            turn0, k0 = k // RING, k % RING

            def sweep(s):
                with sp.Fori(0, NE) as e:
                    turns = e * TURNS_EXP + (s * (NE * TURNS_EXP) + turn0)
                    wg, wu, wd = (io[w][0, bass.ds(e, 1)] for w in ("moe_w_gate", "moe_w_up", "moe_w_down"))

                    def up(w, kk, c, kh):
                        load(turns, kk, w[:, 512 * kh:512 * kh + 512, UC * c:UC * c + UC]
                             .rearrange("a (k p) n -> p (a k) n", p=P))

                    def down(kk, c):
                        for j in range(2):
                            load(turns, kk + j, wd[:, UC * c:UC * c + 512, UC * j:UC * j + UC]
                                 .rearrange("a (k p) n -> p (a k) n", p=P))

                    kk = k0
                    for c in range(NEC):
                        for w in (wg, wu):
                            for kh in range(2):
                                up(w, kk, c, kh)
                                kk += 1
                        if c:
                            down(kk, c - 1)
                            kk += 2
                    down(kk, NEC - 1)

            sweep(0)
            sp.wait_ge(sweeps_ready, 1)
            sweeps = sp.value_load(nsw_i[0:1, 0:1], min_val=1, max_val=2)
            with sp.If(sweeps > 1):
                sweep(1)
            ple(1, sweeps * (NE * TURNS_EXP) + turn0, k0)
            for r in range(4):
                sp.wait_ge(x_ready, 2 * 5 + r // 2 + 1)
                sp.dma_start(out[0].rearrange("(i r) d -> r i d", r=4)[r],
                             x[64 * (r % 2):64 * (r % 2) + 64, r // 2, :]).then_inc(stored, 16)
            sp.wait_ge(stored, 64)

        @block.scalar
        def _(act):
            def split(turns, k, parts=range(PARTS)):
                act.wait_ge(raw_loaded[k % RING], (turns + (k // RING + 1)) * 16)
                for h in parts:
                    if not (isinstance(turns, int) and turns * RING + k < NSPL):
                        act.wait_ge(part_used, turns * (RING * PARTS) + PARTS * (k - NSPL) + h + 1)
                    cols = slice(PC * h, PC * h + PC)
                    act.activation(w_hi[:, k % NSPL, cols], raw[:, k % RING, cols], ACT.Copy).then_inc(hi_ready, 1)

            def pre_norm(i, m):
                n = 3 * i + m
                for t in range(NT):
                    if n:
                        act.wait_ge(x_ready, 2 * (n - 1) + t + 1)
                        act.wait_ge(post_ssq, NT * n)
                    else:
                        act.wait_ge(x_loaded[t], 32)
                    if n or t:
                        act.wait_ge(ssq, NT * n + t)
                    act.activation(junk, x[:, t, :], ACT.Square,
                                   accum_out=small[:, t:t + 1]).then_inc(ssq, 1)
                if m:
                    gain_load(i, m)

            def gain_load(i, m):
                src = io[("g_mix_post", "g_ffn_post", "ple_g_post")[m]][i:i + 1, :]
                act.dma_start(gb, src.to_broadcast([P, DM]))\
                   .then_inc(gb_loaded, 16)

            def pre_norm_hi(i, m):
                n = 3 * i + m
                act.wait_ge(prm_ready, 1)
                for k in range(KT):
                    g = prm[:, (R_MIX, R_FFN, R_PLE)[m] + KT * i + k:][:, 0:1]
                    act.wait_ge(turned, 4 * n + k // 2 + 1)
                    act.activation(hT_hi[:, k, :], h_turned(m, k), ACT.Identity, scale=g)\
                       .then_inc(hT_hi_ready, 1)

            def post_norm(n, ys, ready=None):
                for t in range(NT):
                    if ready:
                        ready(t)
                    if n or t:
                        act.wait_ge(post_ssq, NT * n + t)
                    act.activation(junk, ys(t), ACT.Square, accum_out=small[:, 4 + t:5 + t])\
                       .then_inc(post_ssq, 1)

            def h_vec(i, d, step):
                z = B["zf" if d == 0 else "zb"]
                if step == 0:
                    act.wait_ge(evac_act, 23 * i + 2 + 1)
                    if d:
                        act.wait_ge(h_pe, hpe(i, 0, 6))
                        act.wait_ge(h_dve, hdve(i, 0, 29))
                    act.activation(hL, z, ACT.Sigmoid).then_inc(h_act, 1)
                    act.wait_ge(h_act, hact(i, d, 1))
                    act.activation(z, z, ACT.Sigmoid, scale=-1.0).then_inc(h_act, 1)
                if step == 1:
                    act.wait_ge(h_dve, hdve(i, d, 4))
                    act.activation(hL, hL, ACT.Ln).then_inc(h_act, 1)
                if step == 2:
                    act.wait_ge(h_dve, hdve(i, d, 8))
                    act.activation(h1, hL, ACT.Exp).then_inc(h_act, 1)
                    act.wait_ge(h_act, hact(i, d, 4))
                    act.activation(hL, hL, ACT.Exp, scale=-1.0).then_inc(h_act, 1)
                if step == 3:
                    act.activation(h2, h2, ACT.Exp).then_inc(h_act, 1)
                    act.activation(hC, hC, ACT.Exp).then_inc(h_act, 1)
                if step == 4:
                    act.wait_ge(h_pe, hpe(i, d, 2))
                    act.activation(kdT, ps[:, 2048:3072], ACT.Copy).then_inc(h_act, 1)

            def h_post(i, step):
                if step == 0:
                    act.wait_ge(h_pe, hpe(i, 2, 0))
                    act.wait_ge(h_dve, hdve(i, 2, 0))
                    act.activation(h1, ps[:, 512 * 6:512 * 8], ACT.Copy).then_inc(h_act, 1)
                    act.activation(hL, ps[:, 512 * 6:512 * 8], ACT.Square).then_inc(h_act, 1)
                else:
                    act.wait_ge(h_dve, hdve(i, 2, 14))
                    act.activation(token_order(br_hi[:, 1, :]), time_order(h2), ACT.Copy).then_inc(h_act, 1)

            def mixer(i):
                base = U_L0 * i
                pre_norm(i, 0)
                for k in range(LEAD):
                    if i == 0:
                        split(0, base + k)
                pre_norm_hi(i, 0)
                for u in range(U_MIX):
                    split(0, base + u + LEAD)
                    if i == 0 and u == 2:
                        preamble_tables()
                    if u in ACT_H:
                        h_vec(i, *ACT_H[u])
                    if u == U_INP:
                        act.wait_ge(inp_turned, i + 1)
                        act.activation(B["inp"], ps[:, 2048:3072], ACT.Copy).then_inc(inp_ready, 1)
                    if u == U_CONV + 4:
                        act.wait_ge(conv_step, 15 * i + 14)
                        act.activation(token_order(br_hi[:, 2, :]), time_order(conv["cc"]), ACT.Copy)\
                           .then_inc(conv_hi, 1)
                    if u in ACT_POST:
                        h_post(i, ACT_POST[u])
                    if U_ATT <= u < U_ATT + 9:
                        attend(i, u - U_ATT)
                    if u == U_ATT + 10:
                        p_load(i)
                    if u < U_GATE and u % 2 == 1:
                        c = u // 2
                        name = CHUNKS[c][0]
                        unit_done(act, 0, base + u)
                        if name in ("aq2", "ak2", "av2"):
                            act.wait_ge(conv_hi, i + 1)
                            act.wait_ge(conv_step, 15 * (i + 1))
                        if name == "inp" and i:
                            act.wait_ge(h_dve, hdve(i - 1, 2, 13))
                        dst, src = DEST[name], ps[:, 1024 * (c % 2):1024 * (c % 2) + 1024]
                        if name in IN_TIME:
                            dst, src = time_order(dst), token_order(src)
                        act.activation(dst, src, ACT.Silu if name == "gate" else ACT.Copy).then_inc(evac_act, 1)
                        if name in ROPED:
                            swap_halves(i, ROPED.index(name))
                    if U_GATE <= u < U_OUT and (u - U_GATE) % 3 == 1:
                        m = (u - U_GATE) // 3
                        f = NCHK + 2 * m
                        unit_done(act, 0, base + u)
                        if m:
                            act.wait_ge(evac_dve, 6 * i + m)
                        else:
                            act.wait_ge(h_dve, hdve(i, 1, 20))
                        act.activation(gtile, ps[:, 1024 * (f % 2):1024 * (f % 2) + 1024], ACT.Sigmoid)\
                           .then_inc(evac_act, 1)
                    if u == U_ATT + 9:
                        act.wait_ge(h_pe, hpe(i, 2, 0))
                        gain_load(i, 0)
                    if u in (U_OUT - 2, U_OUT):
                        j = int(u == U_OUT)
                        act.wait_ge(mg, 4 * i + 3 + j)
                        act.activation(br_hi[:, 1 + j, :], merged[:, 1024 * j:1024 * j + 1024], ACT.Copy)\
                           .then_inc(m_hi, 1)

            def swap_halves(i, r):
                n, a = 6 * i + r, A[ROPED[r]]
                act.wait_ge(evac_act, 23 * i + CIDX[ROPED[r]] + 1)
                if r:
                    act.wait_ge(rope_done, n)
                else:
                    act.wait_ge(h_dve, hdve(i, 0, 18))
                half = ROT // 2
                for p in range(2):
                    act.dma_start(swapped[half * p:half * p + half, :], a[half * (1 - p):half * (2 - p), :])\
                       .then_inc(half_swapped, 16)

            def attend(i, g):
                h, odd = g // 2, g % 2
                if not odd and h >= 1:
                    hh = h - 1
                    act.wait_ge(at_v, NH * i + hh + 1)
                    act.activation(br_hi[:, 0, S * hh:S * hh + S], ps[:, 3072:3072 + S], ACT.Copy)\
                       .then_inc(at_hi, 1)
                if not odd and h < NH:
                    for q in range(2):
                        act.wait_ge(at_nm, NH * i + h + 1)
                        act.activation(aP[:, 512 * q:512 * q + 512], bank(4 + q), ACT.Exp, scale=SCALE,
                                       bias=small[:, 16 + q:17 + q], accum_out=small[:, 18 + q:19 + q])\
                           .then_inc(at_exp, 1)
                if odd:
                    act.wait_ge(at_t, 2 * (NH * i + h) + 1)
                    act.activation(aPT[:, 0:512], bank(6), ACT.Copy).then_inc(at_pt_act, 1)

            def preamble_tables():
                act.wait_ge(pre, PRE_ANGLES)
                act.activation(small[:, 64:80], small[:, 48:64], ACT.Exp).then_inc(pre_act, 1)
                act.activation(rc[:, 0, :], rc[:, 0, :], ACT.Sin).then_inc(pre_act, 1)
                act.activation(rc[:, 1, :], rc[:, 1, :], ACT.Sin).then_inc(pre_act, 1)

            def p_load(i):
                act.wait_ge(at_v, NH * (i + 1))
                for r in range(4):
                    act.dma_start(ptok[64 * (r % 2):64 * (r % 2) + 64, PLE * (r // 2):PLE * (r // 2) + PLE],
                                  io["p"][i, 0].rearrange("(i r) c -> r i c", r=4)[r]).then_inc(p_loaded, 16)

            def p_split(i):
                act.wait_ge(p_turned, i + 1)
                act.activation(br_hi[:, 2, 0:512], bank(7), ACT.Copy).then_inc(p_hi, 1)

            def dense(base):
                k = base + LEAD

                def gate(turns, kk, c, n=1024):
                    unit_done(act, turns, kk)
                    act.wait_ge(d_lo, c)
                    act.activation(dsg[:, 0:n], ps[:, 512 * 4:512 * 4 + n], ACT.Silu).then_inc(d_sg, 1)

                def hidden(c, n=1024, b=0):
                    act.wait_ge(d_hid, c + 1)
                    act.activation(br_hi[:, b, 0:n], dsg[:, 0:n], ACT.Copy).then_inc(d_hi, 1)

                for u in range(4):
                    split(0, k)
                    if u == 1:
                        gate(0, base + 1, 0)
                    if u == 3:
                        hidden(0)
                    k += 1
                turn0, k0 = k // RING, k % RING
                with act.Fori(1, NFC) as c:
                    turns = c + (turn0 - 1)
                    for u in range(6):
                        split(turns, k0 + u)
                        if u == 1:
                            gate(turns, k0 - LEAD + 1, c)
                        if u == 5:
                            hidden(c)
                k += 6 * (NFC - 1)
                for u in range(5):
                    split(0, k + u)
                    if u == 0:
                        gate(0, k - LEAD, NFC, 512)
                    if u == 1:
                        hidden(NFC, 512, 1)

            def gathered(it):
                act.wait_ge(e_gath, it + 1)
                act.activation(br_hi[:, 1, :], ps[:, 1024:2048], ACT.Copy).then_inc(e_xhi, 1)

            def experts(base):
                turn0, k0 = base // RING, base % RING
                split(0, base + 1)
                gathered(0)
                act.wait_ge(sweeps_ready, 1)
                sweeps = act.value_load(nsw_i[0:1, 0:1], min_val=1, max_val=2)
                with act.Fori(0, sweeps) as s:
                    with act.Fori(0, NE) as e:
                        it = s * NE + e
                        turns = it * TURNS_EXP + turn0

                        def turn(c):
                            act.wait_ge(e_turn, it * NEC + (c + 1 + ONE))
                            act.activation(br_hi[:, 0, 0:512], bank(6), ACT.Copy).then_inc(e_thi, 1)

                        for u in range(2, U_EXP):
                            split(turns, k0 + u)
                            c, step = divmod(u + 2, 6)
                            if step == 3 and c < NEC or u == 3:
                                c = 0 if u == 3 else c
                                unit_done(act, turns, k0 + (1 if u == 3 else u - 2))
                                if c:
                                    act.wait_ge(e_hid, it * NEC + c)
                                act.activation(msg, bank(4), ACT.Silu).then_inc(e_sg, 1)
                                if c:
                                    turn(c - 1)
                        turn(NEC - 1)
                        gathered(it + 1)
                        split(turns, k0 + U_EXP)
                        split(turns, k0 + U_EXP + 1, [0])
                        unit_done(act, turns, k0 + U_EXP - 1)
                        act.wait_ge(e_slots, it + 1)
                        act.activation(ye_hi, ps[:, 0:1024], ACT.Identity, scale=cslot).then_inc(e_yhi, 1)
                        split(turns, k0 + U_EXP + 1, [1])
                return sweeps

            def ple(i, turns, k):
                for u in range(2, U_PLE) if i == DEPTH - 1 else range(2, U_PLE + LEAD):
                    split(turns, k + u)
                for t in range(NT):
                    y_done(act, 3 * i + 2, t, turns, k + U_PLE - 1)
                    act.activation(sig[:, DM * t:DM * t + DM], y_dense(t), ACT.Sigmoid).then_inc(pl_sig, 1)
                post_norm(3 * i + 2, y_ple, lambda t: act.wait_ge(pl_prod, 2 * i + t + 1))

            mixer(0)
            post_norm(0, y_mixer, lambda t: y_done(act, 0, t, 0, U_MIX - 1))
            pre_norm(0, 1)
            p_split(0)
            pre_norm_hi(0, 1)
            dense(U_MIX)
            post_norm(1, y_dense, lambda t: y_done(act, 1, t, 0, U_MIX + U_DENSE - 1))
            pre_norm(0, 2)
            split(0, U_MIX + U_DENSE + LEAD)
            pre_norm_hi(0, 2)
            ple(0, 0, U_MIX + U_DENSE)
            mixer(1)
            act.wait_ge(rout_zeroed, 1)
            act.dma_start(rout.rearrange("p (k e) -> p k e", k=KT)[:, :, 0:NE],
                          io["moe_router"][0].rearrange("(k p) e -> p k e", p=P)).then_inc(rout_loaded, 16)
            act.dma_start(gfull, io["g_ffn_pre"][1:2, :].to_broadcast([P, DM])).then_inc(gfull_loaded, 16)
            post_norm(3, y_mixer, lambda t: y_done(act, 3, t, 0, U_L0 + U_MIX - 1))
            pre_norm(1, 1)
            act.wait_ge(rout_loaded, 16)
            act.activation(r_hi, rout, ACT.Copy).then_inc(r_split, 1)
            p_split(1)
            pre_norm_hi(1, 1)
            act.wait_ge(r_step, R_DIFF)
            act.activation(rt[:, RT_EX:RT_EX + 16], rt[:, RT_DF:RT_DF + 16], ACT.Exp).then_inc(r_exp, 1)
            sweeps = experts(U_L0 + U_MIX)
            post_norm(4, y_experts, lambda t: act.wait_ge(e_acc, sweeps * (NE * 2) + (2 + t)))
            pre_norm(1, 2)
            pre_norm_hi(1, 2)
            k = U_L0 + U_MIX
            ple(1, sweeps * (NE * TURNS_EXP) + k // RING, k % RING)

        @block.vector
        def _(dve):
            def split(turns, k, parts=range(PARTS)):
                for h in parts:
                    dve.wait_ge(hi_ready, turns * (RING * PARTS) + PARTS * k + h + 1)
                    cols = slice(PC * h, PC * h + PC)
                    dve.tensor_tensor(w_lo[:, k % NSPL, cols], raw[:, k % RING, cols],
                                      w_hi[:, k % NSPL, cols].bitcast(F32), ALU.subtract).then_inc(lo_ready, 1)

            def pre_norm(i, m, meanwhile=None):
                n = 3 * i + m
                for t in range(NT):
                    dve.wait_ge(ssq, NT * n + t + 1)
                    dve.tensor_scalar(small[:, 2 + t:3 + t], small[:, t:t + 1], 1.0 / DM, EPS, ALU.mult, ALU.add)\
                       .then_inc(var_ready, 1)
                    dve.wait_ge(rstd_ready, NT * n + t + 1)
                    dve.tensor_scalar(xn[:, DM * t:DM * t + DM], x[:, t, :], small[:, 8 + t:9 + t], None, ALU.mult)\
                       .then_inc(xn_ready, 1)
                if meanwhile:
                    meanwhile()
                for k in range(KT):
                    g = prm[:, (R_MIX, R_FFN, R_PLE)[m] + KT * i + k:][:, 0:1]
                    dve.wait_ge(hT_hi_ready, KT * n + 2 * (k // 2) + 2)
                    dve.scalar_tensor_tensor(out=hT_lo[:, k, :], in0=h_turned(m, k), scalar=g,
                                             in1=hT_hi[:, k, :].bitcast(F32), op0=ALU.mult, op1=ALU.subtract)\
                       .then_inc(hT_lo_ready, 1)

            def post_norm(n, ys):
                post_start(n)
                for t in range(NT):
                    variance(n, t)
                    gain(n, ys, t)
                    update(n, t)

            def post_norm_sb(n, ys, complete):
                post_start(n)
                complete(0)
                gain(n, ys, 0)
                complete(1)
                variance(n, 0)
                gain(n, ys, 1)
                variance(n, 1)
                update(n, 0)
                update(n, 1)

            def post_start(n):
                dve.wait_ge(gb_loaded, 16 * (n + 1))
                if n:
                    dve.wait_ge(x_ready, 2 * n)

            def variance(n, t):
                dve.wait_ge(post_ssq, NT * n + t + 1)
                dve.tensor_scalar(small[:, 6 + t:7 + t], small[:, 4 + t:5 + t], 1.0 / DM, EPS, ALU.mult, ALU.add)\
                   .then_inc(post_var, 1)

            def gain(n, ys, t):
                dve.tensor_tensor(gained[:, DM * t:DM * t + DM], ys(t), gb, ALU.mult).then_inc(post_gain, 1)

            def update(n, t):
                dve.wait_ge(post_gain, NT * n + t + 1)
                dve.wait_ge(post_rstd, NT * n + t + 1)
                dve.scalar_tensor_tensor(out=x[:, t, :], in0=gained[:, DM * t:DM * t + DM],
                                         scalar=small[:, 10 + t:11 + t], in1=x[:, t, :],
                                         op0=ALU.mult, op1=ALU.add).then_inc(x_ready, 1)

            def h_vec(i, d, step):
                z = B["zf" if d == 0 else "zb"]
                lbs = [lb[:, d, i, h:h + 1] for h in range(NH)]
                oms = [omlb[:, d, i, h:h + 1] for h in range(NH)]
                end, mid = (CH - 1, CH // 2 - 1) if d == 0 else (0, CH // 2)
                if step == 0:
                    dve.wait_ge(h_act, hact(i, d, 1))
                    for h in range(NH):
                        a = hL[:, S * h:S * h + S]
                        dve.tensor_scalar(a, a, oms[h], lbs[h], ALU.mult, ALU.add).then_inc(h_dve, 1)
                if step == 1:
                    dve.wait_ge(h_act, hact(i, d, 3))
                    for r in range(2):
                        a, c = hL[:, 512 * r:512 * r + 512], hC[:, 512 * r:512 * r + 512]
                        if d:
                            a, c = a[:, ::-1], c[:, ::-1]
                        dve.tensor_tensor_scan(out=c, data0=scan_keep, data1=a, initial=0.0,
                                               op0=ALU.mult, op1=ALU.add).then_inc(h_dve, 1)
                    dve.wait_ge(h_dve, hdve(i, d, 6))
                    cv = chunked(hC)
                    dve.tensor_tensor(chunked(hL), cv, cv[:, :, mid:mid + 1].to_broadcast([P, 16, CH]),
                                      ALU.subtract).then_inc(h_dve, 1)
                    dve.tensor_tensor(chunked(h2), cv[:, :, end:end + 1].to_broadcast([P, 16, CH]), cv,
                                      ALU.subtract).then_inc(h_dve, 1)
                if step == 2:
                    dve.wait_ge(evac_act, 23 * i + CIDX["q"] + 1)
                    dve.wait_ge(h_act, hact(i, d, 4))
                    dve.tensor_tensor(h1, h1, B["q"], ALU.mult).then_inc(h_dve, 1)
                    dve.wait_ge(h_act, hact(i, d, 5))
                    for h in range(NH):
                        a = hL[:, S * h:S * h + S]
                        dve.scalar_tensor_tensor(out=a, in0=z[:, S * h:S * h + S], scalar=oms[h], in1=a,
                                                 op0=ALU.mult, op1=ALU.mult).then_inc(h_dve, 1)
                if step == 3:
                    dve.wait_ge(h_act, hact(i, d, 7))
                    dve.tensor_copy(small[:, 32:48].rearrange("p (c a) -> p c a", a=1),
                                    chunked(hC)[:, :, end:end + 1]).then_inc(h_dve, 1)
                    for h in range(NH):
                        a = h2[:, S * h:S * h + S]
                        dve.scalar_tensor_tensor(out=a, in0=z[:, S * h:S * h + S], scalar=oms[h], in1=a,
                                                 op0=ALU.mult, op1=ALU.mult).then_inc(h_dve, 1)
                if step == 4:
                    dve.wait_ge(h_dve, hdve(i, d, 14))
                    dve.tensor_tensor(hC, hC, B["q"], ALU.mult).then_inc(h_dve, 1)
                if step == 5:
                    dve.wait_ge(z_att, 2 * i + d + 1)
                    dve.wait_ge(h_pe, hpe(i, d, 1))
                    if d:
                        dve.wait_ge(h_dve, hdve(i, 1, 19))
                    dve.copy_predicated(attT.rearrange("p (c t) -> p c t", t=P),
                                        causal[d].rearrange("p (a t) -> p a t", a=1).to_broadcast([P, 8, P]),
                                        ps[:, 2048:3072].rearrange("p (c t) -> p c t", t=P)).then_inc(h_dve, 1)
                if step == 6:
                    dve.wait_ge(h_pe, hpe(i, d, 3))
                    dve.tensor_copy(hS, bank(4)).then_inc(h_dve, 1)
                if step in (7, 8):
                    c = step - 6
                    if d:
                        c = NCH - 1 - c
                    dve.wait_ge(h_pe, hpe(i, d, step - 3))
                    dve.wait_ge(h_dve, hdve(i, d, 21 + 4 * (step - 7)))
                    for h in range(NH):
                        a = hS[:, HD * h:HD * h + HD]
                        dve.scalar_tensor_tensor(out=a, in0=a, scalar=small[:, 32 + NCH * h + c:33 + NCH * h + c],
                                                 in1=ps[:, 2048 + HD * h:2048 + HD * h + HD],
                                                 op0=ALU.mult, op1=ALU.add).then_inc(h_dve, 1)

            def h_post(i, step):
                if step == 0:
                    dve.wait_ge(h_pe, hpe(i, 2, 1))
                    dve.tensor_scalar(small[:, 80:88], bank(4)[:, 0:8], 1.0 / HD, EPS, ALU.mult, ALU.add)\
                       .then_inc(h_dve, 1)
                    dve.wait_ge(h_pow, i + 1)
                    for j in range(8):
                        dve.tensor_scalar(hC[:, P * j:P * j + P], ident, small[:, 88 + j:89 + j], None, ALU.mult)\
                           .then_inc(h_dve, 1)
                if step == 1:
                    dve.wait_ge(h_pe, hpe(i, 2, 2))
                    dve.wait_ge(h_act, hact(i, 2, 1))
                    for h in range(NH):
                        dve.scalar_tensor_tensor(out=h2[:, S * h:S * h + S], in0=h1[:, S * h:S * h + S],
                                                 scalar=prm[:, R_NG + NH * i + h:R_NG + NH * i + h + 1],
                                                 in1=ps[:, 2048 + S * h:2048 + S * h + S],
                                                 op0=ALU.mult, op1=ALU.mult).then_inc(h_dve, 1)
                    dve.wait_ge(h_dve, hdve(i, 2, 13))
                    dve.wait_ge(evac_act, 23 * i + CIDX["gate"] + 1)
                    dve.tensor_tensor(h2, h2, B["gate"], ALU.mult).then_inc(h_dve, 1)
                    dve.wait_ge(h_act, hact(i, 2, 3))
                    dve.wait_ge(h_dve, hdve(i, 2, 14))
                    dve.tensor_tensor(token_order(br_lo[:, 1, :]), time_order(h2),
                                      token_order(br_hi[:, 1, :].bitcast(F32)), ALU.subtract)\
                       .then_inc(h_dve, 1)

            def convolve(i, step):
                cu, cb, cc = conv["cu"], conv["cb"], conv["cc"]
                n0 = 15 * i
                taps = [[prm[:, R_CONV + 12 * i + 4 * w + f:][:, 0:1] for w in range(3)] for f in range(4)]
                if step == 0:
                    dve.wait_ge(evac_act, 23 * i + CIDX["cc"] + 1)
                    dve.tensor_tensor(cu, cu, cc, ALU.mult).then_inc(conv_step, 1)
                    dve.wait_ge(conv_step, n0 + 1)
                    for f in range(4):
                        dve.tensor_scalar(cc[:, S * f:S * f + S], cu[:, S * f:S * f + S], taps[f][1], None, ALU.mult)\
                           .then_inc(conv_step, 1)
                for f in range(4):
                    y, s = cc[:, S * f:S * f + S], cu[:, S * f:S * f + S]
                    if step == 1:
                        dve.wait_ge(conv_step, n0 + 2 + f)
                        dve.scalar_tensor_tensor(out=y[:, 1:S], in0=s[:, 0:S - 1], scalar=taps[f][0], in1=y[:, 1:S],
                                                 op0=ALU.mult, op1=ALU.add).then_inc(conv_step, 1)
                    if step == 2:
                        dve.wait_ge(conv_step, n0 + 6 + f)
                        dve.scalar_tensor_tensor(out=y[:, 0:S - 1], in0=s[:, 1:S], scalar=taps[f][2],
                                                 in1=y[:, 0:S - 1], op0=ALU.mult, op1=ALU.add).then_inc(conv_step, 1)
                if step == 3:
                    dve.wait_ge(conv_step, n0 + 13)
                    dve.tensor_tensor(cc, cc, cb, ALU.mult).then_inc(conv_step, 1)

            def conv_lo(i):
                dve.wait_ge(conv_hi, i + 1)
                dve.wait_ge(conv_step, 15 * i + 14)
                dve.tensor_tensor(token_order(br_lo[:, 2, :]), time_order(conv["cc"]),
                                  token_order(br_hi[:, 2, :].bitcast(F32)), ALU.subtract)\
                   .then_inc(conv_step, 1)

            def attend(i, g):
                h, odd = g // 2, g % 2
                nh = NH * i + h
                if not odd and h >= 1:
                    hh = h - 1
                    dve.wait_ge(at_hi, NH * i + hh + 1)
                    dve.tensor_tensor(br_lo[:, 0, S * hh:S * hh + S], ps[:, 3072:3072 + S],
                                      br_hi[:, 0, S * hh:S * hh + S].bitcast(F32), ALU.subtract).then_inc(at_lo, 1)
                if not odd and h < NH:
                    dve.wait_ge(at_s, nh + 1)
                    if nh:
                        dve.wait_ge(at_exp, 2 * nh)
                    dve.tensor_reduce(small[:, 20:22], ps[:, 2048:3072].rearrange("p (q k) -> p q k", q=2),
                                      AX.X, ALU.max).then_inc(at_max, 1)
                    dve.wait_ge(at_max, nh + 1)
                    dve.tensor_scalar(small[:, 16:18], small[:, 20:22], -SCALE, None, ALU.mult).then_inc(at_nm, 1)
                    dve.wait_ge(at_exp, 2 * (nh + 1))
                    dve.reciprocal(small[:, 22:24], small[:, 18:20]).then_inc(at_dve, 1)
                    dve.wait_ge(at_dve, 3 * nh + 1)
                    if nh:
                        dve.wait_ge(at_t, 2 * nh)
                    for q in range(2):
                        dve.tensor_scalar(adiag[:, P * q:P * q + P], ident, small[:, 22 + q:23 + q], None, ALU.mult)\
                           .then_inc(at_dve, 1)
                if odd:
                    dve.wait_ge(at_t, 2 * nh + 2)
                    dve.tensor_copy(aPT[:, 512:1024], bank(7)).then_inc(at_pt_dve, 1)

            def merge(i, m):
                n, j = m // 2, m % 2
                f = NCHK + 2 * m + 1
                a = merged[:, 1024 * j:1024 * j + 1024]
                unit_done(dve, 0, U_L0 * i + fill_unit(f))
                dve.wait_ge(evac_act, 23 * i + NCHK + m + 1)
                if m > 2:
                    dve.wait_ge(mg, 4 * i + m - 2)
                src = ps[:, 1024 * (f % 2):1024 * (f % 2) + 1024]
                if m == 0:
                    dve.wait_ge(rope_done, 6 * (i + 1))
                if n == 0:
                    dve.tensor_tensor(a, gtile, src, ALU.mult).then_inc(evac_dve, 1)
                else:
                    dve.tensor_tensor(utmp, gtile, src, ALU.mult).then_inc(evac_dve, 1)
                    dve.wait_ge(evac_dve, 6 * i + m + 1)
                    dve.tensor_tensor(a, a, utmp, ALU.add).then_inc(mg, 1)

            def mixer(i):
                base = U_L0 * i
                pre_norm(i, 0, parameters if i == 0 else None)
                for u in range(U_MIX):
                    split(0, base + u + LEAD)
                    if i == 0 and u in (1, 3):
                        preamble(u)
                    for d, step in DVE_H.get(u, ()):
                        h_vec(i, d, step)
                    if U_CONV <= u < U_CONV + 4:
                        convolve(i, u - U_CONV)
                    if u == U_CONV + 4:
                        conv_lo(i)
                    if u in DVE_POST:
                        h_post(i, DVE_POST[u])
                    if U_ATT <= u < U_ATT + 9:
                        attend(i, u - U_ATT)
                    if u >= U_GATE + 3 and (u - U_GATE) % 3 == 0 and u < U_OUT + 1:
                        m = (u - U_GATE) // 3 - 1
                        merge(i, m)
                    if u in (U_OUT - 2, U_OUT):
                        j = int(u == U_OUT)
                        dve.wait_ge(m_hi, 2 * i + j + 1)
                        dve.tensor_tensor(br_lo[:, 1 + j, :], merged[:, 1024 * j:1024 * j + 1024],
                                          br_hi[:, 1 + j, :].bitcast(F32), ALU.subtract).then_inc(m_lo, 1)

            def parameters():
                dve.wait_ge(prm_turned, 1)
                dve.tensor_copy(prm[:, :], bank(0)[:, 0:R_END]).then_inc(prm_ready, 1)
                for k in range(LEAD):
                    split(0, k)

            preamble_steps = [0]

            def preamble(u):

                def step(ins):
                    preamble_steps[0] += 1
                    ins.then_inc(pre, 1)
                    dve.wait_ge(pre, preamble_steps[0])

                lg = prm[:, R_LB:R_LB + 16].rearrange("p (s i k) -> p s i k", s=2, i=DEPTH)
                ex = small[:, 48:64].rearrange("p (s i k) -> p s i k", s=2, i=DEPTH)
                e2 = small[:, 64:80].rearrange("p (s i k) -> p s i k", s=2, i=DEPTH)
                mx = small[:, 24:32].rearrange("p (s a k) -> p s a k", s=2, a=1)
                if u == 1:
                    step(dve.tensor_tensor(mx, lg[:, :, 0:1, :], lg[:, :, 1:2, :], ALU.max))
                    for s in range(2):
                        step(dve.tensor_tensor(ex[:, s], lg[:, s], mx[:, s].to_broadcast([P, DEPTH, NH]), ALU.subtract))
                    dve.wait_ge(tables_loaded, 64)
                    pf = arena[0:ROT, 3584:3584 + S]
                    kr = arena[0:ROT, 3840:3840 + S]
                    step(dve.tensor_copy(pf.rearrange("p (r i) -> p r i", r=4),
                                         arena[0:ROT, 3072:3072 + S].bitcast(I32).rearrange("p (i r) -> p r i", r=4)))
                    step(dve.tensor_scalar(pf, pf, inv_freq, None, ALU.mult))
                    for w, (shift, turn) in enumerate(((HALF_PI, 0.25), (0.0, 0.0))):
                        r = rc[:, w, :]
                        step(dve.tensor_scalar(kr, pf, INV_2PI, turn, ALU.mult, ALU.add))
                        step(dve.tensor_scalar(kr, kr, ROUND, ROUND, ALU.add, ALU.subtract))
                        for part in range(3):
                            step(dve.scalar_tensor_tensor(out=r, in0=kr, scalar=-PI2[part], in1=r if part else pf,
                                                          op0=ALU.mult, op1=ALU.add))
                        step(dve.tensor_scalar(r, r, shift, PI_IN, ALU.add, ALU.min))
                        step(dve.tensor_scalar(r, r, -PI_IN, None, ALU.max))
                    assert preamble_steps[0] == PRE_ANGLES
                else:
                    dve.wait_ge(pre_act, 3)
                    step(dve.tensor_tensor(mx, e2[:, :, 0:1, :], e2[:, :, 1:2, :], ALU.add))
                    step(dve.reciprocal(mx, mx))
                    for s in range(2):
                        step(dve.tensor_tensor(e2[:, s], e2[:, s], mx[:, s].to_broadcast([P, DEPTH, NH]), ALU.mult))
                    step(dve.tensor_tensor(ex[:, :, 1:2, :], e2[:, :, 0:1, :], e2[:, :, 1:2, :], ALU.add))
                    step(dve.tensor_tensor(lb[:, :, 0:1, :], e2[:, :, 0:1, :], e2[:, :, 0:1, :], ALU.subtract))
                    step(dve.tensor_tensor(lb[:, :, 1:2, :], ex[:, :, 1:2, :], e2[:, :, 0:1, :], ALU.subtract))
                    step(dve.tensor_scalar(omlb[:, :, :, :], lb[:, :, :, :], -1.0, 1.0, ALU.mult, ALU.add))
                    step(dve.tensor_scalar(rc[:, 1, :], rc[:, 1, :], rot_sign, None, ALU.mult))
                    assert preamble_steps[0] == PRE_END

            def scale_tokens():
                dve.wait_ge(hT_hi_ready, 5 * KT)
                dve.wait_ge(gfull_loaded, 16)
                for t in range(NT):
                    a = xn[:, DM * t:DM * t + DM]
                    dve.tensor_tensor(a, a, gfull, ALU.mult).then_inc(xn_scaled, 1)

            def r_rest():
                dve.wait_ge(r_split, 1)
                dve.tensor_tensor(r_lo, rout, r_hi.bitcast(F32), ALU.subtract).then_inc(r_split, 1)
                p_split(1)

            def p_split(i):
                dve.wait_ge(p_hi, i + 1)
                dve.tensor_tensor(br_lo[:, 2, 0:512], bank(7), br_hi[:, 2, 0:512].bitcast(F32), ALU.subtract)\
                   .then_inc(p_lo, 1)

            def dense(base):
                k = base + LEAD

                def hidden(turns, kk, c, n=1024, b=0):
                    unit_done(dve, turns, kk)
                    dve.wait_ge(d_sg, c + 1)
                    dve.tensor_tensor(dsg[:, 0:n], dsg[:, 0:n], ps[:, 512 * 6:512 * 6 + n], ALU.mult)\
                       .then_inc(d_hid, 1)
                    dve.wait_ge(d_hi, c + 1)
                    dve.wait_ge(d_hid, c + 1)
                    dve.tensor_tensor(br_lo[:, b, 0:n], dsg[:, 0:n], br_hi[:, b, 0:n].bitcast(F32),
                                      ALU.subtract).then_inc(d_lo, 1)

                for u in range(4):
                    split(0, k)
                    k += 1
                hidden(0, base + 3, 0)
                turn0, k0 = k // RING, k % RING
                with dve.Fori(1, NFC) as c:
                    turns = c + (turn0 - 1)
                    for u in range(6):
                        split(turns, k0 + u)
                    hidden(turns, k0 - LEAD + 5, c)
                k += 6 * (NFC - 1)
                for u in range(5):
                    split(0, k + u)
                    if u == 1:
                        hidden(0, k - LEAD + 1, NFC, 512, 1)

            def route():
                n = 0

                def step(*ins):
                    nonlocal n
                    for one in ins:
                        n += 1
                        one.then_inc(r_step, 1)
                    dve.wait_ge(r_step, n)

                def tiles(c):
                    return [rt[:, c + NE * t:c + NE * t + NE] for t in range(NT)]

                step(dve.memset(rt[:, RT_TAB:RT_TAB + 4 * TAB], -1.0))
                dve.wait_ge(r_log, 1)
                dve.tensor_copy(logT, bank(4)[0:NE, 0:S]).then_inc(r_copied, 1)
                dve.wait_ge(r_turned, 1)
                step(dve.tensor_copy(rt[:, RT_LG:RT_LG + 16], bank(5)[:, 0:16]))
                lg, m8, i8, place = tiles(RT_LG), tiles(RT_M8), tiles(RT_I8), tiles(RT_PL)
                step(*[dve.max(out=m8[t], in_=lg[t]) for t in range(NT)])
                step(*[dve.max_index(out=i8[t].bitcast(U32), in_max=m8[t], in_values=lg[t]) for t in range(NT)])
                step(dve.tensor_copy(rt[:, RT_PL:RT_PL + 16], rt[:, RT_I8:RT_I8 + 16].bitcast(U32)))
                first, mask, diff = tiles(RT_OH), tiles(RT_M), tiles(RT_DF)
                step(*[dve.tensor_scalar(first[t], iota8, place[t][:, 0:1], None, ALU.is_equal) for t in range(NT)],
                     *[dve.tensor_scalar(diff[t], lg[t], m8[t][:, 0:1], None, ALU.subtract) for t in range(NT)])
                step(*[dve.scalar_tensor_tensor(out=mask[t], in0=iota8, scalar=place[t][:, 1:2], in1=first[t],
                                                op0=ALU.is_equal, op1=ALU.add) for t in range(NT)])
                assert n == R_DIFF
                dve.wait_ge(r_exp, 1)
                step(dve.tensor_tensor(rt[:, RT_CB:RT_CB + 16], rt[:, RT_EX:RT_EX + 16], rt[:, RT_M:RT_M + 16],
                                       ALU.mult))
                step(dve.tensor_reduce(rt[:, RT_PL:RT_PL + 2],
                                       rt[:, RT_CB:RT_CB + 16].rearrange("p (t e) -> p t e", t=NT),
                                       AX.X, ALU.add))
                step(dve.reciprocal(rt[:, RT_PL + 2:RT_PL + 4], rt[:, RT_PL:RT_PL + 2]))
                dve.wait_ge(r_rank, 1)
                re = rt[:, RT_RE:RT_RE + 16]
                step(dve.scalar_tensor_tensor(out=re, in0=bank(5)[:, 16:32], scalar=1.0, in1=rt[:, RT_M:RT_M + 16],
                                              op0=ALU.add, op1=ALU.mult))
                table = rt[:, RT_TAB:RT_TAB + 4 * TAB].rearrange("p (r c) -> p r c", r=4)
                both = re.rearrange("p (t e) -> p t e", t=NT)
                cb = tiles(RT_CB)
                step(*[dve.tensor_scalar(table[:, 0:2, NE * s:NE * s + NE], both, -1.0 - P * s, None, ALU.add)
                       for s in range(2)],
                     *[dve.tensor_scalar(table[:, 2 + t, NE * s:NE * s + NE], cb[t],
                                         rt[:, RT_PL + 2 + t:RT_PL + 3 + t], None, ALU.mult)
                       for s in range(2) for t in range(NT)])
                select(0)
                step(dve.tensor_reduce(rt[:, RT_PL:RT_PL + 1], bank(5)[:, 32:40], AX.X, ALU.max))
                step(dve.tensor_scalar(rt[:, RT_PL + 1:RT_PL + 2], rt[:, RT_PL:RT_PL + 1], float(P), 1.0, ALU.is_gt,
                                       ALU.add))
                dve.tensor_copy(nsw_i[:, :], rt[:, RT_PL + 1:RT_PL + 2]).then_inc(sweeps_ready, 1)

            def select(it):
                tab = rt[:, RT_TAB:RT_TAB + 4 * TAB].rearrange("p (r c) -> p r c", r=4)
                dve.tensor_copy(rk[:, :].rearrange("p (r a) -> p r a", a=1), tab[:, :, bass.ds(it, 1)])\
                   .then_inc(e_rank, 1)
                dve.wait_ge(e_rank, it + 1)
                for t in range(NT):
                    dve.tensor_scalar(sel[:, P * t:P * t + P], iota, rk[:, t:t + 1], None, ALU.is_equal)\
                       .then_inc(e_sel, 1)

            def gathered(it):
                dve.wait_ge(e_xhi, it + 1)
                dve.tensor_tensor(br_lo[:, 1, :], ps[:, 1024:2048], br_hi[:, 1, :].bitcast(F32), ALU.subtract)\
                   .then_inc(e_xlo, 1)

            def accumulate(it, t, b=2):
                dve.wait_ge(e_scat, it * 2 + (t + 1))
                dve.wait_ge(e_acc, it * 2 + (1 + t))
                a = yacc[:, DM * t:DM * t + DM]
                dve.tensor_tensor(a, a, bank(b, 1024), ALU.add).then_inc(e_acc, 1)

            def experts(base):
                turn0, k0 = base // RING, base % RING
                split(0, base + 1)
                gathered(0)
                dve.wait_ge(sweeps_ready, 1)
                sweeps = dve.value_load(nsw_i[0:1, 0:1], min_val=1, max_val=2)
                with dve.Fori(0, sweeps) as s:
                    with dve.Fori(0, NE) as e:
                        it = s * NE + e
                        turns = it * TURNS_EXP + turn0

                        def turn(c):
                            dve.wait_ge(e_thi, it * NEC + c + 1)
                            dve.tensor_tensor(br_lo[:, 0, 0:512], bank(6), br_hi[:, 0, 0:512].bitcast(F32),
                                              ALU.subtract).then_inc(e_tlo, 1)

                        def hidden(c):
                            dve.wait_ge(e_sg, it * NEC + c + 1)
                            unit_done(dve, turns, k0 + 6 * c + (1 if c else 3))
                            dve.wait_ge(e_turn, it * NEC + (c + ONE))
                            dve.tensor_tensor(hid, msg, bank(5), ALU.mult).then_inc(e_hid, 1)

                        for u in range(2, U_EXP):
                            split(turns, k0 + u)
                            if u == 3:
                                accumulate(it, 0)
                            if u == 5:
                                hidden(0)
                                accumulate(it, 1)
                                dve.tensor_copy(selct, bank(7)[:, 0:256])
                                dve.tensor_copy(cslot, bank(7)[:, 256:257]).then_inc(e_slots, 1)
                            c, step = divmod(u + 2, 6)
                            if step == 3 and 0 < c < NEC:
                                turn(c - 1)
                            if step == 5 and c:
                                hidden(c)
                            if step == 5 and c == 3:
                                select(it + 1)
                        turn(NEC - 1)
                        gathered(it + 1)
                        split(turns, k0 + U_EXP)
                        split(turns, k0 + U_EXP + 1, [0])
                        dve.wait_ge(e_yhi, it + 1)
                        dve.scalar_tensor_tensor(out=ye_lo, in0=ps[:, 0:1024], scalar=cslot, in1=ye_hi.bitcast(F32),
                                                 op0=ALU.mult, op1=ALU.subtract).then_inc(e_ylo, 1)
                        split(turns, k0 + U_EXP + 1, [1])
                return sweeps

            def ple(i, turns, k):
                for u in range(2, U_PLE) if i == DEPTH - 1 else range(2, U_PLE + LEAD):
                    split(turns, k + u)
                def product(t):
                    dve.wait_ge(pl_sig, 2 * i + t + 1)
                    dve.tensor_tensor(y_ple(t), sig[:, DM * t:DM * t + DM], ps[:, 2048 + DM * t:2048 + DM * t + DM],
                                      ALU.mult).then_inc(pl_prod, 1)
                    dve.wait_ge(pl_prod, 2 * i + t + 1)

                post_norm_sb(3 * i + 2, y_ple, product)

            mixer(0)
            post_norm(0, y_mixer)
            pre_norm(0, 1, lambda: p_split(0))
            dense(U_MIX)
            post_norm(1, y_dense)
            pre_norm(0, 2, lambda: split(0, U_MIX + U_DENSE + LEAD))
            ple(0, 0, U_MIX + U_DENSE)
            mixer(1)
            post_norm(3, y_mixer)
            pre_norm(1, 1, r_rest)
            scale_tokens()
            route()
            sweeps = experts(U_L0 + U_MIX)

            def last_sum(t):
                accumulate(sweeps * NE, t, 2 + 2 * t)
                dve.wait_ge(e_acc, sweeps * (NE * 2) + (2 + t))

            post_norm_sb(4, y_experts, last_sum)
            pre_norm(1, 2)
            k = U_L0 + U_MIX
            ple(1, sweeps * (NE * TURNS_EXP) + k // RING, k % RING)

        @block.gpsimd
        def _(pool):
            pool.memset(minus_half[:, :], -0.5).then_inc(half_ready, 1)
            pool.wait_ge(half_ready, 1)

            def root(src, dst, ready, count, done):
                pool.wait_ge(ready, count)
                pool.tensor_tensor(small[:, dst:dst + 1], small[:, src:src + 1], minus_half[:, 0:1], ALU.pow)\
                    .then_inc(done, 1)

            def rope(i, r):
                n = 6 * i + r
                qr = A[ROPED[r]][0:ROT, :].rearrange("p (h t) -> p h t", h=NH)
                sw = swapped.rearrange("p (h t) -> p h t", h=NH)
                cos = rc[:, 0:1, :].to_broadcast([ROT, NH, S])
                sin = rc[:, 1:2, :].to_broadcast([ROT, NH, S])
                pool.wait_ge(half_swapped, 32 * (n + 1))
                pool.tensor_tensor(sw, sw, sin, ALU.mult).then_inc(rope_step, 1)
                pool.tensor_tensor(qr, qr, cos, ALU.mult).then_inc(rope_step, 1)
                pool.wait_ge(rope_step, 2 * (n + 1))
                pool.tensor_tensor(qr, qr, sw, ALU.add).then_inc(rope_done, 1)

            for i in range(DEPTH):
                for m in range(3):
                    n = 3 * i + m
                    for t in range(NT):
                        root(2 + t, 8 + t, var_ready, NT * n + t + 1, rstd_ready)
                    if n == 4:
                        pool.memset(yacc, 0.0).then_inc(e_acc, 1)
                        pool.wait_ge(r_log, 1)
                        for a in (ye_hi, ye_lo, selct):
                            pool.memset(a.bitcast(F32), 0.0).then_inc(e_ylo, 1)
                    if m == 0:
                        for d in range(2):
                            if d:
                                pool.wait_ge(h_pe, hpe(i, 0, 3))
                            else:
                                pool.wait_ge(xn_ready, NT * (n + 1))
                            pool.memset(attT, 0.0).then_inc(z_att, 1)
                        if i == 0:
                            pool.wait_ge(pre, PRE_END)
                        for r in range(len(ROPED)):
                            rope(i, r)
                        pool.wait_ge(h_dve, hdve(i, 2, 1))
                        pool.tensor_tensor(small[:, 88:96], small[:, 80:88], minus_half[:, :], ALU.pow).then_inc(h_pow, 1)
                        if i == 1:
                            pool.wait_ge(at_v, NH * DEPTH)
                            pool.memset(rout, 0.0).then_inc(rout_zeroed, 1)
                    for t in range(NT):
                        root(6 + t, 10 + t, post_var, NT * n + t + 1, post_rstd)

        @block.tensor
        def _(pe):
            def mm3(o, l_hi, l_lo, r_hi_, r_lo_, start):
                pe.matmul(o, l_hi, r_hi_, start=start, stop=False, skip_group_check=True)
                pe.matmul(o, l_hi, r_lo_, start=False, stop=False, skip_group_check=True)
                return pe.matmul(o, l_lo, r_hi_, start=False, stop=True, skip_group_check=True)

            def take(turns, k, h):
                pe.wait_ge(lo_ready, turns * (RING * PARTS) + PARTS * k + h + 1)

            def feat_unit(turns, k, b0, kh, a_hi, a_lo, norm=None):
                wh, wl = unit_w(w_hi, k), unit_w(w_lo, k)
                for h in range(PARTS):
                    take(turns, k, h)
                    if norm is not None:
                        h_split(norm, 4 * kh + 2 * h + 2)
                    for f in range(4):
                        o = ps[:, 512 * b0 + S * f:512 * b0 + S * f + S]
                        for kk in (2 * h, 2 * h + 1):
                            ins = mm3(o, wh[:, kk, P * f:P * f + P], wl[:, kk, P * f:P * f + P],
                                      a_hi[:, 4 * kh + kk, :], a_lo[:, 4 * kh + kk, :],
                                      start=(kh == 0 and kk == 0 and f % 2 == 0))
                    ins.then_inc(part_used, 1)

            def last_tok_unit(turns, k, outs, a):
                wh, wl = unit_w(w_hi, k), unit_w(w_lo, k)
                for h in range(PARTS):
                    take(turns, k, h)
                for t, o in enumerate(outs):
                    for kk in range(4):
                        ah, al = a(t, 4 + kk)
                        ins = mm3(o, ah, al, wh[:, kk, :], wl[:, kk, :], start=False)
                    if t == 0:
                        ins.then_inc(y0_done, 1)
                ins.then_inc(part_used, PARTS)

            def tok_unit(turns, k, outs, kh, a, starts):
                wh, wl = unit_w(w_hi, k), unit_w(w_lo, k)
                for h in range(PARTS):
                    take(turns, k, h)
                    for t, o in enumerate(outs):
                        for kk in (2 * h, 2 * h + 1):
                            ah, al = a(t, 4 * kh + kk)
                            ins = mm3(o, ah, al, wh[:, kk, :], wl[:, kk, :], start=(starts and kk == 0))
                    ins.then_inc(part_used, 1)

            def merged_nat(t, k):
                b, c = 1 + k // 4, S * (k % 4) + P * t
                return br_hi[:, b, c:c + P], br_lo[:, b, c:c + P]

            def hT_nat(t, k):
                return hT_hi[:, k, P * t:P * t + P], hT_lo[:, k, P * t:P * t + P]

            def pre_norm(i, m):
                n = 3 * i + m
                for t in range(NT):
                    pe.wait_ge(xn_ready, NT * n + t + 1)
                    for k in range(KT):
                        ins = pe.transpose(h_turned(m, k)[:, P * t:P * t + P],
                                           xn[:, DM * t + P * k:DM * t + P * k + P], ident)
                        if t and k % 2:
                            ins.then_inc(turned, 1)

            def h_split(n, tiles=KT):
                pe.wait_ge(hT_lo_ready, KT * n + tiles)

            def fill_wait(i, f):
                f -= 2
                if f < 0:
                    return
                if f < NCHK:
                    pe.wait_ge(evac_act, 23 * i + f + 1)
                elif (f - NCHK) % 2 == 0:
                    pe.wait_ge(evac_act, 23 * i + NCHK + (f - NCHK) // 2 + 1)
                else:
                    pe.wait_ge(evac_dve, 6 * i + (f - NCHK) // 2 + 1)

            def h_step(i, d, step):
                chunks = range(NCH) if d == 0 else range(NCH - 1, -1, -1)
                v = B["inp"]

                def inter(c):
                    for h in range(NH):
                        ins = pe.matmul(ps[:, 3072 + S * h + CH * c:3072 + S * h + CH * c + CH],
                                        hS[:, HD * h:HD * h + HD], hC[:, S * h + CH * c:S * h + CH * c + CH],
                                        start=False, stop=True, skip_group_check=True)
                    return ins

                def outer(c):
                    p0, t = CH * (c % 2), c // 2
                    for h in range(NH):
                        ins = pe.matmul(bank(4)[:, HD * h:HD * h + HD],
                                        kdT[p0:p0 + CH, 256 * h + P * t:256 * h + P * t + P],
                                        v[p0:p0 + CH, 512 * t + HD * h:512 * t + HD * h + HD], start=True, stop=True)
                    return ins

                if step == 1:
                    pe.wait_ge(h_dve, hdve(i, d, 13))
                    for j in range(NH * NT):
                        cols = slice(P * j, P * j + P)
                        ins = pe.matmul(ps[:, 2048 + P * j:2048 + P * j + P], hL[:, cols], h1[:, cols],
                                        start=True, stop=True)
                    ins.then_inc(h_pe, 1)
                if step == 2:
                    pe.wait_ge(h_dve, hdve(i, d, 20))
                    for j in range(NH * NT):
                        ins = pe.transpose(ps[:, 2048 + P * j:2048 + P * j + P], h2[:, P * j:P * j + P], ident)
                    ins.then_inc(h_pe, 1)
                if step == 3:
                    pe.wait_ge(inp_ready, i + 1)
                    pe.wait_ge(h_act, hact(i, d, 8))
                    for h in range(NH):
                        for t in range(NT):
                            j = NT * h + t
                            pe.matmul(ps[:, 3072 + P * j:3072 + P * j + P],
                                      B["inp"][:, 512 * t + HD * h:512 * t + HD * h + HD], attT[:, P * j:P * j + P],
                                      start=(d == 0 and t == 0 and h % 2 == 0), stop=True, skip_group_check=True)
                    outer(chunks[0]).then_inc(h_pe, 1)
                if step in (4, 5):
                    pe.wait_ge(h_dve, hdve(i, d, 21 + 4 * (step - 4)))
                    if step == 4:
                        pe.wait_ge(h_dve, hdve(i, d, 19))
                    inter(chunks[step - 3])
                    outer(chunks[step - 3]).then_inc(h_pe, 1)
                if step == 6:
                    pe.wait_ge(h_dve, hdve(i, d, 29))
                    inter(chunks[3]).then_inc(h_pe, 1)

            def h_post(i, step):
                if step == 0:
                    pe.wait_ge(h_act, hact(i, 2, 2))
                    for j in range(8):
                        ins = pe.matmul(bank(4)[:, j:j + 1], hL[:, P * j:P * j + P], ones[:, 0:1], start=True, stop=True)
                    ins.then_inc(h_pe, 1)
                else:
                    pe.wait_ge(h_dve, hdve(i, 2, 9))
                    for j in range(2):
                        ins = pe.matmul(bank(4 + j), ones, hC[:, 512 * j:512 * j + 512], start=True, stop=True)
                    ins.then_inc(h_pe, 1)

            def attend(i, g):
                h, odd = g // 2, g % 2
                nh = NH * i + h
                if not odd and h >= 1:
                    hh = h - 1
                    pe.wait_ge(at_pt_act, NH * i + hh + 1)
                    pe.wait_ge(at_pt_dve, NH * i + hh + 1)
                    for q in range(2):
                        o = ps[:, 3072 + P * q:3072 + P * q + P]
                        for j, (grp, t) in enumerate(((0, 0), (0, 1), (1, q), (2, q))):
                            ins = pe.matmul(o, A[f"av{grp}"][:, 512 * t + HD * hh:512 * t + HD * hh + HD],
                                            aPT[:, 512 * q + P * j:512 * q + P * j + P], start=(j == 0), stop=(j == 3))
                    ins.then_inc(at_v, 1)
                if not odd and h < NH:
                    if h == 0:
                        pe.wait_ge(rope_done, 6 * (i + 1))
                        pe.wait_ge(evac_act, 23 * i + NCHK)
                        pe.wait_ge(h_dve, hdve(i, 2, 13))
                    else:
                        pe.wait_ge(at_exp, 2 * nh)
                    hs = slice(S * h, S * h + S)
                    for q in range(2):
                        pe.matmul(bank(4 + q), identb[:, :], maskb[:, q, :], start=True, stop=False,
                                  skip_group_check=True)
                        for grp in range(NG):
                            qT = A[f"aq{grp}"][:, S * h + P * q:S * h + P * q + P]
                            kT = A[f"ak{grp}"][:, hs]
                            if grp == 0:
                                o = ps[:, 2048 + 512 * q:2048 + 512 * q + S]
                            else:
                                kT = A[f"ak{grp}"][:, S * h + P * q:S * h + P * q + P]
                                o = ps[:, 2048 + 512 * q + P * (grp + 1):2048 + 512 * q + P * (grp + 2)]
                            ins = pe.matmul(o, qT, kT, start=False, stop=True, skip_group_check=True)
                    ins.then_inc(at_s, 1)
                if odd:
                    pe.wait_ge(at_dve, 3 * (nh + 1))
                    if h:
                        pe.wait_ge(at_lo, NH * i + h)
                    else:
                        pe.wait_ge(h_act, hact(i, 2, 2))
                    for q in range(2):
                        for j in range(4):
                            ins = pe.matmul(bank(6 + q)[:, P * j:P * j + P], aP[:, 512 * q + P * j:512 * q + P * j + P],
                                            adiag[:, P * q:P * q + P], start=True, stop=True)
                        ins.then_inc(at_t, 1)

            def mixer(i):
                base = U_L0 * i
                pre_norm(i, 0)
                if i == 0:
                    parameters()
                for u in range(U_MIX):
                    k = base + u
                    if k == 1:
                        pe.wait_ge(tables_loaded, 64)
                    if u < U_GATE:
                        c, kh = u // 2, u % 2
                        name, _, layout = CHUNKS[c]
                        if kh == 0:
                            fill_wait(i, c)
                        b0 = 2 * (c % 2)
                        if layout == "feat":
                            feat_unit(0, k, b0, kh, hT_hi, hT_lo, norm=3 * i if c == 0 else None)
                        else:
                            tok_unit(0, k, [bank(b0), bank(b0 + 1)], kh, hT_nat, kh == 0)
                    elif u < U_OUT:
                        m, r = divmod(u - U_GATE, 3)
                        f = NCHK + 2 * m + (r == 2)
                        if r != 1:
                            fill_wait(i, f)
                        b0 = 2 * (f % 2)
                        if r < 2:
                            feat_unit(0, k, b0, r, hT_hi, hT_lo)
                        else:
                            n = BRANCH_ORDER[m // 2]
                            if n == 2:
                                pe.wait_ge(conv_step, 15 * (i + 1))
                            elif n == 1:
                                pe.wait_ge(h_dve, hdve(i, 2, 15))
                            else:
                                pe.wait_ge(at_lo, NH * (i + 1))
                            feat_unit(0, k, b0, 0, br_hi[:, n, :].rearrange("p (k t) -> p k t", k=4),
                                      br_lo[:, n, :].rearrange("p (k t) -> p k t", k=4))
                    else:
                        kh, j = divmod(u - U_OUT, 2)
                        if j == 0:
                            pe.wait_ge(m_lo, 2 * i + kh + 1)
                        if u < U_MIX - 1:
                            tok_unit(0, k, [bank(4 + j), bank(6 + j)], kh, merged_nat, kh == 0)
                        else:
                            last_tok_unit(0, k, [bank(4 + j), bank(6 + j)], merged_nat)
                    if u == 8:
                        pe.wait_ge(evac_act, 23 * i + CIDX["inp"] + 1)
                        for t in range(NT):
                            for h in range(NH):
                                ins = pe.transpose(bank(4 + t)[:, HD * h:HD * h + HD],
                                                   h1[:, S * h + P * t:S * h + P * t + P], ident)
                        ins.then_inc(inp_turned, 1)
                    if u in PE_H:
                        h_step(i, *PE_H[u])
                    if u in PE_POST:
                        h_post(i, PE_POST[u])
                    if U_ATT <= u < U_ATT + 9:
                        attend(i, u - U_ATT)

            def p_turn(i):
                pe.wait_ge(p_loaded, 64 * (i + 1))
                pe.wait_ge(post_gain, NT * 3 * i + 2)
                for kk in range(2):
                    for t in range(NT):
                        ins = pe.transpose(bank(7)[:, S * kk + P * t:S * kk + P * t + P],
                                           ptok[:, PLE * t + P * kk:PLE * t + P * kk + P], ident)
                ins.then_inc(p_turned, 1)

            def dense(base):
                k = base

                def feats(turns, kk, b0, kh, norm=None):
                    feat_unit(turns, kk, b0, kh, hT_hi, hT_lo, norm)

                def hT4(t, kk):
                    return (br_hi[:, 0, S * kk + P * t:S * kk + P * t + P],
                            br_lo[:, 0, S * kk + P * t:S * kk + P * t + P])

                def down(turns, kk, c, first=False):
                    for j in range(2):
                        tok_unit(turns, kk + j, [bank(j), bank(2 + j)], 0, hT4, first)

                for kh in range(2):
                    feats(0, k + kh, 4, kh, norm=1)
                pe.wait_ge(p_lo, 1)
                for kh in range(2):
                    feats(0, k + 2 + kh, 6, kh)
                k += 4

                def body(turns, kk, c, first):
                    pe.wait_ge(d_sg, c)
                    for kh in range(2):
                        feats(turns, kk + kh, 4, kh)
                        pe.wait_ge(d_lo, c)
                    down(turns, kk + 2, c - 1, first)
                    for kh in range(2):
                        feats(turns, kk + 4 + kh, 6, kh)

                body(0, k, 1, True)
                k += 6
                turn0, k0 = k // RING, k % RING
                with pe.Fori(2, NFC) as c:
                    body(c + (turn0 - 2), k0, c, False)
                k += 6 * (NFC - 2)
                def half(kk, b):
                    wh, wl = (w[:, kk % NSPL, :].rearrange("p (k n) -> p k n", k=KT) for w in (w_hi, w_lo))
                    for h in range(PARTS):
                        take(0, kk, h)
                        for f in range(2):
                            for kx in range(4 * h, 4 * h + 4):
                                ins = mm3(ps[:, 512 * b + S * f:512 * b + S * f + S], wh[:, kx, P * f:P * f + P],
                                          wl[:, kx, P * f:P * f + P], hT_hi[:, kx, :], hT_lo[:, kx, :],
                                          start=(kx == 0 and f == 0))
                        ins.then_inc(part_used, 1)

                pe.wait_ge(d_sg, NFC)
                half(k, 4)
                pe.wait_ge(d_hid, NFC)
                half(k + 1, 6)
                pe.wait_ge(d_lo, NFC)
                down(0, k + 2, NFC - 1)
                pe.wait_ge(d_lo, NFC + 1)
                kk = k + 4
                wh, wl = (w[:, kk % NSPL, :].rearrange("p (k n) -> p k n", k=2) for w in (w_hi, w_lo))
                for kx in range(2):
                    take(0, kk, kx)
                for t in range(NT):
                    for j in range(2):
                        for kx in range(2):
                            cols = slice(S * kx + P * t, S * kx + P * t + P)
                            ins = mm3(bank(2 * t + j), br_hi[:, 1, cols], br_lo[:, 1, cols],
                                      wh[:, kx, 512 * j:512 * j + 512], wl[:, kx, 512 * j:512 * j + 512], start=False)
                    if t == 0:
                        ins.then_inc(y0_done, 1)
                ins.then_inc(part_used, PARTS)

            def route():
                h_split(4)
                pe.wait_ge(r_split, 2)
                for k in range(KT):
                    cols = slice(P * k, P * k + P)
                    ins = mm3(bank(4)[:, 0:S], r_hi[:, cols], r_lo[:, cols], hT_hi[:, k, :], hT_lo[:, k, :],
                              start=(k == 0))
                ins.then_inc(r_log, 1)
                pe.wait_ge(r_copied, 1)
                for t in range(NT):
                    ins = pe.transpose(bank(5)[:, NE * t:NE * t + NE], logT[:, P * t:P * t + P],
                                       cst[0:NE, C_ID:C_ID + NE])
                ins.then_inc(r_turned, 1)
                pe.wait_ge(r_step, R_DIFF)
                mk = [rt[:, RT_M + NE * t:RT_M + NE * t + NE] for t in range(NT)]
                b = bank(5)
                pe.matmul(b[:, 16:24], lower, mk[0], start=True, stop=True)
                pe.matmul(b[:, 24:32], lower, mk[1], start=True, stop=False)
                pe.matmul(b[:, 24:32], ones, mk[0], start=False, stop=True)
                pe.matmul(b[:, 32:40], ones, mk[0], start=True, stop=False)
                pe.matmul(b[:, 32:40], ones, mk[1], start=False, stop=True).then_inc(r_rank, 1)

            def gather(it):
                pe.wait_ge(e_sel, (it + 1) * 2)
                for k in range(KT):
                    for t in range(NT):
                        ins = pe.matmul(ps[:, 1024 + P * k:1024 + P * k + P],
                                        xn[:, DM * t + P * k:DM * t + P * k + P], sel[:, P * t:P * t + P],
                                        start=(t == 0), stop=(t == NT - 1))
                for t in range(NT):
                    pe.transpose(bank(7)[:, P * t:P * t + P], sel[:, P * t:P * t + P], ident)
                for t in range(NT):
                    ins = pe.matmul(bank(7)[:, 256:257], sel[:, P * t:P * t + P], rk[:, 2 + t:3 + t],
                                    start=(t == 0), stop=(t == NT - 1))
                ins.then_inc(e_gath, 1)

            def scatter(it, t, b=2):
                pe.wait_ge(e_ylo, it + 3)
                if t and b == 2:
                    pe.wait_ge(e_acc, it * 2 + 2)
                for j in range(2):
                    cols = slice(512 * j, 512 * j + 512)
                    pe.matmul(bank(b + j), selct[:, P * t:P * t + P], ye_hi[:, cols], start=True, stop=False)
                    ins = pe.matmul(bank(b + j), selct[:, P * t:P * t + P], ye_lo[:, cols], start=False, stop=True)
                ins.then_inc(e_scat, 1)

            def experts(base):
                turn0, k0 = base // RING, base % RING
                pe.sem_inc(e_turn, ONE)
                pe.wait_ge(xn_scaled, NT)
                gather(0)
                pe.wait_ge(sweeps_ready, 1)
                sweeps = pe.value_load(nsw_i[0:1, 0:1], min_val=1, max_val=2)
                with pe.Fori(0, sweeps) as s:
                    with pe.Fori(0, NE) as e:
                        it = s * NE + e
                        turns = it * TURNS_EXP + turn0

                        def xg4(t, k):
                            return br_hi[:, 1, P * k:P * k + P], br_lo[:, 1, P * k:P * k + P]

                        def hid4(t, k):
                            return br_hi[:, 0, P * k:P * k + P], br_lo[:, 0, P * k:P * k + P]

                        def turn(c):
                            pe.wait_ge(e_hid, it * NEC + c + 1)
                            for f in range(4):
                                ins = pe.transpose(bank(6)[:, P * f:P * f + P], hid[:, P * f:P * f + P], ident)
                            ins.then_inc(e_turn, 1)

                        pe.wait_ge(e_xlo, it + 1)
                        kk = k0
                        for c in range(NEC):
                            if c:
                                pe.wait_ge(e_sg, it * NEC + c)
                            for kh in range(2):
                                tok_unit(turns, kk, [bank(4)], kh, xg4, kh == 0)
                                kk += 1
                            if c:
                                turn(c - 1)
                            else:
                                scatter(it, 0)
                            for kh in range(2):
                                tok_unit(turns, kk, [bank(5)], kh, xg4, kh == 0)
                                kk += 1
                            if c:
                                pe.wait_ge(e_tlo, it * NEC + c)
                                for j in range(2):
                                    tok_unit(turns, kk, [bank(j)], 0, hid4, c == 1)
                                    kk += 1
                            else:
                                scatter(it, 1)
                        turn(NEC - 1)
                        pe.wait_ge(e_slots, it + 1)
                        pe.wait_ge(e_acc, it * 2 + 3)
                        gather(it + 1)
                        pe.wait_ge(e_tlo, it * NEC + NEC)
                        for j in range(2):
                            tok_unit(turns, kk, [bank(j)], 0, hid4, False)
                            kk += 1
                pe.wait_ge(e_xlo, sweeps * NE + 1)
                scatter(sweeps * NE, 0)
                scatter(sweeps * NE, 1, 4)
                return sweeps

            def ple(i, turns, k, left=None):
                pe.wait_ge(p_lo, i + 1)
                wh, wl = (w[:, k % NSPL, :].rearrange("p (k n) -> p k n", k=2) for w in (w_hi, w_lo))
                for kx in range(2):
                    take(turns, k, kx)
                    for t in (1, 0):
                        if left and kx == 0 and t == 0:
                            left()
                        for j in range(2):
                            ins = mm3(bank(4 + 2 * t + j), br_hi[:, 2, S * kx + P * t:S * kx + P * t + P],
                                      br_lo[:, 2, S * kx + P * t:S * kx + P * t + P],
                                      wh[:, kx, 512 * j:512 * j + 512], wl[:, kx, 512 * j:512 * j + 512],
                                      start=(kx == 0))
                    ins.then_inc(part_used, 1)
                pre_norm(i, 2)
                for j in range(2):
                    for kh in range(2):
                        k += 1
                        if j == 0:
                            h_split(3 * i + 2, 4 * kh + 4)
                        if j and kh:
                            last_tok_unit(turns, k, [bank(j), bank(2 + j)], hT_nat)
                        else:
                            tok_unit(turns, k, [bank(j), bank(2 + j)], kh, hT_nat, kh == 0)

            def parameters():
                pe.wait_ge(const_loaded, 16 * 6)
                pe.transpose(bank(0)[:, 0:R_END], arena[0:R_END, 2048:2048 + P], cst[0:R_END, C_ID:C_ID + R_END])\
                  .then_inc(prm_turned, 1)

            pe.wait_ge(ident_loaded, 16)
            mixer(0)
            p_turn(0)
            pre_norm(0, 1)
            dense(U_MIX)
            ple(0, 0, U_MIX + U_DENSE)
            mixer(1)
            p_turn(1)
            pre_norm(1, 1)
            route()
            sweeps = experts(U_L0 + U_MIX)
            k = U_L0 + U_MIX
            ple(1, sweeps * (NE * TURNS_EXP) + k // RING, k % RING,
                lambda: pe.wait_ge(e_acc, sweeps * (NE * 2) + 3))


PE_H = {13: (0, 1), 14: (0, 2), 15: (0, 3), 16: (0, 4), 17: (0, 5), 18: (0, 6),
        27: (1, 1), 28: (1, 2), 29: (1, 3), 30: (1, 4), 31: (1, 5), 32: (1, 6)}
ACT_H = {6: (0, 0), 8: (0, 1), 10: (0, 2), 12: (0, 3), 15: (0, 4),
         20: (1, 0), 22: (1, 1), 24: (1, 2), 26: (1, 3), 29: (1, 4)}
DVE_H = {7: [(0, 0)], 9: [(0, 1)], 11: [(0, 2)], 13: [(0, 3)], 14: [(0, 4), (0, 5)], 16: [(0, 6)], 17: [(0, 7)],
         18: [(0, 8)], 21: [(1, 0)], 23: [(1, 1)], 25: [(1, 2)], 27: [(1, 3)], 28: [(1, 4), (1, 5)],
         30: [(1, 6)], 31: [(1, 7)], 32: [(1, 8)]}
PE_POST = {33: 0, 34: 1}
ACT_POST = {33: 0, 35: 1}
DVE_POST = {34: 0, 35: 1}
U_INP = 11
U_CONV = 16
U_ATT = 36
ONE = 1
RT_LG, RT_M8, RT_I8, RT_PL, RT_OH, RT_M, RT_DF, RT_TAB = 0, 16, 32, 48, 64, 80, 96, 120
RT_EX, RT_CB, RT_RE = RT_M8, RT_I8, RT_DF
TAB = 2 * NE + 1
R_DIFF = 3 + 5 * NT
PRE_ANGLES = 3 + 2 + 14
PRE_END = PRE_ANGLES + 9
INV_2PI = 0.15915494309189535
HALF_PI = 1.5707963267948966
PI_IN = 3.1415925
PI2 = (6.28125, 0.0019350051879882812, 3.0199159819567e-07)
ROUND = 12582912.0


def shape_constants(np):
    c = np.zeros((P, C_END), np.float32)
    r = np.arange(P)
    c[:, C_ID:C_ID + P] = np.eye(P)
    c[:, C_ONE:C_ONE + P] = 1.0
    c[:, C_LT:C_LT + P] = r[:, None] < r[None, :]
    c[:, C_IOTA:C_IOTA + P] = r[None, :]
    c[:, C_SCAN:C_SCAN + 512] = np.arange(512)[None, :] % CH != 0
    s, t = r[:, None], r[None, :]
    c[:, C_MASK:C_MASK + P] = (s <= t) & (s // CH == t // CH)
    c[:, C_MASK + P:C_MASK + 2 * P] = (s >= t) & (s // CH == t // CH)
    half = ROT // 2
    c[0:ROT, C_SIGN] = np.where(np.arange(ROT) < half, -1.0, 1.0)
    c[0:ROT, C_INV] = (500000.0 ** (-(np.arange(ROT) % half) * 2.0 / ROT)).astype(np.float32)
    c[:, C_I8:C_I8 + NE] = np.arange(NE)[None, :]
    order = np.array([4 * i + res for res in range(4) for i in range(S // 4)])
    mask = np.zeros((P, 2, 512), np.float32)
    for q in range(2):
        tq = order[P * q:P * q + P][:, None]
        own = order[P * q:P * q + P][None, :]
        mask[:, q, 0:S] = np.where(np.abs(tq - order[None, :]) <= 64, 0.0, -1e30)
        mask[:, q, S:S + P] = np.where((tq - own) % 4 == 0, 0.0, -1e30)
        mask[:, q, S + P:S + 2 * P] = np.where((tq - own) % 16 == 0, 0.0, -1e30)
    return c, mask, np.eye(P)


_INS = ["x", "p", "positions", "w_in", "conv_w", "hgrn_lb_logits", "hgrn_norm_g", "w_branch", "w_out",
        "g_mix_pre", "g_mix_post", "g_ffn_pre", "g_ffn_post", "dense_w_gate", "dense_w_up", "dense_w_down",
        "moe_router", "moe_w_gate", "moe_w_up", "moe_w_down", "ple_w_proj", "ple_w_gate", "ple_g_in", "ple_g_post"]


def kernel(**inputs):
    import ml_dtypes as _ml
    import numpy as _np
    import concourse.bacc as _bacc
    from concourse import mybir as _mybir
    from concourse.bass_utils import run_bass_kernel_spmd as _run

    nc = _bacc.Bacc("TRN2", target_bir_lowering=False, num_devices=1, dynamic_dma_scratch_size=1024)
    arrays, io = {}, {}

    def give(name, a):
        arrays[f"in_{name}_dram"] = a
        io[name] = nc.dram_tensor(f"in_{name}_dram", a.shape, _mybir.dt.from_np(a.dtype), kind="ExternalInput").ap()

    for name in _INS:
        give(name, _np.ascontiguousarray(inputs[name]))
    const, mask, eye = shape_constants(_np)
    give("const", const)
    give("maskb", mask.astype(_ml.bfloat16))
    give("identb", eye.astype(_ml.bfloat16))
    out = nc.dram_tensor("out_0_dram", (1, S, DM), F32, kind="ExternalOutput").ap()
    build(nc, io, out)
    r = _run(nc, [arrays], core_ids=[0])
    return r.results[0]["out_0_dram"]
```
